# Optimizing a Trainium2 kernel written in Bass

```python
import jax, jax.numpy as jnp
from jax import lax
import numpy as np

D_MODEL = 1024
BATCH = 1
SEQ = 512
DEPTH = 1

GRID_W = 64
HEAD_DIM = 64
A_HEADS = D_MODEL // (2 * HEAD_DIM)
A_KV_HEADS = A_HEADS // 4
A_WINDOW = 128
A_BLOCK = 128
B_HEADS = D_MODEL // (2 * HEAD_DIM)
B_KH_MAX = 8
B_KW = 16
D_FF = 4 * D_MODEL
EPS = 1e-6
A_WIDTH = A_HEADS * HEAD_DIM
A_KV_WIDTH = A_KV_HEADS * HEAD_DIM
B_WIDTH = B_HEADS * HEAD_DIM
IN_WIDTH = A_WIDTH + 2 * A_KV_WIDTH + 3 * B_WIDTH + 2 * D_MODEL


def rms_norm(x, g):
    xf = x.astype(jnp.float32)
    var = jnp.mean(xf * xf, axis=-1, keepdims=True)
    return (xf * lax.rsqrt(var + EPS)).astype(x.dtype) * g

def alibi_slopes(n):
    return 2.0 ** (-8.0 * jnp.arange(1, n + 1, dtype=jnp.float32) / n)

def windowed_gqa(q, k, v, sink):
    b, s, _, d = q.shape
    nb = s // A_BLOCK
    grp = A_HEADS // A_KV_HEADS
    qb = q.reshape(b, nb, A_BLOCK, A_KV_HEADS, grp, d)
    pad = ((0, 0), (A_BLOCK, A_BLOCK), (0, 0), (0, 0))
    kp = jnp.pad(k, pad)
    vp = jnp.pad(v, pad)
    slopes = alibi_slopes(A_HEADS).reshape(A_KV_HEADS, grp)
    sink_f = sink.astype(jnp.float32).reshape(A_KV_HEADS, grp)
    scale = d ** -0.5

    def block(i):
        qi = qb[:, i]
        ki = lax.dynamic_slice_in_dim(kp, i * A_BLOCK, 3 * A_BLOCK, axis=1)
        vi = lax.dynamic_slice_in_dim(vp, i * A_BLOCK, 3 * A_BLOCK, axis=1)
        q_pos = i * A_BLOCK + jnp.arange(A_BLOCK)
        k_pos = (i - 1) * A_BLOCK + jnp.arange(3 * A_BLOCK)
        dist = jnp.abs(q_pos[:, None] - k_pos[None, :])
        valid = (dist <= A_WINDOW) & (k_pos[None, :] >= 0) & (k_pos[None, :] < s)
        sc = jnp.einsum('bqkgd,bskd->bkgqs', qi, ki).astype(jnp.float32) * scale
        sc = sc - slopes[:, :, None, None] * dist.astype(jnp.float32)
        sc = jnp.where(valid, sc, -jnp.inf)
        sink_col = jnp.broadcast_to(sink_f[None, :, :, None, None], sc.shape[:-1] + (1,))
        p = jax.nn.softmax(jnp.concatenate([sc, sink_col], axis=-1), axis=-1)[..., :-1]
        return jnp.einsum('bkgqs,bskd->bqkgd', p.astype(v.dtype), vi)

    out = lax.map(block, jnp.arange(nb))
    return jnp.moveaxis(out, 0, 1).reshape(b, s, A_WIDTH)

def neighborhood_attn(q, k, v, rpb):
    b, s, h, d = q.shape
    rows = s // GRID_W
    kh = min(B_KH_MAX, rows)
    qg = q.reshape(b, rows, GRID_W, h, d)
    kg = k.reshape(b, rows, GRID_W, h, d)
    vg = v.reshape(b, rows, GRID_W, h, d)
    cols = jnp.arange(GRID_W)
    col_start = jnp.clip(cols - B_KW // 2, 0, GRID_W - B_KW)
    col_idx = col_start[:, None] + jnp.arange(B_KW)[None, :]
    dc = col_idx - cols[:, None] + (B_KW - 1)
    rpb_f = rpb.astype(jnp.float32)
    scale = d ** -0.5

    def row(r):
        r0 = jnp.clip(r - kh // 2, 0, rows - kh)
        kr = lax.dynamic_slice_in_dim(kg, r0, kh, axis=1)
        vr = lax.dynamic_slice_in_dim(vg, r0, kh, axis=1)
        kn = kr[:, :, col_idx]
        vn = vr[:, :, col_idx]
        qr = lax.dynamic_index_in_dim(qg, r, axis=1, keepdims=False)
        sc = jnp.einsum('bchd,brckhd->bhcrk', qr, kn).astype(jnp.float32) * scale
        dr = r0 + jnp.arange(kh) - r + (B_KH_MAX - 1)
        bias = rpb_f[:, dr[:, None, None], dc[None, :, :]]
        sc = sc + jnp.transpose(bias, (0, 2, 1, 3))[None]
        p = jax.nn.softmax(sc.reshape(b, h, GRID_W, kh * B_KW), axis=-1)
        p = p.reshape(b, h, GRID_W, kh, B_KW).astype(v.dtype)
        return jnp.einsum('bhcrk,brckhd->bchd', p, vn)

    out = lax.map(row, jnp.arange(rows))
    return jnp.moveaxis(out, 0, 1).reshape(b, s, B_WIDTH)

def first_inputs(seed: int = 0) -> dict:
    key = jax.random.key(seed)
    ks = jax.random.split(key, 14)
    f32 = jnp.float32

    def nrm(k, shape, scale):
        return jax.random.normal(k, shape, f32) * scale

    return {
        "x": nrm(ks[0], (BATCH, SEQ, D_MODEL), 1.0),
        "norm_mix": 1.0 + nrm(ks[1], (DEPTH, D_MODEL), 0.02),
        "w_in": nrm(ks[2], (DEPTH, D_MODEL, IN_WIDTH), D_MODEL ** -0.5),
        "b_gate": nrm(ks[3], (DEPTH, 2 * D_MODEL), 0.01),
        "sink": nrm(ks[4], (DEPTH, A_HEADS), 0.5),
        "rpb": nrm(ks[5], (DEPTH, B_HEADS, 2 * B_KH_MAX - 1, 2 * B_KW - 1), 0.1),
        "w_proj_a": nrm(ks[6], (DEPTH, A_WIDTH, D_MODEL), A_WIDTH ** -0.5),
        "w_proj_b": nrm(ks[7], (DEPTH, B_WIDTH, D_MODEL), B_WIDTH ** -0.5),
        "w_out": nrm(ks[8], (DEPTH, D_MODEL, D_MODEL), D_MODEL ** -0.5),
        "norm_mlp": 1.0 + nrm(ks[9], (DEPTH, D_MODEL), 0.02),
        "w_up": nrm(ks[10], (DEPTH, D_MODEL, D_FF), D_MODEL ** -0.5),
        "w_down": nrm(ks[11], (DEPTH, D_FF, D_MODEL), D_FF ** -0.5),
        "norm_final": 1.0 + nrm(ks[12], (D_MODEL,), 0.02),
    }

def first_block(x, norm_mix, w_in, b_gate, sink, rpb, w_proj_a, w_proj_b, w_out,
              norm_mlp, w_up, w_down, norm_final):
    b, s, _ = x.shape
    sizes = [A_WIDTH, A_KV_WIDTH, A_KV_WIDTH, B_WIDTH, B_WIDTH, B_WIDTH, D_MODEL, D_MODEL]
    offsets = [int(o) for o in np.cumsum(sizes)[:-1]]
    for l in range(DEPTH):
        h = rms_norm(x, norm_mix[l])
        z = h @ w_in[l]
        q_a, k_a, v_a, q_b, k_b, v_b, g_a, g_b = jnp.split(z, offsets, axis=-1)
        y_a = windowed_gqa(q_a.reshape(b, s, A_HEADS, HEAD_DIM),
                           k_a.reshape(b, s, A_KV_HEADS, HEAD_DIM),
                           v_a.reshape(b, s, A_KV_HEADS, HEAD_DIM), sink[l])
        y_b = neighborhood_attn(q_b.reshape(b, s, B_HEADS, HEAD_DIM),
                                k_b.reshape(b, s, B_HEADS, HEAD_DIM),
                                v_b.reshape(b, s, B_HEADS, HEAD_DIM), rpb[l])
        gates = jax.nn.sigmoid((jnp.concatenate([g_a, g_b], axis=-1) + b_gate[l])
                               .astype(jnp.float32)).astype(x.dtype)
        merged = (gates[..., :D_MODEL] * (y_a @ w_proj_a[l])
                  + gates[..., D_MODEL:] * (y_b @ w_proj_b[l]))
        x = x + merged @ w_out[l]
        h2 = rms_norm(x, norm_mlp[l])
        x = x + jnp.square(jax.nn.relu(h2 @ w_up[l])) @ w_down[l]
    return rms_norm(x, norm_final)


DEPTH_2 = 2

N_HEADS = D_MODEL // 128
QK_NOPE_DIM = 64
QK_ROPE_DIM = 32
QK_HEAD_DIM = QK_NOPE_DIM + QK_ROPE_DIM
V_HEAD_DIM = 64
ATTN_WIDTH = N_HEADS * V_HEAD_DIM
Q_LORA_RANK = D_MODEL // 4
KV_LORA_RANK = D_MODEL // 4
ROPE_THETA = 10000.0
Q_BLOCK = 128
FOURIER_WIDTH = D_MODEL // 2
FOURIER_GROUP_DIM = 128
N_FOURIER_GROUPS = FOURIER_WIDTH // FOURIER_GROUP_DIM
N_BRANCHES = 2
NORM_EPS = 1e-6
IN_WIDTH_2 = (Q_LORA_RANK + KV_LORA_RANK + QK_ROPE_DIM + ATTN_WIDTH
            + 2 * FOURIER_WIDTH + N_BRANCHES * D_MODEL)


def _rms_norm(x, g):
    xf = x.astype(jnp.float32)
    y = xf * lax.rsqrt(jnp.mean(xf * xf, axis=-1, keepdims=True) + NORM_EPS)
    return (y * g.astype(jnp.float32)).astype(x.dtype)

def _rope_tables(seq_len, dtype):
    half = QK_ROPE_DIM // 2
    inv_freq = ROPE_THETA ** (-jnp.arange(half, dtype=jnp.float32) / half)
    pos = jnp.arange(seq_len, dtype=jnp.float32)
    ang = pos[:, None] * inv_freq[None, :]
    return jnp.cos(ang).astype(dtype), jnp.sin(ang).astype(dtype)

def _apply_rope(x, cos, sin):
    half = QK_ROPE_DIM // 2
    x1, x2 = x[..., :half], x[..., half:]
    c, s = cos[:, None, :], sin[:, None, :]
    return jnp.concatenate([x1 * c - x2 * s, x2 * c + x1 * s], axis=-1)

def _split_in(p):
    sizes = [Q_LORA_RANK, KV_LORA_RANK, QK_ROPE_DIM, ATTN_WIDTH,
             FOURIER_WIDTH, FOURIER_WIDTH, D_MODEL]
    idx = []
    acc = 0
    for s in sizes:
        acc += s
        idx.append(acc)
    return jnp.split(p, idx, axis=-1)

def _bidirectional_attention(q, k, v):
    b, h, s, dk = q.shape
    nb = s // Q_BLOCK
    scale = QK_HEAD_DIM ** -0.5
    qb = q.reshape(b, h, nb, Q_BLOCK, dk).transpose(2, 0, 1, 3, 4)

    def one_block(q_blk):
        sc = jnp.einsum('bhqd,bhkd->bhqk', q_blk, k).astype(jnp.float32) * scale
        p = jax.nn.softmax(sc, axis=-1)
        return jnp.einsum('bhqk,bhkd->bhqd', p.astype(v.dtype), v)

    o = lax.map(one_block, qb)
    return o.transpose(1, 2, 0, 3, 4).reshape(b, h, s, V_HEAD_DIM)

def _mla_branch(c_q, c_kv, k_pe, q_latent_g, kv_latent_g, w_uq, w_ukv,
                q_head_g, k_head_g, cos, sin):
    b, s, _ = c_q.shape
    q = (_rms_norm(c_q, q_latent_g) @ w_uq).reshape(b, s, N_HEADS, QK_HEAD_DIM)
    kv = (_rms_norm(c_kv, kv_latent_g) @ w_ukv).reshape(b, s, N_HEADS, QK_NOPE_DIM + V_HEAD_DIM)
    k_nope, v = kv[..., :QK_NOPE_DIM], kv[..., QK_NOPE_DIM:]
    k_pe_h = jnp.broadcast_to(k_pe[:, :, None, :], (b, s, N_HEADS, QK_ROPE_DIM))
    k = jnp.concatenate([k_nope, k_pe_h], axis=-1)
    q = _rms_norm(q, q_head_g)
    k = _rms_norm(k, k_head_g)
    q = jnp.concatenate([q[..., :QK_NOPE_DIM], _apply_rope(q[..., QK_NOPE_DIM:], cos, sin)], axis=-1)
    k = jnp.concatenate([k[..., :QK_NOPE_DIM], _apply_rope(k[..., QK_NOPE_DIM:], cos, sin)], axis=-1)
    o = _bidirectional_attention(q.transpose(0, 2, 1, 3), k.transpose(0, 2, 1, 3),
                                 v.transpose(0, 2, 1, 3))
    return o.transpose(0, 2, 1, 3).reshape(b, s, ATTN_WIDTH)

def _fourier_branch(u):
    b, s, _ = u.shape
    ug = u.astype(jnp.float32).reshape(b, s, N_FOURIER_GROUPS, FOURIER_GROUP_DIM)
    f = jnp.real(jnp.fft.fft2(ug, axes=(1, 3), norm='ortho'))
    return f.reshape(b, s, FOURIER_WIDTH).astype(u.dtype)

def second_inputs(seed: int = 0) -> dict:
    key = jax.random.key(seed)
    ks = jax.random.split(key, 14)
    L, D = DEPTH_2, D_MODEL

    def nrm(k, shape, fan_in):
        return jax.random.normal(k, shape, jnp.float32) * fan_in ** -0.5

    def gain(k, shape):
        return 1.0 + 0.05 * jax.random.normal(k, shape, jnp.float32)

    return {
        "x": jax.random.normal(ks[0], (BATCH, SEQ, D), jnp.float32),
        "norm_g": gain(ks[1], (L, D)),
        "w_in": nrm(ks[2], (L, D, IN_WIDTH_2), D),
        "q_latent_g": gain(ks[3], (L, Q_LORA_RANK)),
        "kv_latent_g": gain(ks[4], (L, KV_LORA_RANK)),
        "w_uq": nrm(ks[5], (L, Q_LORA_RANK, N_HEADS * QK_HEAD_DIM), Q_LORA_RANK),
        "w_ukv": nrm(ks[6], (L, KV_LORA_RANK, N_HEADS * (QK_NOPE_DIM + V_HEAD_DIM)), KV_LORA_RANK),
        "q_head_g": gain(ks[7], (L, QK_HEAD_DIM)),
        "k_head_g": gain(ks[8], (L, QK_HEAD_DIM)),
        "w_attn_proj": nrm(ks[9], (L, ATTN_WIDTH, D), ATTN_WIDTH),
        "w_fourier_proj": nrm(ks[10], (L, FOURIER_WIDTH, D), FOURIER_WIDTH),
        "b_merge": 0.1 * jax.random.normal(ks[11], (L, N_BRANCHES, D), jnp.float32),
        "w_out": nrm(ks[12], (L, D, D), D) * (2 * DEPTH_2) ** -0.5,
    }

def second_block(x, norm_g, w_in, q_latent_g, kv_latent_g, w_uq, w_ukv, q_head_g,
              k_head_g, w_attn_proj, w_fourier_proj, b_merge, w_out):
    _, s, _ = x.shape
    cos, sin = _rope_tables(s, x.dtype)
    for l in range(DEPTH_2):
        h = _rms_norm(x, norm_g[l])
        p = h @ w_in[l]
        c_q, c_kv, k_pe, z_a, u_f, z_f, g_a, g_f = _split_in(p)
        o_a = _mla_branch(c_q, c_kv, k_pe, q_latent_g[l], kv_latent_g[l], w_uq[l], w_ukv[l],
                          q_head_g[l], k_head_g[l], cos, sin)
        y_a = (o_a * jax.nn.silu(z_a)) @ w_attn_proj[l]
        y_f = (_fourier_branch(u_f) * jax.nn.silu(z_f)) @ w_fourier_proj[l]
        m = (jax.nn.sigmoid(g_a + b_merge[l, 0]) * y_a
             + jax.nn.sigmoid(g_f + b_merge[l, 1]) * y_f)
        x = x + m @ w_out[l]
    return x


def setup_inputs(seed=0):
    out = dict(first_inputs(seed))
    for name, value in second_inputs(seed + 1).items():
        if name != "x":
            out[name + "_2"] = value
    return out


def reference(
    x, norm_mix, w_in, b_gate, sink, rpb, w_proj_a, w_proj_b, w_out, norm_mlp, w_up, w_down,
    norm_final, norm_g_2, w_in_2, q_latent_g_2, kv_latent_g_2, w_uq_2, w_ukv_2, q_head_g_2,
    k_head_g_2, w_attn_proj_2, w_fourier_proj_2, b_merge_2, w_out_2,
):
    x = first_block(
        x, norm_mix, w_in, b_gate, sink, rpb, w_proj_a, w_proj_b, w_out, norm_mlp, w_up, w_down,
        norm_final,
    )
    return second_block(
        x, norm_g_2, w_in_2, q_latent_g_2, kv_latent_g_2, w_uq_2, w_ukv_2, q_head_g_2,
        k_head_g_2, w_attn_proj_2, w_fourier_proj_2, b_merge_2, w_out_2,
    )


_drawn_inputs = setup_inputs


def setup_inputs(seed=0):
    import zlib

    import numpy as np

    out = dict(_drawn_inputs(seed))
    spreads = {}
    factors = {'norm_mix': 8.0,
     'b_gate': 8.0,
     'sink': 8.0,
     'rpb': 6.852,
     'norm_mlp': 3.139,
     'norm_final': 2.822,
     'norm_g_2': 4.31,
     'q_latent_g_2': 8.0,
     'kv_latent_g_2': 8.0,
     'w_uq_2': 3.374,
     'q_head_g_2': 8.0,
     'k_head_g_2': 8.0,
     'b_merge_2': 8.0}
    for name, (base, spread) in spreads.items():
        noise = np.random.default_rng([zlib.crc32(name.encode()), seed]).standard_normal(out[name].shape)
        drawn = base * np.exp(spread * noise) if base else spread * noise
        out[name] = __import__('jax').numpy.asarray(drawn.astype(out[name].dtype))
    for name, factor in factors.items():
        out[name] = (out[name] * factor).astype(out[name].dtype)
    return out
```

```python
from contextlib import ExitStack

import numpy as np
import concourse.bass as bass
from concourse import mybir

F32 = mybir.dt.float32
F32R = mybir.dt.float32r
ALU = mybir.AluOpType
ACT = mybir.ActivationFunctionType
AX_X = mybir.AxisListType.X

P = 128
SEQ = 512
D = 1024
KT = D // P
TT = SEQ // P
HEADS = 8
HD = 64
HALF = HEADS // 2
D_FF = 4 * D
CHUNKS = D_FF // D
LAYERS = 2
QK = 96
NOPE = 64
ROPE = 32
LAT = 256
GRID_W = 64
KH, KW = 8, 16
EPS = 1e-6
MASKED = -1e30

SLAB = 2048
SCOL = 256
GB = 4
QA0, KVA0, QB0, KB0, VB0, GA0, GB0 = 0, 512, 768, 1280, 1792, 2304, 3328
CQ0, CKV0, KPE0, ZA0, UF0, ZF0, MA0, MF0 = 0, 256, 512, 544, 1056, 1568, 2080, 3104
W2 = 4128

TAB_PAD = 64
TAB_H = (2 * KH - 1) * GRID_W
TAB = 8192

J_IN, J_MERGE, J_OUT, J_MLP = 0, 9, 21, 25
J_L, JL = 57, 28
J_END = J_L + LAYERS * JL
G_X, G_IN, G_A, G_B, G_MERGE, G_OUT, G_MLP = 0, 8, 26, 34, 42, 74, 82
G_L, GL = 146, 108
F_X, F_IN, F_MERGE, F_OUT, F_MLP = 0, 8, 26, 58, 66
F_L, FL = 130, 100
H_IN, H_MERGE, H_MLP, H_L, HL = 0, 18, 26, 58, 32
S_A, S_B, S_N2, S_NF, S_L, SL = 2, 34, 66, 68, 70, 36
U_A, U_B, U_L, UL = 0, 32, 64, 32
LP_NORM, LP_MERGE, LP_LAT, LP_HEAD = 0, 8, 24, 28
LP_N = LP_HEAD + 2 * QK
PASSES = ((0, 0), (0, 1), (1, 0))
FOURIER = (("dim", 0), ("dim", 1), ("seq", 0), ("dim", 2), ("seq", 1), ("dim", 3), ("seq", 2), ("seq", 3))
GAIN_DMAS, PAR_DMAS = 4, 4 + LAYERS * 7


class Num:

    def __init__(self, k, *terms):
        self.k, self.terms = k, tuple(t for t in terms if not isinstance(t[0], int))
        self.k += sum(t[0] * t[1] for t in terms if isinstance(t[0], int))

    def __add__(self, n):
        return Num(self.k + n, *self.terms)

    def __sub__(self, n):
        return self + (-n)

    def __mod__(self, m):
        assert all(per % m == 0 for _, per in self.terms)
        return self.k % m

    def __floordiv__(self, m):
        assert all(per % m == 0 for _, per in self.terms)
        return Num(self.k // m, *((r, per // m) for r, per in self.terms))

    def __mul__(self, m):
        return Num(self.k * m, *((r, per * m) for r, per in self.terms))

    def due(self):
        return self.k > 0

    def value(self):
        v = self.k
        for r, per in self.terms:
            v = r * per + v
        return v


class Core:
    pass


def build(nc, a, out):
    with ExitStack() as ctx:
        K = Core()
        K.a, K.out = a, out
        allocate(nc, ctx, K)
        block = ctx.enter_context(nc.Block())

        @block.sync
        def _(sp):
            program_sync(nc, sp, K)

        @block.gpsimd
        def _(pool):
            program_pool(nc, pool, K)

        @block.scalar
        def _(act):
            program_act(nc, act, K)

        @block.vector
        def _(dve):
            program_vector(nc, dve, K)

        @block.tensor
        def _(pe):
            program_pe(nc, pe, K)


def allocate(nc, ctx, K):
    def sb(name, shape, dt):
        return ctx.enter_context(nc.sbuf_tensor(name, shape, dt))

    def semaphore(name):
        return ctx.enter_context(nc.semaphore(name))

    K.raw = sb("raw", [P, 2, SLAB], F32)
    K.w = sb("w", [P, 2, 2, SLAB], F32R)
    K.x = sb("x", [P, KT, SEQ], F32)
    K.gx = sb("gx", [P, 2, KT, SEQ], F32R)
    K.rstd = sb("rstd", [P, SEQ], F32)
    K.sumsq = sb("sumsq", [P, SEQ], F32)
    K.sq = sb("sq", [P, 2, SEQ], F32)
    K.t = sb("t", [P, 3, SEQ], F32)
    K.ident = sb("ident", [P, P], F32)
    K.ones = sb("ones", [P, P], F32)
    K.r4 = sb("r4", [P, TT], F32)
    K.v4 = sb("v4", [P, TT], F32)
    K.d4 = sb("d4", [P, TT], F32)
    K.lat_v = sb("lat_v", [P, 2 * TT], F32)
    K.lat_d = sb("lat_d", [P, 2 * TT], F32)
    K.lat_r = sb("lat_r", [P, 2 * TT], F32)
    K.hs = sb("hs", [P, 2, TT * HEADS], F32)
    K.hd_ = sb("hd_", [P, 2, TT * HEADS], F32)
    K.hr = sb("hr", [P, 2, TT * HEADS], F32)
    K.mx = sb("mx", [P, 4], F32)
    K.nm = sb("nm", [P, 4], F32)
    K.den = sb("den", [P, 4], F32)
    K.rden = sb("rden", [P, 4], F32)
    K.gains = sb("gains", [P, 3, KT], F32)
    K.bg = sb("bg", [P, 2 * KT], F32)
    K.sink = sb("sink", [P, HEADS], F32)
    K.lp_all = sb("lp_all", [P, LAYERS, LP_N], F32)
    K.lp = sb("lp", [P, LP_N], F32)
    K.rope = sb("rope", [P, TT, ROPE], F32)
    K.kpe = sb("kpe", [P, TT, ROPE], F32)
    p0 = nc.sbuf_base
    sb("pt_area", [P, 8 * 256], F32)
    a0 = nc.sbuf_base
    sb("arena", [P, 84 * 256], F32)

    def at(name, kb, shape, dt, start=None):
        off = (a0 if start is None else start) + kb * 1024
        return nc.alloc_sbuf_tensor_at(name, shape, dt, offset=off)

    K.pt = at("pt", 0, [P, 2, 2, SEQ], F32R, p0)
    K.hsq = at("hsq", 0, [P, 2, HEADS * QK], F32, p0)
    K.sraw = at("sraw", 0, [P, 512], F32, p0)
    K.zero = at("zero", 6, [P, TAB // P], F32, p0)
    K.rt = at("rt", 6, [P, 3, P], F32, p0)
    K.qa = at("qa", 0, [P, 2, HALF, SEQ], F32R)
    K.ka = at("ka", 16, [P, 2, SEQ], F32R)
    K.va = at("va", 20, [P, 2, TT, P], F32R)
    K.qb = at("qb", 24, [P, 2, HALF, SEQ], F32R)
    K.kvb = at("kvb", 40, [P, 2 * 2 * HALF * SEQ], F32R)
    n = 2 * HALF * SEQ
    K.kb = K.kvb[:, 0:n].rearrange("p (h t s) -> p h t s", h=2, t=HALF)
    K.vb = K.kvb[:, n:2 * n].rearrange("p (h t s) -> p h t s", h=2, t=TT)
    K.big = K.kvb[:, :].rearrange("p (h t s) -> p h t s", h=2, t=KT)
    K.maskr = at("maskr", 72, [P, SEQ], F32R)
    K.biasa = at("biasa", 74, [P, 2, 3 * P], F32)
    K.biasb = at("biasb", 77, [P, 3, SEQ], F32)
    K.identr = at("identr", 83, [P, P], F32R)
    K.sig1 = at("sig1", 74, [P, 4, SEQ], F32)
    K.xin = at("xin", 24, [P, TT, D], F32)
    K.maskf = at("maskf", 40, [P, SEQ], F32)
    K.xout = at("xout", 0, [P, TT, D], F32)
    K.v = at("v", 0, [P, 2, TT, SEQ], F32R)
    K.qk = at("qk", 16, [P, 2, TT, HEADS * QK], F32)
    K.ab = at("ab", 40, [P, 2, 2, TT, SCOL], F32R)
    K.qkh = K.ab[:, :, :, :, :].rearrange("p r h t s -> p (r h t s)").rearrange(
        "p (r q h s) -> p r q h s", r=2, q=2, h=2)
    K.u = at("u", 56, [P, 2, 4, SEQ], F32R)
    K.z = at("z", 72, [P, 4, SEQ], F32)
    K.sw = at("sw", 80, [P, 2, 512], F32R)
    K.sig2 = at("sig2", 16, [P, 4, SEQ], F32)
    K.m2 = at("m2", 24, [P, 2, KT, SEQ], F32R)

    K.G = [ctx.enter_context(nc.psum_tensor(f"G{i}", [P, 512], F32)) for i in range(GB)]
    K.S = [ctx.enter_context(nc.psum_tensor(f"S{i}", [P, 512], F32)) for i in range(2)]
    K.T = [ctx.enter_context(nc.psum_tensor(f"T{i}", [P, 512], F32)) for i in range(2)]
    K.tab = nc.dram_tensor("bias_table", (TAB,), F32).ap()

    K.x_in = semaphore("x_in")
    K.gain_in = semaphore("gain_in")
    K.par_in = semaphore("par_in")
    K.ones_ok = semaphore("ones_ok")
    K.zero_ok = semaphore("zero_ok")
    K.tab_zeroed = semaphore("tab_zeroed")
    K.tab_in = semaphore("tab_in")
    K.prep_ok = semaphore("prep_ok")
    K.w_hi = semaphore("w_hi")
    K.w_lo = semaphore("w_lo")
    K.small_in = semaphore("small_in")
    K.small_hi = semaphore("small_hi")
    K.small_lo = semaphore("small_lo")
    K.tile_full = semaphore("tile_full")
    K.tile_out = semaphore("tile_out")
    K.split_hi = semaphore("split_hi")
    K.split_lo = semaphore("split_lo")
    K.s_full = semaphore("s_full")
    K.s_taken = semaphore("s_taken")
    K.sq_ok = semaphore("sq_ok")
    K.sum_ok = semaphore("sum_ok")
    K.gx_hi = semaphore("gx_hi")
    K.gx_lo = semaphore("gx_lo")
    K.stat_sqrt = semaphore("stat_sqrt")
    K.stat_rec = semaphore("stat_rec")
    K.stat_diag = semaphore("stat_diag")
    K.x_fin = semaphore("x_fin")
    K.max_ok = semaphore("max_ok")
    K.exp_ok = semaphore("exp_ok")
    K.rden_ok = semaphore("rden_ok")
    K.probs_ok = semaphore("probs_ok")
    K.trans_full = semaphore("trans_full")
    K.pt_hi = semaphore("pt_hi")
    K.pt_lo = semaphore("pt_lo")
    K.pv_done = semaphore("pv_done")
    K.qk_hi = semaphore("qk_hi")
    K.sig_ok = semaphore("sig_ok")
    K.mix_ok = semaphore("mix_ok")
    K.up_sq = semaphore("up_sq")
    K.lp_ok = semaphore("lp_ok")
    K.lat_sq = semaphore("lat_sq")
    K.lat_sqrt = semaphore("lat_sqrt")
    K.lat_rec = semaphore("lat_rec")
    K.q_out = semaphore("q_out")
    K.k_out = semaphore("k_out")
    K.kpe_ok = semaphore("kpe_ok")
    K.head_sq = semaphore("head_sq")
    K.head_red = semaphore("head_red")
    K.head_v = semaphore("head_v")
    K.head_sqrt = semaphore("head_sqrt")
    K.head_rec = semaphore("head_rec")
    K.head_scaled = semaphore("head_scaled")
    K.rope_ok = semaphore("rope_ok")
    K.qk_ready = semaphore("qk_ready")
    K.pool_ok = semaphore("pool_ok")
    K.out_done = semaphore("out_done")
    K.y_hi = semaphore("y_hi")
    K.ab_hi = semaphore("ab_hi")
    K.w_in_sem = [semaphore(f"slab_in{i}") for i in range(2)]
    K.biasa_in = [semaphore(f"biasa_in{i}") for i in range(2)]
    K.biasb_in = [semaphore(f"biasb_in{i}") for i in range(3)]


def in_tiles():
    tiles = [(t // 2, t % 2, "q", ("qa", t)) for t in range(HALF)]
    tiles += [(2, 0, "k", ("ka", 0)), (2, 1, "tm", ("va", 0))]
    tiles += [(3 + t // 2, t % 2, "q", ("qb", t)) for t in range(HALF)]
    tiles += [(5 + t // 2, t % 2, "k", ("kb", t)) for t in range(HALF)]
    tiles += [(7 + t // 2, t % 2, "tm", ("vb", t)) for t in range(HALF)]
    return tiles


IN_TILES = in_tiles()
IN_ENDS = [F_IN + 1 + max(i for i, t in enumerate(IN_TILES) if t[0] == j) for j in range(9)]


def in_dest(K, to, part):
    name, t = to
    if name == "qa":
        return K.qa[:, part, t, :]
    if name == "qb":
        return K.qb[:, part, t, :].rearrange("p (i c) -> p i c", c=P)[:, :, ::-1]
    if name == "kb":
        return K.kb[:, part, t, :]
    if name == "ka":
        return K.ka[:, part, :]
    if name == "va":
        return K.va[:, part, :, :]
    return K.vb[:, part, 2 * (t % 2):2 * (t % 2) + 2, (t // 2) * SCOL:(t // 2 + 1) * SCOL]


def in_shape(to, ap):
    if to[0] in ("va", "qb"):
        return ap.rearrange("p (t c) -> p t c", t=TT)
    if to[0] == "vb":
        return ap.rearrange("p (t c) -> p t c", t=2)
    return ap


class Heads:

    def __init__(self, K, kind, layer=0):
        self.kind = kind
        self.u0 = {"A": Num(U_A), "B": Num(U_B), "L": Num(U_L, (layer, UL))}[kind]
        self.s0 = {"A": Num(S_A), "B": Num(S_B), "L": Num(S_L + 4, (layer, SL))}[kind]
        self.g0 = {"A": Num(G_A), "B": Num(G_B), "L": Num(G_L + 40, (layer, GL))}[kind]
        self.f0 = Num(F_L + 40, (layer, FL)) if kind == "L" else None
        self.K = K

    def where(self, n):
        h, i = divmod(n, TT)
        lo, hi = (max(0, i - 1), min(TT, i + 2)) if self.kind == "A" else (0, TT)
        return h // 2, h % 2, i, lo, hi

    def g_out(self, h):
        return self.g0 + (h if self.kind != "L" else (4 + 3 * h if h < HEADS - 1 else 3 * HEADS - 1))

    def g_qk(self, h):
        return self.g0 + (0, 2)[h] if h < 2 else self.g0 + (5 + 3 * (h - 2))

    def rows(self, ap):
        return ap.rearrange("p (i c) -> p i c", c=P)

    def in_order(self, ap):
        return self.rows(ap)[:, :, ::-1] if self.kind == "B" else self.rows(ap)

    def first(self):
        return 1 if self.kind == "A" else 0


def program_sync(nc, sp, K):
    a = K.a

    def slab(j, pieces):
        if (j - 1).due():
            sp.wait_ge(K.w_lo, (j - 1).value())
        sp.wait_ge(K.x_in, 16 * TT)
        inc = 64 // len(pieces(K.raw[:, j % 2, :]))
        for dst, src, *n in pieces(K.raw[:, j % 2, :]):
            sp.dma_start(dst, src).then_inc(K.w_in_sem[j % 2], n[0] if n else inc)

    def columns(w, c0, rows=None):
        src = w.rearrange("(k p) n -> p k n", p=P)[:, :, c0] if not isinstance(c0, int) else \
            w.rearrange("(k p) n -> p k n", p=P)[:, :, c0:c0 + SCOL]

        def pieces(raw):
            dst = raw.rearrange("p (k n) -> p k n", k=KT)
            return [(dst[:, 0:4, :], src[:, 0:4, :]), (dst[:, 4:8, :], src[:, 4:8, :])]
        return pieces

    def qa_columns(s):
        src = a["w_in"][0].rearrange("(k p) n -> p k n", p=P)

        def pieces(raw):
            dst = raw.rearrange("p (k n) -> p k n", k=KT)
            out = []
            for m in range(2):
                for e in range(2):
                    c = QA0 + e * HALF * HD + (2 * s + m) * HD
                    out.append((dst[:, :, m * P + e * HD:m * P + (e + 1) * HD], src[:, :, c:c + HD]))
            return out
        return pieces

    def pair(wa, wb, c0, permuted):
        def cols(w):
            return w[:, c0] if not isinstance(c0, int) else w[:, c0:c0 + SCOL]

        def pieces(raw):
            dst = raw.rearrange("p (k n) -> p k n", k=KT)
            second = (dst[:, HALF:KT, :], cols(wb).rearrange("(k p) n -> p k n", p=P), 32)
            if not permuted:
                return [(dst[:, 0:HALF, :], cols(wa).rearrange("(k p) n -> p k n", p=P), 32), second]
            rows = cols(wa).rearrange("(e k p) n -> e p k n", e=2, p=HD)
            return [(dst[e * HD:(e + 1) * HD, 0:HALF, :], rows[e], 16) for e in range(2)] + [second]
        return pieces

    xs = a["x"][0].rearrange("(t p) d -> p t d", p=P)
    for t in range(TT):
        sp.dma_start(K.xin[:, t, :], xs[:, t, :]).then_inc(K.x_in, 16)

    def in_slab(j):
        if j < 2:
            slab(Num(j), qa_columns(j))
        else:
            c0 = [KVA0, QB0, QB0 + SCOL, KB0, KB0 + SCOL, VB0, VB0 + SCOL][j - 2]
            slab(Num(j), columns(a["w_in"][0], c0))

    for j in range(3):
        in_slab(j)
    sp.wait_ge(K.zero_ok, 1)
    sp.dma_start(K.tab.rearrange("(p n) -> p n", p=P), K.zero[:, :]).then_inc(K.tab_zeroed, 16)
    sp.wait_ge(K.tab_zeroed, 16)
    rows = K.tab[TAB_PAD:TAB_PAD + HEADS * TAB_H].rearrange("(r c) -> r c", c=GRID_W)
    sp.dma_start(rows[:, 0:2 * KW - 1], a["rpb"][0].rearrange("h r c -> (h r) c")).then_inc(K.tab_in, 16)
    for j in range(3, 9):
        in_slab(j)
    slab(Num(J_MERGE), columns(a["w_in"][0], GA0))
    slab(Num(J_MERGE + 1), columns(a["w_in"][0], GB0))

    for h in range(HEADS):
        if h >= 2:
            sp.wait_ge(K.s_taken, S_A + TT * (h - 1))
        head = (h % 2) * HALF + h // 2
        sp.dma_start(K.biasa[:, h % 2, :], a["alibi"][head]).then_inc(K.biasa_in[h % 2], 16)
    sp.wait_ge(K.tab_in, 16)
    for n in range(HEADS * TT):
        if n >= 3:
            sp.wait_ge(K.s_taken, S_B + n - 2)
        h, i = divmod(n, TT)
        start = TAB_PAD + h * TAB_H + (KH - 1 - 2 * i) * GRID_W + KW - 1 - (P - 1)
        src = bass.AP(K.tab.tensor, start, [[1, P], [1, SEQ]])
        sp.dma_start(K.biasb[:, n % 3, :], src).then_inc(K.biasb_in[n % 3], 16)

    for i in range(4):
        if i:
            slab(Num(J_MERGE + 3 * i), columns(a["w_in"][0], GA0 + i * SCOL))
            slab(Num(J_MERGE + 3 * i + 1), columns(a["w_in"][0], GB0 + i * SCOL))
        slab(Num(J_MERGE + 3 * i + 2), pair(a["w_proj_a"][0], a["w_proj_b"][0], i * SCOL, True))
    for i in range(4):
        slab(Num(J_OUT + i), columns(a["w_out"][0], i * SCOL))
    with sp.Fori(0, CHUNKS) as c:
        for i in range(4):
            slab(Num(J_MLP + i, (c, 8)), columns(a["w_up"][0], bass.ds(c * D + i * SCOL, SCOL)))
        for i in range(4):
            down = a["w_down"][0][bass.ds(c * D, D), :]
            slab(Num(J_MLP + 4 + i, (c, 8)), columns(down, i * SCOL))

    with sp.Fori(0, LAYERS) as l:
        def of(w):
            return w[bass.ds(l, 1)].rearrange("o r c -> (o r) c")

        j0 = Num(J_L, (l, JL))
        w_in = of(a["w_in_2"])
        for k, c0 in enumerate((CQ0, CKV0)):
            slab(j0 + k, columns(w_in, c0))
        small(sp, K, l, w_in)
        slab(j0 + 2, lambda raw: [(raw[:, 0:2 * HEADS * QK].rearrange("p (k n) -> p k n", k=2),
                                   of(a["w_uq_2"]).rearrange("(k p) n -> p k n", p=P))])
        slab(j0 + 3, lambda raw: [(raw.rearrange("p (k n) -> p k n", k=2),
                                   of(a["w_ukv_2"]).rearrange("(k p) n -> p k n", p=P))])
        for k, c0 in enumerate((UF0, UF0 + SCOL, ZF0, ZF0 + SCOL)):
            slab(j0 + 4 + k, columns(w_in, c0))
        for k in range(2):
            slab(j0 + 8 + k, lambda raw: [(raw.rearrange("p (k n) -> p k n", k=TT),
                                           a["dft_seq"][k].rearrange("(k p) n -> p k n", p=P))])
        for k in range(2):
            slab(j0 + 10 + k, columns(w_in, ZA0 + k * SCOL))
        for i in range(4):
            slab(j0 + 12 + 3 * i, columns(w_in, MA0 + i * SCOL))
            slab(j0 + 13 + 3 * i, columns(w_in, MF0 + i * SCOL))
            slab(j0 + 14 + 3 * i, pair(of(a["w_attn_proj_2"]), of(a["w_fourier_proj_2"]), i * SCOL, False))
        for i in range(4):
            slab(j0 + 24 + i, columns(of(a["w_out_2"]), i * SCOL))
    slab(Num(J_END), lambda raw: [(raw[:, 0:TAB // P], a["dft_seq"][0][0:P, 0:TAB // P])])

    os_ = K.out[0].rearrange("(t p) d -> p t d", p=P)
    g_end = G_L + LAYERS * GL
    for t in range(TT):
        sp.wait_ge(K.tile_out, g_end + 2 * t + 2)
        sp.dma_start(os_[:, t, :], K.xout[:, t, :]).then_inc(K.out_done, 16)
    sp.wait_ge(K.out_done, 16 * TT)


def small(sp, K, l, w_in):
    sp.wait_ge(K.split_lo, Num(H_L, (l, HL)).value())
    sp.wait_ge(K.x_in, 16 * TT)
    sp.dma_start(K.sraw[:, 0:SCOL], K.a["dft_dim"]).then_inc(K.small_in, 16)
    sp.dma_start(K.sraw[:, SCOL:2 * SCOL].rearrange("p (k n) -> p k n", k=KT),
                 w_in[:, KPE0:KPE0 + ROPE].rearrange("(k p) n -> p k n", p=P)).then_inc(K.small_in, 16)


def program_pool(nc, pool, K):
    nc.gpsimd.memset(K.zero[:, :], 0.0).then_inc(K.zero_ok, 1)
    nc.gpsimd.memset(K.ones[:, :], 1.0).then_inc(K.ones_ok, 1)

    def sums(norm):
        for k in range(1, KT):
            pool.wait_ge(K.sq_ok, (norm * KT + k + 1).value())
            if (norm * (KT - 1) + k - 1).due():
                pool.wait_ge(K.sum_ok, (norm * (KT - 1) + k - 1).value())
            nc.gpsimd.tensor_tensor(K.sumsq[:, :], K.sumsq[:, :], K.sq[:, k % 2, :], ALU.add).then_inc(K.sum_ok, 1)

    def probabilities(A):
        for n in range(HEADS * TT):
            _, _, _, lo, hi = A.where(n)
            c = slice(A.first(), A.first() + (hi - lo) * P)
            pool.wait_ge(K.rden_ok, (A.u0 + n + 1).value())
            p = K.t[:, n % 3, c]
            nc.gpsimd.tensor_tensor(p, p, K.rden[:, n % 4:n % 4 + 1].broadcast_to([P, (hi - lo) * P]),
                                    ALU.mult).then_inc(K.probs_ok, 1)

    def mixed(sig, h0, g0):
        for m in range(2):
            pool.wait_ge(K.tile_out, (g0 + 4 + 2 * m + 2).value())
            pool.wait_ge(K.split_lo, (h0 + m - 1).value())
            nc.gpsimd.tensor_tensor(K.t[:, m, :], sig[:, m, :], sig[:, 2 + m, :], ALU.add).then_inc(K.mix_ok, 1)

    sums(Num(0))
    probabilities(Heads(K, "A"))
    probabilities(Heads(K, "B"))
    for i in range(4):
        mixed(K.sig1, Num(H_MERGE + 2 * i), Num(G_MERGE + 8 * i))
    sums(Num(1))
    sums(Num(2))
    pool.wait_ge(K.par_in, 16 * PAR_DMAS)
    with pool.Fori(0, LAYERS) as l:
        sums(Num(3, (l, 1)))
        head = K.qk
        for q in range(2):
            pool.wait_ge(K.head_scaled, Num(q + 1, (l, 2)).value())
            v = head[:, q, :, :].rearrange("p t (h c) -> p (t h) c", h=HEADS)
            g = K.lp[:, LP_HEAD + q * QK:LP_HEAD + (q + 1) * QK]
            r0 = Num(6 * TT * q, (l, 12 * TT))
            nc.gpsimd.tensor_tensor(v, v, g.unsqueeze(1).broadcast_to([P, TT * HEADS, QK]),
                                    ALU.mult).then_inc(K.qk_ready, 1)
            pool.wait_ge(K.qk_ready, Num(q + 1, (l, 2)).value())
            for t in range(TT):
                x = head[:, q, t, :].rearrange("p (h c) -> p h c", h=HEADS)
                half = ROPE // 2
                x1, x2 = x[:, :, NOPE:NOPE + half], x[:, :, NOPE + half:QK]
                cos = K.rope[:, t, 0:half].unsqueeze(1).broadcast_to([P, HEADS, half])
                sin = K.rope[:, t, half:ROPE].unsqueeze(1).broadcast_to([P, HEADS, half])
                ra, rb, rc = [K.rt[:, i, :].rearrange("p (h c) -> p h c", h=HEADS) for i in range(3)]
                r = r0 + 6 * t
                if r.due():
                    pool.wait_ge(K.rope_ok, r.value())
                nc.gpsimd.tensor_tensor(ra, x1, cos, ALU.mult).then_inc(K.rope_ok, 1)
                nc.gpsimd.tensor_tensor(rb, x2, sin, ALU.mult).then_inc(K.rope_ok, 1)
                nc.gpsimd.tensor_tensor(rc, x1, sin, ALU.mult).then_inc(K.rope_ok, 1)
                nc.gpsimd.tensor_tensor(x2, x2, cos, ALU.mult).then_inc(K.rope_ok, 1)
                pool.wait_ge(K.rope_ok, (r + 4).value())
                nc.gpsimd.tensor_tensor(x1, ra, rb, ALU.subtract).then_inc(K.rope_ok, 1)
                last = nc.gpsimd.tensor_tensor(x2, x2, rc, ALU.add)
                last.then_inc(K.rope_ok, 1)
            if q == 0:
                silu_f(nc, pool, K, l)
        probabilities(Heads(K, "L", l))
        for t in range(HALF):
            pool.wait_ge(K.sig_ok, (sig_num(l, 4 + t) + 1).value())
            nc.gpsimd.tensor_tensor(K.sq[:, t % 2, :], K.sq[:, t % 2, :], K.t[:, t % 3, :],
                                    ALU.mult).then_inc(K.pool_ok, 1)
            pool.wait_ge(K.pool_ok, Num(4 + 2 * t + 1, (l, 12)).value())
            nc.gpsimd.tensor_tensor(K.t[:, t % 3, :], K.sq[:, t % 2, :], K.z[:, t, :],
                                    ALU.mult).then_inc(K.pool_ok, 1)
        for i in range(4):
            mixed(K.sig2, Num(H_L + 24 + 2 * i, (l, HL)), Num(G_L + 68 + 8 * i, (l, GL)))


def sig_num(l, k):
    return Num(16 + k, (l, 24))


def silu_f(nc, pool, K, l):
    for t in range(4):
        pool.wait_ge(K.sig_ok, (sig_num(l, t) + 1).value())
        nc.gpsimd.tensor_tensor(K.z[:, t, :], K.t[:, t % 3, :], K.sq[:, t % 2, :], ALU.mult).then_inc(K.pool_ok, 1)


def program_act(nc, act, K):
    a = K.a
    def by_feature(v):
        return v.rearrange("(k p) -> p k", p=P)

    act.dma_start(K.ident[:, :], a["ident"]).then_inc(K.gain_in, 16)
    for i, g in enumerate((a["norm_mix"][0], a["norm_mlp"][0], a["norm_final"])):
        act.dma_start(K.gains[:, i, :], by_feature(g), allow_slow_non_contiguous=True).then_inc(K.gain_in, 16)
    act.dma_start(K.maskf[:, :], a["mask"]).then_inc(K.par_in, 16)
    act.dma_start(K.bg[:, :], by_feature(a["b_gate"][0]), allow_slow_non_contiguous=True).then_inc(K.par_in, 16)
    act.dma_start(K.sink[:, :], a["sink"][0].partition_broadcast(P)).then_inc(K.par_in, 16)
    act.dma_start(K.rope[:, :, :], a["rope"].rearrange("(t p) c -> p t c", p=P)).then_inc(K.par_in, 16)
    for l in range(LAYERS):
        for c, n, src in ((LP_NORM, KT, by_feature(a["norm_g_2"][l])),
                          (LP_MERGE, KT, by_feature(a["b_merge_2"][l, 0])),
                          (LP_MERGE + KT, KT, by_feature(a["b_merge_2"][l, 1])),
                          (LP_LAT, 2, by_feature(a["q_latent_g_2"][l])),
                          (LP_LAT + 2, 2, by_feature(a["kv_latent_g_2"][l]))):
            act.dma_start(K.lp_all[:, l, c:c + n], src, allow_slow_non_contiguous=True).then_inc(K.par_in, 16)
        for c, g in ((LP_HEAD, a["q_head_g_2"]), (LP_HEAD + QK, a["k_head_g_2"])):
            act.dma_start(K.lp_all[:, l, c:c + QK], g[l].partition_broadcast(P)).then_inc(K.par_in, 16)

    def split(j, used):
        act.wait_ge(K.w_in_sem[j % 2], ((j // 2 + 1) * 64).value())
        if used.due():
            act.wait_ge(K.tile_full, used.value())
        nc.scalar.activation(K.w[:, j % 2, 0, :], K.raw[:, j % 2, :], ACT.Copy).then_inc(K.w_hi, 1)

    def norm_tile(norm, k, gains, ready):
        act.wait_ge(K.tile_out, ready.value())
        if k > 2:
            act.wait_ge(K.sum_ok, (norm * (KT - 1) + k - 2).value())
        nc.scalar.activation(K.sq[:, k % 2, :] if k else K.sumsq[:, :], K.x[:, k, :],
                             ACT.Square).then_inc(K.sq_ok, 1)
        if gains is not None:
            nc.scalar.activation(K.gx[:, 0, k, :], K.x[:, k, :], ACT.Copy,
                                 scale=gains[:, k:k + 1]).then_inc(K.gx_hi, 1)

    def stat(norm, s):
        act.wait_ge(K.s_taken, (s + 1).value())
        nc.scalar.activation(K.d4[:, :], K.v4[:, :], ACT.Sqrt).then_inc(K.stat_sqrt, 1)

    def hi(dst, src):
        nc.scalar.activation(dst, src, ACT.Copy).then_inc(K.split_hi, 1)

    def attention(A):
        U, S = A.u0, A.s0

        def exps(n):
            _, _, _, lo, hi_ = A.where(n)
            width = A.first() + (hi_ - lo) * P
            act.wait_ge(K.max_ok, (U + n + 1).value())
            if (U + n - 2).due():
                act.wait_ge(K.trans_full, (U + n - 2).value())
            src = K.S[(S + n) % 2][:, :] if A.kind == "L" else K.sq[:, n % 2, 0:width]
            scale = float(QK) ** -0.5 if A.kind == "L" else 1.0
            e = nc.scalar.activation(K.t[:, n % 3, 0:width], src, ACT.Exp, bias=K.nm[:, n % 4:n % 4 + 1],
                                     scale=scale, accum_out=K.den[:, n % 4:n % 4 + 1])
            e.then_inc(K.exp_ok, 1)

        def qk_hi(h):
            for q in range(2):
                act.wait_ge(K.tile_full, (A.f0 + 2 * h + q + 1).value())
                nc.scalar.activation(K.qkh[0:QK, h % 2, q, 0, :], K.G[(A.g_qk(h) + q) % GB][0:QK, :],
                                     ACT.Copy).then_inc(K.qk_hi, 1)

        def out_hi(h):
            act.wait_ge(K.pv_done, (U + TT * (h + 1)).value())
            t, e = h // 2, h % 2
            r = slice(e * HD, (e + 1) * HD)
            q = K.qa if A.kind == "A" else K.qb
            nc.scalar.activation(A.rows(q[r, 0, t, :]), A.in_order(K.G[A.g_out(h) % GB][r, :]), ACT.Copy).then_inc(K.y_hi, 1)

        if A.kind == "L":
            qk_hi(0)
        exps(0)
        exps(1)
        for n in range(HEADS * TT):
            if n % TT == 1:
                if n > TT and A.kind != "L":
                    out_hi((n - 5) // TT)
                if A.kind == "L" and n // TT + 1 < HEADS:
                    qk_hi(n // TT + 1)
            _, _, _, lo, hi_ = A.where(n)
            act.wait_ge(K.trans_full, (U + n + 1).value())
            if (U + n - 1).due():
                act.wait_ge(K.pv_done, (U + n - 1).value())
            nc.scalar.activation(K.pt[:, n % 2, 0, 0:(hi_ - lo) * P], K.T[(U + n) % 2][:, 0:(hi_ - lo) * P],
                                 ACT.Copy).then_inc(K.pt_hi, 1)
            if n + 2 < HEADS * TT:
                exps(n + 2)
        if A.kind != "L":
            out_hi(HEADS - 1)

    def sigmoid(dst, src, bias=0.0):
        nc.scalar.activation(dst, src, ACT.Sigmoid, bias=bias).then_inc(K.sig_ok, 1)

    def merge(sig, dst, bias, j, g, f, mix, pair_):
        for b in range(2):
            split(j + b + 1, f + 2 * b)
            for k in range(2):
                col = b * KT + 2 * pair_ + k
                act.wait_ge(K.tile_out, (g + 2 * b + k + 1).value())
                sigmoid(sig[:, 2 * b + k, :], sig[:, 2 * b + k, :], bias=bias[:, col:col + 1])
        split(j + 3, f + 4)
        for k in range(2):
            act.wait_ge(K.mix_ok, (mix + k + 1).value())
            hi(dst[:, 0, 2 * pair_ + k, :], K.t[:, k, :])

    split(Num(0), Num(0))
    act.wait_ge(K.gain_in, 16 * GAIN_DMAS)
    for k in range(KT):
        norm_tile(Num(0), k, K.gains[:, 0, :], Num(G_X + k + 1))
    act.wait_ge(K.par_in, 16 * PAR_DMAS)
    nc.scalar.activation(K.maskr[:, :], K.maskf[:, :], ACT.Copy).then_inc(K.prep_ok, 1)
    nc.scalar.activation(K.identr[:, :], K.ident[:, :], ACT.Copy).then_inc(K.prep_ok, 1)
    last = -1
    for k, (j, _, form, to) in enumerate(IN_TILES):
        if j != last:
            split(Num(j + 1), Num(IN_ENDS[j - 1] if j else 0))
            last = j
        if k == 0:
            stat(Num(0), Num(0))
        act.wait_ge(K.tile_out, Num(G_IN + k + 1).value())
        hi(in_dest(K, to, 0), in_shape(to, K.t[:, k % 3, :]))
    attention(Heads(K, "A"))
    attention(Heads(K, "B"))
    for i in range(4):
        merge(K.sig1, K.big, K.bg, Num(J_MERGE + 3 * i), Num(G_MERGE + 8 * i), Num(F_MERGE + 8 * i), Num(2 * i), i)
    for i in range(4):
        split(Num(J_OUT + i + 1), Num(F_OUT + 2 * i))
        for k in range(2 * i, 2 * i + 2):
            norm_tile(Num(1), k, K.gains[:, 1, :], Num(G_OUT + k + 1))
    stat(Num(1), Num(S_N2))
    with act.Fori(0, CHUNKS) as c:
        for i in range(8):
            split(Num(J_MLP + i + 1, (c, 8)), Num(F_MLP + 2 * i, (c, 16)))
            for k in range(2 * i, 2 * i + 2):
                if i < 4:
                    h = Num(H_MLP + k, (c, 8))
                    act.wait_ge(K.tile_out, Num(G_MLP + k + 1, (c, 16)).value())
                    act.wait_ge(K.split_lo, (h - 1).value())
                    nc.scalar.activation(K.sq[:, k % 2, :], K.t[:, k % 3, :], ACT.Square).then_inc(K.up_sq, 1)
                    nc.scalar.activation(K.big[:, 0, k, :], K.t[:, k % 3, :], ACT.Square).then_inc(K.split_hi, 1)
    for k in range(KT):
        norm_tile(Num(2), k, None, Num(G_L - KT + k + 1))
    stat(Num(2), Num(S_NF))
    with act.Fori(0, LAYERS) as l:
        j, g, f, h, s = (Num(n, (l, per)) for n, per in ((J_L, JL), (G_L, GL), (F_L, FL), (H_L, HL), (S_L, SL)))
        act.wait_ge(K.lp_ok, Num(1, (l, 1)).value())
        act.wait_ge(K.x_fin, KT)
        for k in range(KT):
            norm_tile(Num(3, (l, 1)), k, K.lp[:, LP_NORM:LP_NORM + KT], g - KT + k + 1)
        act.wait_ge(K.small_in, Num(32, (l, 32)).value())
        nc.scalar.activation(K.sw[:, 0, :], K.sraw[:, :], ACT.Copy).then_inc(K.small_hi, 1)
        stat(Num(3, (l, 1)), s)
        squares = [K.sq[:, 0, :], K.sq[:, 1, :], K.hsq[:, 0, 0:SEQ], K.hsq[:, 1, 0:SEQ]]
        for k in range(4):
            if k % 2 == 0:
                split(j + k // 2 + 1, f + 2 * (k // 2 + 1) - 2)
            act.wait_ge(K.tile_out, (g + k + 1).value())
            nc.scalar.activation(squares[k], K.t[:, k % 3, :], ACT.Square).then_inc(K.lat_sq, 1)
            nc.scalar.activation(K.u[:, 0, k, :], K.t[:, k % 3, :], ACT.Copy,
                                 scale=K.lp[:, LP_LAT + k:LP_LAT + k + 1]).then_inc(K.split_hi, 1)
        split(j + 3, f + 4)
        act.wait_ge(K.s_taken, (s + 4).value())
        nc.scalar.activation(K.lat_d[:, :], K.lat_v[:, :], ACT.Sqrt).then_inc(K.lat_sqrt, 1)
        split(j + 4, f + 12)
        for t in range(TT):
            for half in range(2):
                k = 2 * t + half
                act.wait_ge(K.tile_out, (g + 12 + k + 1).value())
                hi(K.v[:, 0, t, half * SCOL:(half + 1) * SCOL], K.t[:, k % 3, 0:SCOL])
        for i in range(4):
            split(j + 5 + i, f + 20 + 2 * i)
            for k in range(2 * i, 2 * i + 2):
                q, t = divmod(k, TT)
                act.wait_ge(K.tile_out, (g + (4, 12)[q] + 2 * t + 2).value())
                if Num(k - 1, (l, 2 * TT)).due():
                    act.wait_ge(K.head_red, Num(k - 1, (l, 2 * TT)).value())
                nc.scalar.activation(K.hsq[:, k % 2, :], K.qk[:, q, t, :], ACT.Square).then_inc(K.head_sq, 1)
                if i < 2:
                    act.wait_ge(K.tile_out, (g + 20 + k + 1).value())
                    hi(K.u[:, 0, k, :], K.t[:, k % 3, :])
                else:
                    if Num(k - 4 - 1, (l, 12)).due():
                        act.wait_ge(K.pool_ok, Num(k - 4 - 1, (l, 12)).value())
                    act.wait_ge(K.tile_out, (g + 20 + k + 1).value())
                    sigmoid(K.sq[:, k % 2, :], K.t[:, (k - 4) % 3, :])
            if i % 2 == 1:
                q = i // 2
                act.wait_ge(K.head_v, Num(q + 1, (l, 2)).value())
                nc.scalar.activation(K.hd_[:, q, :], K.hs[:, q, :], ACT.Sqrt).then_inc(K.head_sqrt, 1)
        split(j + 9, f + 28)
        gi = 28
        for stage, grp in FOURIER:
            if stage == "dim":
                for half in range(2):
                    act.wait_ge(K.tile_full, (f + gi + 1).value())
                    nc.scalar.activation(K.ab[:, grp % 2, 0, 2 * half:2 * half + 2, :],
                                         K.G[(g + gi) % GB][:, :].rearrange("p (t c) -> p t c", t=2),
                                         ACT.Copy).then_inc(K.ab_hi, 1)
                    gi += 1
            else:
                act.wait_ge(K.tile_out, (g + gi + 1).value())
                hi(K.u[:, 0, grp, :], K.t[:, grp % 3, :])
                gi += 1
        split(j + 10, f + 40)
        attention(Heads(K, "L", l))
        for i in range(2):
            split(j + 11 + i, f + 56 + 2 * i)
            for t in range(2 * i, 2 * i + 2):
                act.wait_ge(K.pool_ok, Num(4 + 2 * t - 2, (l, 12)).value())
                act.wait_ge(K.tile_out, (g + 64 + t + 1).value())
                sigmoid(K.sq[:, t % 2, :], K.t[:, t % 3, :])
                act.wait_ge(K.pool_ok, Num(4 + 2 * t + 2, (l, 12)).value())
                hi(K.v[:, 0, t, :], K.t[:, t % 3, :])
        for i in range(4):
            merge(K.sig2, K.m2, K.lp[:, LP_MERGE:LP_MERGE + 2 * KT], j + 12 + 3 * i, g + 68 + 8 * i,
                  f + 60 + 8 * i, Num(KT + 2 * i, (l, KT)), i)
        for i in range(4):
            split(j + 24 + i + 1, f + 92 + 2 * i)


def program_vector(nc, dve, K):
    def split(j):
        dve.wait_ge(K.w_hi, (j + 1).value())
        s = j % 2
        nc.vector.tensor_tensor(K.w[:, s, 1, :], K.raw[:, s, :], K.w[:, s, 0, :].bitcast(F32),
                                ALU.subtract).then_inc(K.w_lo, 1)

    def lo(dst, src, hi, h):
        dve.wait_ge(K.split_hi, (h + 1).value())
        nc.vector.tensor_tensor(dst, src, hi.bitcast(F32), ALU.subtract).then_inc(K.split_lo, 1)

    def lo_gain(dst, src, gain, hi, done):
        nc.vector.scalar_tensor_tensor(out=dst, in0=src, scalar=gain, in1=hi.bitcast(F32), op0=ALU.mult,
                                       op1=ALU.subtract).then_inc(done, 1)

    def gx_lo(k, gains, gx):
        dve.wait_ge(K.gx_hi, (gx + k + 1).value())
        lo_gain(K.gx[:, 1, k, :], K.x[:, k, :], gains[:, k:k + 1], K.gx[:, 0, k, :], K.gx_lo)

    def full(f):
        dve.wait_ge(K.tile_full, (f + 1).value())

    def psum(g):
        return K.G[g % GB]

    def normed(dst, g, f, scale=1.0):
        full(f)
        nc.vector.scalar_tensor_tensor(out=dst, in0=psum(g)[:, :], scalar=scale, in1=K.rstd[:, :], op0=ALU.mult,
                                       op1=ALU.mult).then_inc(K.tile_out, 1)

    def rsqrt(y, root, v, sem, n):
        nc.vector.reciprocal(y, root).then_inc(sem, 1)
        dve.wait_ge(sem, (n + 1).value())
        nc.vector.tensor_tensor(root, y, y, ALU.mult).then_inc(sem, 1)
        dve.wait_ge(sem, (n + 2).value())
        nc.vector.scalar_tensor_tensor(out=root, in0=root, scalar=-0.5, in1=v, op0=ALU.mult, op1=ALU.mult).then_inc(sem, 1)
        dve.wait_ge(sem, (n + 3).value())
        nc.vector.scalar_tensor_tensor(out=y, in0=root, scalar=1.5, in1=y, op0=ALU.add, op1=ALU.mult).then_inc(sem, 1)
        dve.wait_ge(sem, (n + 4).value())

    def stat(norm, s):
        dve.wait_ge(K.s_full, (s + 1).value())
        nc.vector.tensor_scalar(K.v4[:, :], K.S[s % 2][:, 0:TT], 1.0 / D, EPS, ALU.mult, ALU.add).then_inc(K.s_taken, 1)
        dve.wait_ge(K.stat_sqrt, (norm + 1).value())
        rsqrt(K.r4[:, :], K.d4[:, :], K.v4[:, :], K.stat_rec, norm * 4)
        diag = K.sq[:, 0, :].rearrange("p (t c) -> p t c", t=TT)
        nc.vector.tensor_tensor(diag, K.ident[:, :].unsqueeze(1).broadcast_to([P, TT, P]),
                                K.r4[:, :].unsqueeze(2).broadcast_to([P, TT, P]), ALU.mult).then_inc(K.stat_diag, 1)
        dve.wait_ge(K.s_full, (s + 2).value())
        nc.vector.tensor_copy(K.rstd[:, :], K.S[(s + 1) % 2][:, :]).then_inc(K.s_taken, 1)
        dve.wait_ge(K.s_taken, (s + 2).value())

    def attention(A):
        U, S = A.u0, A.s0
        total = HEADS * TT

        def scores(n):
            h = n // TT
            t, e, i, b0, b1 = A.where(n)
            bank = K.S[(S + n) % 2]
            c = slice(A.first(), A.first() + (b1 - b0) * P)
            m = K.mx[:, n % 4:n % 4 + 1]
            if A.kind == "L":
                dve.wait_ge(K.s_full, (S + n + 1).value())
                nc.vector.tensor_reduce(m, bank[:, :], AX_X, ALU.max).then_inc(K.s_taken, 1)
                return
            if (U + n - 1).due():
                dve.wait_ge(K.exp_ok, (U + n - 1).value())
            first = -3.0e38
            if A.kind == "A":
                head = e * HALF + t
                dve.wait_ge(K.biasa_in[h % 2], 16 * (h // 2 + 1))
                off = (b0 - i + 1) * P
                bias = K.biasa[:, h % 2, off:off + (b1 - b0) * P]
                first = K.sink[:, head:head + 1]
                nc.vector.tensor_copy(K.sq[:, n % 2, 0:1], first)
            else:
                dve.wait_ge(K.biasb_in[n % 3], 16 * (n // 3 + 1))
                bias = K.biasb[:, n % 3, :]
            dve.wait_ge(K.s_full, (S + n + 1).value())
            nc.vector.tensor_tensor_reduce(K.sq[:, n % 2, c], bank[:, 0:(b1 - b0) * P], bias, 1.0, first,
                                           ALU.add, ALU.max, m).then_inc(K.s_taken, 1)

        def negate(n):
            c = slice(n % 4, n % 4 + 1)
            dve.wait_ge(K.s_taken, (S + n + 1).value())
            scale = -float(QK) ** -0.5 if A.kind == "L" else -1.0
            nc.vector.tensor_scalar(K.nm[:, c], K.mx[:, c], scale, None, ALU.mult).then_inc(K.max_ok, 1)

        def rden(n):
            c = slice(n % 4, n % 4 + 1)
            dve.wait_ge(K.exp_ok, (U + n + 1).value())
            nc.vector.reciprocal(K.rden[:, c], K.den[:, c]).then_inc(K.rden_ok, 1)

        def out(h):
            g = A.g_out(h)
            t, e = h // 2, h % 2
            r = slice(e * HD, (e + 1) * HD)
            if A.kind == "L":
                dve.wait_ge(K.pv_done, (U + TT * (h + 1)).value())
                nc.vector.tensor_copy(K.z[r, t, :], psum(g)[r, :]).then_inc(K.tile_out, 1)
                return
            q = K.qa if A.kind == "A" else K.qb
            dve.wait_ge(K.y_hi, (0 if A.kind == "A" else HEADS) + h + 1)
            nc.vector.tensor_tensor(A.rows(q[r, 1, t, :]), A.in_order(psum(g)[r, :]), A.rows(q[r, 0, t, :]).bitcast(F32),
                                    ALU.subtract).then_inc(K.tile_out, 1)

        def qk_lo(h):
            for q in range(2):
                dve.wait_ge(K.qk_hi, Num(2 * h + q + 1, *[(r, 2 * HEADS) for r, _ in U.terms]).value())
                nc.vector.tensor_tensor(K.qkh[0:QK, h % 2, q, 1, :], psum(A.g_qk(h) + q)[0:QK, :],
                                        K.qkh[0:QK, h % 2, q, 0, :].bitcast(F32), ALU.subtract).then_inc(K.tile_out, 1)

        if A.kind == "L":
            qk_lo(0)
        for n in range(2):
            scores(n)
            negate(n)
        rden(0)
        for n in range(total):
            if n % TT == 1:
                if n > TT:
                    out((n - 5) // TT)
                if A.kind == "L" and n // TT + 1 < HEADS:
                    qk_lo(n // TT + 1)
            if n + 1 < total:
                rden(n + 1)
            if n + 2 < total:
                scores(n + 2)
            _, _, _, b0, b1 = A.where(n)
            w = (b1 - b0) * P
            dve.wait_ge(K.pt_hi, (U + n + 1).value())
            nc.vector.tensor_tensor(K.pt[:, n % 2, 1, 0:w], K.T[(U + n) % 2][:, 0:w],
                                    K.pt[:, n % 2, 0, 0:w].bitcast(F32), ALU.subtract).then_inc(K.pt_lo, 1)
            if n + 2 < total:
                negate(n + 2)
        out(HEADS - 1)

    def merge(sig, dst, j, g, f, h, mix, sig0, pair_):
        for b in range(2):
            split(j + b + 1)
            for k in range(2):
                if b == 0:
                    if (mix + k - 1).due():
                        dve.wait_ge(K.mix_ok, (mix + k - 1).value())
                normed(sig[:, 2 * b + k, :], g + 2 * b + k, f + 2 * b + k)
        split(j + 3)
        for k in range(2):
            for b in range(2):
                n = 4 + 2 * k + b
                full(f + n)
                dve.wait_ge(K.sig_ok, (sig0 + 2 * b + k + 1).value())
                s = sig[:, 2 * b + k, :]
                nc.vector.tensor_tensor(s, psum(g + n)[:, :], s, ALU.mult).then_inc(K.tile_out, 1)
        for k in range(2):
            c = 2 * pair_ + k
            lo(dst[:, 1, c, :], K.t[:, k, :], dst[:, 0, c, :], h + k)

    split(Num(0))
    for k in range(KT + 1):
        if k < KT:
            full(Num(F_X + k))
            nc.vector.tensor_copy(K.x[:, k, :], psum(Num(G_X + k))[:, :]).then_inc(K.tile_out, 1)
        if k:
            if k == 1:
                dve.wait_ge(K.gain_in, 16 * GAIN_DMAS)
            gx_lo(k - 1, K.gains[:, 0, :], Num(0))
    def in_lo(k):
        to = IN_TILES[k][3]
        lo(in_dest(K, to, 1), in_shape(to, K.t[:, k % 3, :]), in_dest(K, to, 0), Num(H_IN + k))

    last = -1
    for k, (j, _, form, to) in enumerate(IN_TILES):
        if j != last:
            split(Num(j + 1))
            last = j
        if k == 0:
            stat(Num(0), Num(0))
        t = K.t[:, k % 3, :]
        g, f = Num(G_IN + k), Num(F_IN + k)
        if H_IN + k - 2 > 0:
            dve.wait_ge(K.split_lo, H_IN + k - 2)
        if form == "tm":
            tts = slice(0, TT) if to[0] == "va" else slice(2 * (to[1] % 2), 2 * (to[1] % 2) + 2)
            n = tts.stop - tts.start
            full(f)
            nc.vector.tensor_tensor(in_shape(to, t), in_shape(to, psum(g)[:, :]),
                                    K.r4[:, tts].unsqueeze(2).broadcast_to([P, n, SEQ // n]),
                                    ALU.mult).then_inc(K.tile_out, 1)
        else:
            normed(t, g, f, float(HD) ** -0.5 if form == "q" else 1.0)
        if k:
            in_lo(k - 1)
    in_lo(len(IN_TILES) - 1)
    dve.wait_ge(K.par_in, 16 * PAR_DMAS)
    attention(Heads(K, "A"))
    attention(Heads(K, "B"))
    for i in range(4):
        merge(K.sig1, K.big, Num(J_MERGE + 3 * i), Num(G_MERGE + 8 * i), Num(F_MERGE + 8 * i),
              Num(H_MERGE + 2 * i), Num(2 * i), Num(4 * i), i)

    def residual(k, g, f):
        full(f)
        nc.vector.tensor_tensor(K.x[:, k, :], psum(g)[:, :], K.x[:, k, :], ALU.add).then_inc(K.tile_out, 1)

    for i in range(4):
        split(Num(J_OUT + i + 1))
        for k in range(2 * i, 2 * i + 2):
            residual(k, Num(G_OUT + k), Num(F_OUT + k))
            if k:
                gx_lo(k - 1, K.gains[:, 1, :], Num(KT))
    gx_lo(KT - 1, K.gains[:, 1, :], Num(KT))
    stat(Num(1), Num(S_N2))
    with dve.Fori(0, CHUNKS) as c:
        def up_lo(k):
            lo(K.big[:, 1, k, :], K.sq[:, k % 2, :], K.big[:, 0, k, :], Num(H_MLP + k, (c, 8)))

        for i in range(8):
            split(Num(J_MLP + i + 1, (c, 8)))
            for k in range(2 * i, 2 * i + 2):
                g, f = Num(G_MLP + k, (c, 16)), Num(F_MLP + k, (c, 16))
                if i < 4:
                    full(f)
                    nc.vector.scalar_tensor_tensor(out=K.t[:, k % 3, :], in0=psum(g)[:, :], scalar=0.0, in1=K.rstd[:, :],
                                                   op0=ALU.max, op1=ALU.mult).then_inc(K.tile_out, 1)
                else:
                    residual(k - KT, g, f)
                if 0 < k < KT:
                    up_lo(k - 1)
                if k == KT - 1:
                    up_lo(k)
    stat(Num(2), Num(S_NF))
    for k in range(KT):
        nc.vector.scalar_tensor_tensor(out=K.x[:, k, :], in0=K.x[:, k, :], scalar=K.gains[:, 2, k:k + 1],
                                       in1=K.rstd[:, :], op0=ALU.mult, op1=ALU.mult).then_inc(K.x_fin, 1)
    with dve.Fori(0, LAYERS) as l:
        j, g, f, h, s = (Num(n, (l, per)) for n, per in ((J_L, JL), (G_L, GL), (F_L, FL), (H_L, HL), (S_L, SL)))
        nc.vector.tensor_copy(K.lp[:, :], K.lp_all[:, bass.ds(l, 1), :].rearrange("p o c -> p (o c)")).then_inc(K.lp_ok, 1)
        dve.wait_ge(K.lp_ok, Num(1, (l, 1)).value())
        dve.wait_ge(K.x_fin, KT)
        for k in range(KT):
            gx_lo(k, K.lp[:, LP_NORM:LP_NORM + KT], Num(2 * KT, (l, KT)))
        dve.wait_ge(K.small_hi, Num(1, (l, 1)).value())
        nc.vector.tensor_tensor(K.sw[:, 1, :], K.sraw[:, :], K.sw[:, 0, :].bitcast(F32), ALU.subtract).then_inc(K.small_lo, 1)
        stat(Num(3, (l, 1)), s)

        def lat_lo(k):
            dve.wait_ge(K.split_hi, (h + k + 1).value())
            lo_gain(K.u[:, 1, k, :], K.t[:, k % 3, :], K.lp[:, LP_LAT + k:LP_LAT + k + 1], K.u[:, 0, k, :], K.split_lo)

        for k in range(4):
            if k % 2 == 0:
                split(j + k // 2 + 1)
            if k == 3:
                dve.wait_ge(K.split_lo, (h + 1).value())
            normed(K.t[:, k % 3, :], g + k, f + k)
            if k:
                lat_lo(k - 1)
        lat_lo(3)
        dve.wait_ge(K.s_full, (s + 3).value())
        nc.vector.tensor_tensor(K.kpe[:, :, :], K.S[(s + 2) % 2][:, 0:TT * ROPE].rearrange("p (t c) -> p t c", t=TT),
                                K.r4[:, :].unsqueeze(2).broadcast_to([P, TT, ROPE]), ALU.mult).then_inc(K.s_taken, 1)
        dve.wait_ge(K.s_taken, (s + 3).value())
        nc.vector.tensor_copy(
            K.qk[:, 1, :, :].rearrange("p t (h c) -> p t h c", h=HEADS)[:, :, :, NOPE:QK],
            K.kpe[:, :, :].unsqueeze(2).broadcast_to([P, TT, HEADS, ROPE])).then_inc(K.kpe_ok, 1)
        dve.wait_ge(K.s_full, (s + 4).value())
        nc.vector.tensor_scalar(K.lat_v[:, :], K.S[(s + 3) % 2][:, 0:2 * TT], 1.0 / LAT, EPS, ALU.mult,
                                ALU.add).then_inc(K.s_taken, 1)
        split(j + 3)
        dve.wait_ge(K.lat_sqrt, Num(1, (l, 1)).value())
        rsqrt(K.lat_r[:, :], K.lat_d[:, :], K.lat_v[:, :], K.lat_rec, Num(0, (l, 4)))
        for t in range(TT):
            for half in range(2):
                k = 4 + 2 * t + half
                w = HEADS * QK // 2
                full(f + k)
                nc.vector.tensor_scalar(K.qk[:, 0, t, half * w:(half + 1) * w], psum(g + k)[:, 0:w],
                                        K.lat_r[:, t:t + 1], None, ALU.mult).then_inc(K.tile_out, 1)
        split(j + 4)
        def v_lo(i):
            t, c = i // 2, slice(i % 2 * SCOL, (i % 2 + 1) * SCOL)
            lo(K.v[:, 1, t, c], K.t[:, i % 3, 0:SCOL], K.v[:, 0, t, c], h + 4 + i)

        for t in range(TT):
            for half in range(2):
                i = 2 * t + half
                k = 12 + i
                n = HEADS // 2
                src = psum(g + k)[:, :].rearrange("p (h c) -> p h c", h=n)
                dst = K.qk[:, 1, t, :].rearrange("p (h c) -> p h c", h=HEADS)[:, half * n:(half + 1) * n, 0:NOPE]
                full(f + k)
                nc.vector.tensor_scalar(dst, src[:, :, 0:NOPE], K.lat_r[:, TT + t:TT + t + 1], None,
                                        ALU.mult).then_inc(K.k_out, 1)
                dve.wait_ge(K.split_lo, (h + 4 + i - 2).value())
                v = K.t[:, i % 3, 0:SCOL]
                nc.vector.tensor_scalar(v.rearrange("p (h c) -> p h c", h=n), src[:, :, NOPE:P],
                                        K.lat_r[:, TT + t:TT + t + 1], None, ALU.mult).then_inc(K.tile_out, 1)
                if i:
                    v_lo(i - 1)
        v_lo(2 * TT - 1)

        def u_lo(k):
            lo(K.u[:, 1, k, :], K.t[:, k % 3, :], K.u[:, 0, k, :], h + 12 + k)

        def head_scale(q):
            dve.wait_ge(K.head_sqrt, Num(q + 1, (l, 2)).value())
            rsqrt(K.hr[:, q, :], K.hd_[:, q, :], K.hs[:, q, :], K.head_rec, Num(4 * q, (l, 8)))
            v = K.qk[:, q, :, :].rearrange("p t (h c) -> p (t h) c", h=HEADS)
            nc.vector.tensor_tensor(v, v, K.hr[:, q, :].unsqueeze(2).broadcast_to([P, TT * HEADS, QK]),
                                    ALU.mult).then_inc(K.head_scaled, 1)

        for i in range(4):
            split(j + 5 + i)
            if i == 2:
                head_scale(0)
            for k in range(2 * i, 2 * i + 2):
                dve.wait_ge(K.head_sq, Num(k + 1, (l, 2 * TT)).value())
                nc.vector.tensor_reduce(K.hs[:, k // TT, (k % TT) * HEADS:(k % TT + 1) * HEADS],
                                        K.hsq[:, k % 2, :].rearrange("p (h c) -> p h c", h=HEADS), AX_X,
                                        ALU.add).then_inc(K.head_red, 1)
                if i < 2:
                    dve.wait_ge(K.split_lo, (h + 10 + k + (k < 2)).value())
                    normed(K.t[:, k % 3, :], g + 20 + k, f + 20 + k)
                    if k:
                        u_lo(k - 1)
                else:
                    t = k - 4
                    dve.wait_ge(K.split_lo, (h + 16).value())
                    if Num(t - 2, (l, 12)).due():
                        dve.wait_ge(K.pool_ok, Num(t - 2, (l, 12)).value())
                    normed(K.t[:, t % 3, :], g + 20 + k, f + 20 + k)
            if i == 1:
                u_lo(TT - 1)
            if i % 2 == 1:
                q = i // 2
                dve.wait_ge(K.head_red, Num(TT * (q + 1), (l, 2 * TT)).value())
                nc.vector.tensor_scalar(K.hs[:, q, :], K.hs[:, q, :], 1.0 / QK, EPS, ALU.mult, ALU.add).then_inc(K.head_v, 1)
        head_scale(1)
        split(j + 9)
        gi, n, ab = 28, 16, 0
        for stage, grp in FOURIER:
            if stage == "dim":
                for half in range(2):
                    ab += 1
                    part = K.ab[:, grp % 2, :, 2 * half:2 * half + 2, :]
                    dve.wait_ge(K.ab_hi, Num(ab, (l, 8)).value())
                    nc.vector.tensor_tensor(part[:, 1], psum(g + gi)[:, :].rearrange("p (t c) -> p t c", t=2),
                                            part[:, 0].bitcast(F32), ALU.subtract).then_inc(K.tile_out, 1)
                    gi += 1
            else:
                dve.wait_ge(K.pool_ok, Num(4, (l, 12)).value())
                if grp == 3:
                    dve.wait_ge(K.split_lo, (h + 17).value())
                full(f + gi)
                nc.vector.tensor_tensor(K.t[:, grp % 3, :], psum(g + gi)[:, :], K.z[:, grp, :],
                                        ALU.mult).then_inc(K.tile_out, 1)
                lo(K.u[:, 1, grp, :], K.t[:, grp % 3, :], K.u[:, 0, grp, :], h + n)
                gi, n = gi + 1, n + 1
        split(j + 10)
        attention(Heads(K, "L", l))

        def za_lo(t):
            lo(K.v[:, 1, t, :], K.t[:, t % 3, :], K.v[:, 0, t, :], h + 20 + t)

        for i in range(2):
            split(j + 11 + i)
            for t in range(2 * i, 2 * i + 2):
                if t == 3:
                    za_lo(0)
                    dve.wait_ge(K.split_lo, (h + 21).value())
                normed(K.t[:, t % 3, :], g + 64 + t, f + 56 + t)
        for t in range(1, 4):
            za_lo(t)
        for i in range(4):
            merge(K.sig2, K.m2, j + 12 + 3 * i, g + 68 + 8 * i, f + 60 + 8 * i, h + 24 + 2 * i,
                  Num(KT + 2 * i, (l, KT)), sig_num(l, 8 + 4 * i), i)
        for i in range(4):
            split(j + 24 + i + 1)
            for k in range(2 * i, 2 * i + 2):
                residual(k, g + 100 + k, f + 92 + k)
    g, f = Num(G_L + LAYERS * GL), Num(F_L + LAYERS * FL)
    for k in range(2 * TT):
        full(f + k)
        nc.vector.tensor_copy(K.xout[:, k // 2, (k % 2) * SEQ:(k % 2 + 1) * SEQ], psum(g + k)[:, :]).then_inc(K.tile_out, 1)


def program_pe(nc, pe, K):
    def product(bank, pairs, stop_sem):
        for i, (lhs, rhs) in enumerate(pairs):
            mm = nc.tensor.matmul(bank, lhs, rhs, start=(i == 0), stop=(i == len(pairs) - 1))
        if stop_sem is not None:
            mm.then_inc(stop_sem, 1)

    def bank(g):
        if (g - GB + 1).due():
            pe.wait_ge(K.tile_out, (g - GB + 1).value())
        return K.G[g % GB]

    def fm(g, w, x, kts=KT, ready=None):
        b = bank(g)
        for k in range(kts):
            if ready is not None:
                ready(k)
            for i, (p, q) in enumerate(PASSES):
                mm = nc.tensor.matmul(b[:, :], w(p, k), x(q, k), start=(k == i == 0),
                                      stop=(k == kts - 1 and i == len(PASSES) - 1))
        mm.then_inc(K.tile_full, 1)

    def slab_ready(j):
        pe.wait_ge(K.w_lo, (j + 1).value())

    def wcol(j, m, kt0=0):
        v = K.w[:, j % 2, :, :].rearrange("p h (k c) -> p h k c", k=KT)
        return lambda part, k: v[:, part, kt0 + k, m * P:(m + 1) * P]

    def gx(part, k):
        return K.gx[:, part, k, :]

    def norm_ready(gx0):
        def ready(k):
            pe.wait_ge(K.gx_lo, (gx0 + k + 1).value())
        return ready

    def split_ready(h):
        def ready(k):
            pe.wait_ge(K.split_lo, (h + k + 1).value())
        return ready

    def stat_sum(norm, s):
        pe.wait_ge(K.sum_ok, (norm * (KT - 1) + KT - 1).value())
        if (s - 1).due():
            pe.wait_ge(K.s_taken, (s - 1).value())
        for t in range(TT):
            mm = nc.tensor.matmul(K.S[s % 2][:, t:t + 1], K.sumsq[:, t * P:(t + 1) * P], K.ones[:, 0:1],
                                  start=True, stop=True)
        mm.then_inc(K.s_full, 1)

    def stat_spread(norm, s):
        pe.wait_ge(K.stat_diag, (norm + 1).value())
        if s.due():
            pe.wait_ge(K.s_taken, s.value())
        nc.tensor.matmul(K.S[(s + 1) % 2][:, :], K.ones[:, :], K.sq[:, 0, :], start=True, stop=True).then_inc(K.s_full, 1)

    def attention(A):
        U, S = A.u0, A.s0
        total = HEADS * TT

        def scores(n):
            t, e, i, b0, b1 = A.where(n)
            h = n // TT
            r = slice(e * HD, (e + 1) * HD)
            w = (b1 - b0) * P
            qs = slice(i * P, (i + 1) * P)
            if A.kind == "L" and n >= 2:
                pe.wait_ge(K.exp_ok, (U + n - 1).value())
            else:
                pe.wait_ge(K.s_taken, (S + n - 1).value())
            if A.kind == "A":
                pairs = [(K.qa[r, p, t, qs], K.ka[r, q, b0 * P:b1 * P]) for p, q in PASSES]
            elif A.kind == "B":
                pairs = [(K.qb[r, p, t, qs], K.kb[r, q, t, :]) for p, q in PASSES]
                pairs.append((K.identr[:, :], K.maskr[:, :]))
            else:
                if i == 0:
                    pe.wait_ge(K.tile_out, (A.g_qk(h) + 2).value())
                pairs = [(K.qkh[0:QK, h % 2, 0, p, qs], K.qkh[0:QK, h % 2, 1, q, :]) for p, q in PASSES]
            product(K.S[(S + n) % 2][:, 0:w], pairs, K.s_full)

        def transposes(n):
            _, _, _, b0, b1 = A.where(n)
            pe.wait_ge(K.probs_ok, (U + n + 1).value())
            if (U + n - 1).due():
                pe.wait_ge(K.pt_lo, (U + n - 1).value())
            for k in range(b1 - b0):
                c = A.first() + k * P
                mm = nc.tensor.transpose(K.T[(U + n) % 2][:, k * P:(k + 1) * P], K.t[:, n % 3, c:c + P], K.ident[:, :])
            mm.then_inc(K.trans_full, 1)

        def values(n):
            t, e, i, b0, b1 = A.where(n)
            h = n // TT
            b = bank(A.g_out(h)) if i == 0 else K.G[A.g_out(h) % GB]
            pe.wait_ge(K.pt_lo, (U + n + 1).value())
            pairs = []
            for k in range(b0, b1):
                for p, q in PASSES:
                    v = {"A": lambda: K.va[:, p, k, :], "B": lambda: K.vb[:, p, k, t * P:(t + 1) * P],
                         "L": lambda: K.v[:, p, k, t * P:(t + 1) * P]}[A.kind]()
                    pairs.append((v, K.pt[:, n % 2, q, (k - b0) * P:(k - b0 + 1) * P]))
            product(b[:, i * P:(i + 1) * P], pairs, K.pv_done)

        def turn(h):
            for q in range(2):
                b = bank(A.g_qk(h) + q)
                for t in range(TT):
                    mm = nc.tensor.transpose(b[0:QK, t * P:(t + 1) * P], K.qk[:, q, t, h * QK:(h + 1) * QK], K.ident[:, :])
                mm.then_inc(K.tile_full, 1)

        if A.kind == "L":
            turn(0)
        scores(0)
        scores(1)
        for n in range(total):
            transposes(n)
            if n + 2 < total:
                scores(n + 2)
            if A.kind == "L" and n % TT == 0 and n // TT + 1 < HEADS:
                turn(n // TT + 1)
            if n:
                values(n - 1)
        values(total - 1)

    def merge(j, g, ya, yb, y_ready):
        for b in range(2):
            slab_ready(j + b)
            for m in range(2):
                fm(g + 2 * b + m, wcol(j + b, m), gx)
        slab_ready(j + 2)
        y_ready()
        for m in range(2):
            fm(g + 4 + 2 * m, wcol(j + 2, m), ya, HALF)
            fm(g + 5 + 2 * m, wcol(j + 2, m, HALF), yb, HALF)

    def eight(j, g, x, ready=None):
        for i in range(4):
            slab_ready(j + i)
            for m in range(2):
                fm(g + 2 * i + m, wcol(j + i, m), x, ready=ready if i == m == 0 else None)

    pe.wait_ge(K.gain_in, 16 * GAIN_DMAS)
    pe.wait_ge(K.ones_ok, 1)
    pe.wait_ge(K.x_in, 16 * TT)
    for k in range(KT):
        b = bank(Num(G_X + k))
        for t in range(TT):
            mm = nc.tensor.transpose(b[:, t * P:(t + 1) * P], K.xin[:, t, k * P:(k + 1) * P], K.ident[:, :])
        mm.then_inc(K.tile_full, 1)
    for k, (j, m, form, to) in enumerate(IN_TILES):
        g = Num(G_IN + k)
        slab_ready(Num(j))
        if form != "tm":
            fm(g, wcol(Num(j), m), gx, ready=norm_ready(Num(0)) if k == 0 else None)
        else:
            b = bank(g)
            w = K.w[:, j % 2, :, :].rearrange("p h (k c) -> p h k c", k=KT)
            whole = to[0] == "va"
            cols, n = (slice(P, 2 * P), P) if whole else (slice(0, SCOL), SCOL)
            tts = range(TT) if whole else range(2 * (to[1] % 2), 2 * (to[1] % 2) + 2)
            for i, t in enumerate(tts):
                pairs = [(K.gx[:, p, kt, t * P:(t + 1) * P], w[:, q, kt, cols]) for kt in range(KT) for p, q in PASSES]
                product(b[:, i * n:(i + 1) * n], pairs, K.tile_full if i == len(tts) - 1 else None)
        if k == 0:
            stat_sum(Num(0), Num(0))
        if k == 1:
            stat_spread(Num(0), Num(0))
    pe.wait_ge(K.split_lo, Num(H_MERGE).value())
    attention(Heads(K, "A"))
    pe.wait_ge(K.prep_ok, 2)
    attention(Heads(K, "B"))

    def heads_ready():
        pe.wait_ge(K.tile_out, G_B + HEADS)

    for i in range(4):
        merge(Num(J_MERGE + 3 * i), Num(G_MERGE + 8 * i), lambda p, k: K.qa[:, p, k, :], lambda p, k: K.qb[:, p, k, :],
              heads_ready)

    def big(part, k):
        return K.big[:, part, k, :]

    eight(Num(J_OUT), Num(G_OUT), big, split_ready(Num(H_MERGE)))
    pe.wait_ge(K.gx_lo, 2 * KT)
    stat_sum(Num(1), Num(S_N2))
    stat_spread(Num(1), Num(S_N2))
    with pe.Fori(0, CHUNKS) as c:
        eight(Num(J_MLP, (c, 8)), Num(G_MLP, (c, 16)), gx)
        eight(Num(J_MLP + 4, (c, 8)), Num(G_MLP + 8, (c, 16)), big, split_ready(Num(H_MLP, (c, 8))))
    stat_sum(Num(2), Num(S_NF))
    stat_spread(Num(2), Num(S_NF))
    with pe.Fori(0, LAYERS) as l:
        j, g, f, h, s = (Num(n, (l, per)) for n, per in ((J_L, JL), (G_L, GL), (F_L, FL), (H_L, HL), (S_L, SL)))
        norm = Num(3, (l, 1))
        for k in range(4):
            slab_ready(j + k // 2)
            fm(g + k, wcol(j + k // 2, k % 2), gx,
               ready=norm_ready(Num(2 * KT, (l, KT))) if k == 0 else None)
            if k == 0:
                stat_sum(norm, s)
            if k == 1:
                stat_spread(norm, s)
        pe.wait_ge(K.small_lo, Num(1, (l, 1)).value())
        pe.wait_ge(K.s_taken, (s + 1).value())
        wk = K.sw[:, :, SCOL:2 * SCOL].rearrange("p h (k c) -> p h k c", k=KT)
        for t in range(TT):
            pairs = [(K.gx[:, p, kt, t * P:(t + 1) * P], wk[:, q, kt, :]) for kt in range(KT) for p, q in PASSES]
            product(K.S[(s + 2) % 2][:, t * ROPE:(t + 1) * ROPE], pairs, K.s_full if t == TT - 1 else None)
        squares = [K.sq[:, 0, :], K.sq[:, 1, :], K.hsq[:, 0, 0:SEQ], K.hsq[:, 1, 0:SEQ]]
        pe.wait_ge(K.lat_sq, Num(4, (l, 4)).value())
        pe.wait_ge(K.s_taken, (s + 2).value())
        for i in range(2):
            for t in range(TT):
                for m in range(2):
                    mm = nc.tensor.matmul(K.S[(s + 3) % 2][:, i * TT + t:i * TT + t + 1],
                                          squares[2 * i + m][:, t * P:(t + 1) * P], K.ones[:, 0:1],
                                          start=(m == 0), stop=(m == 1))
        mm.then_inc(K.s_full, 1)
        pe.wait_ge(K.split_lo, (h + 4).value())
        for i, n in enumerate((HEADS * QK // 2, SEQ)):
            slab_ready(j + 2 + i)
            w = K.w[:, (j + 2 + i) % 2, :, 0:4 * n].rearrange("p h (k c) -> p h k c", k=2)
            for t in range(TT):
                for half in range(2):
                    b = bank(g + 4 + 8 * i + 2 * t + half)
                    pairs = [(K.u[:, p, 2 * i + k, t * P:(t + 1) * P], w[:, q, k, half * n:(half + 1) * n])
                             for k in range(2) for p, q in PASSES]
                    product(b[:, 0:n], pairs, K.tile_full)
        for k in range(8):
            slab_ready(j + 4 + k // 2)
            fm(g + 20 + k, wcol(j + 4 + k // 2, k % 2), gx)
        gi = 28
        for stage, grp in FOURIER:
            if stage == "dim":
                pe.wait_ge(K.split_lo, (h + 12 + grp + 1).value())
                for half in range(2):
                    b = bank(g + gi)
                    for i, t in enumerate((2 * half, 2 * half + 1)):
                        pairs = [(K.u[:, p, grp, t * P:(t + 1) * P], K.sw[:, q, 0:SCOL]) for p, q in PASSES]
                        product(b[:, i * SCOL:(i + 1) * SCOL], pairs, K.tile_full if i else None)
                    gi += 1
            else:
                b = bank(g + gi)
                pe.wait_ge(K.tile_out, (g + fourier_tile(grp)).value())
                slab_ready(j + 9)
                pairs = []
                for part in range(2):
                    w = K.w[:, (j + 8 + part) % 2, :, :].rearrange("p h (k c) -> p h k c", k=TT)
                    pairs += [(K.ab[:, grp % 2, p, t, part * P:(part + 1) * P], w[:, q, t, :])
                              for t in range(TT) for p, q in PASSES]
                product(b[:, :], pairs, K.tile_full)
                gi += 1
        pe.wait_ge(K.rope_ok, Num(12 * TT, (l, 12 * TT)).value())
        attention(Heads(K, "L", l))
        for k in range(4):
            slab_ready(j + 10 + k // 2)
            fm(g + 64 + k, wcol(j + 10 + k // 2, k % 2), gx)

        def branches_ready():
            pe.wait_ge(K.split_lo, (h + 24).value())

        for i in range(4):
            merge(j + 12 + 3 * i, g + 68 + 8 * i, lambda p, k: K.v[:, p, k, :], lambda p, k: K.u[:, p, k, :],
                  branches_ready)
        eight(j + 24, g + 100, lambda p, k: K.m2[:, p, k, :], split_ready(h + 24))
    g = Num(G_L + LAYERS * GL)
    for k in range(2 * TT):
        b = bank(g + k)
        pe.wait_ge(K.tile_out, (g if k % 2 else g - KT // 2).value())
        for i in range(KT // 2):
            kt = (k % 2) * (KT // 2) + i
            mm = nc.tensor.transpose(b[:, i * P:(i + 1) * P], K.x[:, kt, (k // 2) * P:(k // 2 + 1) * P], K.ident[:, :])
        mm.then_inc(K.tile_full, 1)


def fourier_tile(grp):
    n = 28
    for stage, of in FOURIER:
        n += 2 if stage == "dim" else 1
        if (stage, of) == ("dim", grp):
            return n


_INS = ["x", "norm_mix", "w_in", "b_gate", "sink", "rpb", "w_proj_a", "w_proj_b", "w_out", "norm_mlp", "w_up", "w_down",
        "norm_final", "norm_g_2", "w_in_2", "q_latent_g_2", "kv_latent_g_2", "w_uq_2", "w_ukv_2", "q_head_g_2",
        "k_head_g_2", "w_attn_proj_2", "w_fourier_proj_2", "b_merge_2", "w_out_2"]


def constants():
    f = np.float32
    c = {"ident": np.eye(P, dtype=f)}
    dist = np.abs(np.arange(P)[:, None] - (np.arange(3 * P) - P)[None, :])
    slopes = np.exp2(-8.0 * np.arange(1, HEADS + 1, dtype=f) / HEADS).astype(f)
    c["alibi"] = np.where(dist <= P, -slopes[:, None, None] * dist.astype(f), f(MASKED)).astype(f)
    col = np.arange(GRID_W)
    start = np.clip(col - KW // 2, 0, GRID_W - KW)
    near = ((col[None, :] >= start[:, None]) & (col[None, :] < start[:, None] + KW))[::-1]
    c["mask"] = np.tile(np.where(near, f(0), f(MASKED)), (2, KH)).astype(f)
    s = np.outer(np.arange(SEQ), np.arange(SEQ)) % SEQ * (2 * np.pi / SEQ)
    c["dft_seq"] = np.stack([np.cos(s), -np.sin(s)]).astype(f)
    d = np.outer(np.arange(P), np.arange(P)) % P * (2 * np.pi / P)
    c["dft_dim"] = (np.concatenate([np.cos(d), np.sin(d)], 1) / np.sqrt(SEQ * P)).astype(f)
    half = ROPE // 2
    inv = (f(10000.0) ** (-np.arange(half, dtype=f) / f(half))).astype(f)
    ang = np.arange(SEQ, dtype=f)[:, None] * inv[None, :]
    c["rope"] = np.concatenate([np.cos(ang), np.sin(ang)], 1).astype(f)
    return c


def kernel(**inputs):
    import concourse.bacc as _bacc
    from concourse.bass_utils import run_bass_kernel_spmd as _run

    nc = _bacc.Bacc("TRN2", target_bir_lowering=False, num_devices=1)
    arrays, a = {}, {}
    given = {n: np.ascontiguousarray(inputs[n]) for n in _INS}
    for name, v in {**given, **constants()}.items():
        arrays[f"in_{name}"] = v
        a[name] = nc.dram_tensor(f"in_{name}", v.shape, mybir.dt.from_np(v.dtype), kind="ExternalInput").ap()
    out = nc.dram_tensor("out", (1, SEQ, D), F32, kind="ExternalOutput").ap()
    build(nc, a, out)
    r = _run(nc, [arrays], core_ids=[0])
    return r.results[0]["out"]
```

```python
from contextlib import ExitStack

import numpy as np
import concourse.bass as bass
from concourse import mybir

F32 = mybir.dt.float32
F32R = mybir.dt.float32r
ALU = mybir.AluOpType
ACT = mybir.ActivationFunctionType
AX_X = mybir.AxisListType.X

P = 128
SEQ = 512
D = 1024
KT = D // P
TT = SEQ // P
HEADS = 8
HD = 64
HALF = HEADS // 2
D_FF = 4 * D
CHUNKS = D_FF // D
LAYERS = 2
QK = 96
NOPE = 64
ROPE = 32
LAT = 256
GRID_W = 64
KH, KW = 8, 16
EPS = 1e-6
MASKED = -1e30

SLAB = 2048
SCOL = 256
GB = 4
QA0, KVA0, QB0, KB0, VB0, GA0, GB0 = 0, 512, 768, 1280, 1792, 2304, 3328
CQ0, CKV0, KPE0, ZA0, UF0, ZF0, MA0, MF0 = 0, 256, 512, 544, 1056, 1568, 2080, 3104
W2 = 4128

TAB_PAD = 64
TAB_H = (2 * KH - 1) * GRID_W
TAB = 8192
BIAS_ROWS = 2 * KH - 2

J_IN, J_MERGE, J_OUT, J_MLP = 0, 9, 21, 25
J_L, JL = 57, 28
J_END = J_L + LAYERS * JL
G_X, G_IN, G_A, G_B, G_MERGE, G_OUT, G_MLP = 0, 8, 26, 34, 42, 74, 82
G_L, GL = 146, 108
F_X, F_IN, F_MERGE, F_OUT, F_MLP = 0, 8, 26, 58, 66
F_L, FL = 130, 100
H_IN, H_MERGE, H_MLP, H_L, HL = 0, 18, 26, 58, 32
S_A, S_B, S_N2, S_NF, S_L, SL = 2, 34, 66, 68, 70, 36
U_A, U_B, U_L, UL = 0, 32, 64, 32
MIDWAY = 18
AHEAD = 3
LP_MERGE, LP_LAT, LP_HEAD = 0, 2 * KT, 2 * KT + 4
LP_N = LP_HEAD + 2 * QK
PASSES = ((0, 0), (0, 1), (1, 0))
FOURIER = (("dim", 0), ("dim", 1), ("seq", 0), ("dim", 2), ("seq", 1), ("dim", 3), ("seq", 2), ("seq", 3))
HEAD_SQUARES = ((0, 1), (2,), (3, 4), (5,), (6,), (7,), (), ())
HEAD_ROOT, HEAD_SCALE = {2: 0, 5: 1}, {3: 0, 6: 1}
GAIN_DMAS, PAR_DMAS = 4, 5 + LAYERS * 7


class Num:

    def __init__(self, k, *terms):
        self.k, self.terms = k, tuple(t for t in terms if not isinstance(t[0], int))
        self.k += sum(t[0] * t[1] for t in terms if isinstance(t[0], int))

    def __add__(self, n):
        return Num(self.k + n, *self.terms)

    def __sub__(self, n):
        return self + (-n)

    def __mod__(self, m):
        assert all(per % m == 0 for _, per in self.terms)
        return self.k % m

    def __floordiv__(self, m):
        assert all(per % m == 0 for _, per in self.terms)
        return Num(self.k // m, *((r, per // m) for r, per in self.terms))

    def __mul__(self, m):
        return Num(self.k * m, *((r, per * m) for r, per in self.terms))

    def due(self):
        return self.k > 0

    def value(self):
        v = self.k
        for r, per in self.terms:
            v = r * per + v
        return v


class Core:
    pass


def build(nc, a, out):
    with ExitStack() as ctx:
        K = Core()
        K.a, K.out = a, out
        allocate(nc, ctx, K)
        block = ctx.enter_context(nc.Block())

        @block.sync
        def _(sp):
            program_sync(nc, sp, K)

        @block.gpsimd
        def _(pool):
            program_pool(nc, pool, K)

        @block.scalar
        def _(act):
            program_act(nc, act, K)

        @block.vector
        def _(dve):
            program_vector(nc, dve, K)

        @block.tensor
        def _(pe):
            program_pe(nc, pe, K)


def allocate(nc, ctx, K):
    def sb(name, shape, dt):
        return ctx.enter_context(nc.sbuf_tensor(name, shape, dt))

    def semaphore(name):
        return ctx.enter_context(nc.semaphore(name))

    raw0 = (nc.sbuf_base + 31) // 32 * 32
    K.raw = sb("raw", [P, 2, SLAB], F32)
    K.w = sb("w", [P, 2, 2, SLAB], F32R)
    K.x = sb("x", [P, KT, SEQ], F32)
    K.gx = sb("gx", [P, 2, KT, SEQ], F32R)
    K.rstd = sb("rstd", [P, SEQ], F32)
    K.sumsq = sb("sumsq", [P, SEQ], F32)
    K.sq = sb("sq", [P, 2, SEQ], F32)
    K.t = sb("t", [P, 3, SEQ], F32)
    K.ident = sb("ident", [P, P], F32)
    K.ones = sb("ones", [P, P], F32)
    K.r4 = sb("r4", [P, TT], F32)
    K.v4 = sb("v4", [P, TT], F32)
    K.d4 = sb("d4", [P, TT], F32)
    K.lat_v = sb("lat_v", [P, 2 * TT], F32)
    K.lat_d = sb("lat_d", [P, 2 * TT], F32)
    K.lat_r = sb("lat_r", [P, 2 * TT], F32)
    K.hs = sb("hs", [P, 2, TT * HEADS], F32)
    K.hd_ = sb("hd_", [P, 2, TT * HEADS], F32)
    K.hr = sb("hr", [P, 2, TT * HEADS], F32)
    K.mx = sb("mx", [P, 4], F32)
    K.nm = sb("nm", [P, 4], F32)
    K.den = sb("den", [P, 4], F32)
    K.rden = sb("rden", [P, 4], F32)
    K.gains = sb("gains", [P, 4, KT], F32)
    K.norm_all = sb("norm_all", [P, LAYERS + 1, KT], F32)
    K.norm_next = sb("norm_next", [P, KT], F32)
    K.prior = sb("prior", [P, TT], F32)
    K.prior2 = sb("prior2", [P, TT], F32)
    K.bg = sb("bg", [P, 2 * KT], F32)
    K.sink = sb("sink", [P, HEADS], F32)
    K.lp_all = sb("lp_all", [P, LAYERS, LP_N], F32)
    K.lp = sb("lp", [P, LP_N], F32)
    K.rope = sb("rope", [P, TT, ROPE], F32)
    p0 = nc.sbuf_base
    sb("pt_area", [P, 8 * 256], F32)
    a0 = nc.sbuf_base
    sb("arena", [P, 84 * 256], F32)

    def at(name, kb, shape, dt, start=None):
        off = (a0 if start is None else start) + kb * 1024
        return nc.alloc_sbuf_tensor_at(name, shape, dt, offset=off)

    pt0 = at("pt0", 0, [P, 2, TT, 2, P], F32R, p0)
    K.pt = {"L": [pt0, at("pt1_l", 0, [P, 2, TT, 2, P], F32R, raw0)]}
    K.pt["A"] = K.pt["B"] = [pt0, at("pt1", 0, [P, 2, TT, 2, P], F32R, raw0 + SLAB * 4)]
    K.hsq = at("hsq", 0, [P, 2, HEADS * QK], F32, p0)
    K.sraw = at("sraw", 0, [P, 512], F32, p0)
    K.zero = at("zero", 6, [P, TAB // P], F32, p0)
    K.rt = at("rt", 6, [P, 2, 2 * P], F32, p0)
    K.qa = at("qa", 0, [P, 2, HALF, SEQ], F32R)
    K.ka = at("ka", 16, [P, 2, SEQ], F32R)
    K.va = at("va", 20, [P, 2, TT, P], F32R)
    K.qb = at("qb", 24, [P, 2, HALF, SEQ], F32R)
    K.kvb = at("kvb", 40, [P, 2 * 2 * HALF * SEQ], F32R)
    n = 2 * HALF * SEQ
    K.kb = K.kvb[:, 0:n].rearrange("p (h t s) -> p h t s", h=2, t=HALF)
    K.vb = K.kvb[:, n:2 * n].rearrange("p (h t s) -> p h t s", h=2, t=TT)
    K.big = K.kvb[:, :].rearrange("p (h t s) -> p h t s", h=2, t=KT)
    K.mask = at("mask", 72, [P, GRID_W], F32)
    K.biasa = at("biasa", 74, [P, 2, 3 * P], F32)
    K.biasb = at("biasb", 77, [P, 2, BIAS_ROWS * GRID_W], F32)
    K.sig1 = at("sig1", 74, [P, 4, SEQ], F32)
    K.sumsq_f = at("sumsq_f", 0, [P, SEQ], F32)
    K.sq_f = at("sq_f", 2, [P, 2, SEQ], F32)
    K.xin = at("xin", 24, [P, TT, D], F32)
    K.xout = at("xout", 0, [P, TT, D], F32)
    K.v = at("v", 0, [P, 2, TT, SEQ], F32R)
    K.qk = at("qk", 16, [P, 2, TT, HEADS * QK], F32)
    K.ab = at("ab", 40, [P, 2, 2, TT, SCOL], F32R)
    K.qkh = K.ab[:, :, :, :, :].rearrange("p r h t s -> p (r h t s)").rearrange(
        "p (r q h s) -> p r q h s", r=2, q=2, h=2)
    K.u = at("u", 56, [P, 2, 4, SEQ], F32R)
    K.kpe = at("kpe", 78, [P, TT, ROPE], F32)
    K.z = at("z", 72, [P, 4, SEQ], F32)
    K.sw = at("sw", 80, [P, 2, 512], F32R)
    K.sig2 = at("sig2", 16, [P, 4, SEQ], F32)
    K.m2 = at("m2", 24, [P, 2, KT, SEQ], F32R)

    K.G = [ctx.enter_context(nc.psum_tensor(f"G{i}", [P, 512], F32)) for i in range(GB)]
    K.S = [ctx.enter_context(nc.psum_tensor(f"S{i}", [P, 512], F32)) for i in range(2)]
    K.T = [ctx.enter_context(nc.psum_tensor(f"T{i}", [P, 512], F32)) for i in range(2)]
    K.tab = nc.dram_tensor("bias_table", (TAB,), F32).ap()

    K.x_in = semaphore("x_in")
    K.gain_in = semaphore("gain_in")
    K.par_in = semaphore("par_in")
    K.ones_ok = semaphore("ones_ok")
    K.zero_ok = semaphore("zero_ok")
    K.tab_zeroed = semaphore("tab_zeroed")
    K.tab_in = semaphore("tab_in")
    K.biasb_ok = semaphore("biasb_ok")
    K.w_hi = semaphore("w_hi")
    K.w_lo = semaphore("w_lo")
    K.small_in = semaphore("small_in")
    K.small_hi = semaphore("small_hi")
    K.small_lo = semaphore("small_lo")
    K.tile_full = semaphore("tile_full")
    K.tile_out = semaphore("tile_out")
    K.split_hi = semaphore("split_hi")
    K.split_lo = semaphore("split_lo")
    K.s_full = semaphore("s_full")
    K.s_taken = semaphore("s_taken")
    K.sq_ok = semaphore("sq_ok")
    K.sum_ok = semaphore("sum_ok")
    K.gx_hi = semaphore("gx_hi")
    K.gx_lo = semaphore("gx_lo")
    K.stat_sqrt = semaphore("stat_sqrt")
    K.prior_ok = semaphore("prior_ok")
    K.gain_ok = semaphore("gain_ok")
    K.next_ok = semaphore("next_ok")
    K.stat_rec = semaphore("stat_rec")
    K.stat_diag = semaphore("stat_diag")
    K.x_fin = semaphore("x_fin")
    K.max_ok = semaphore("max_ok")
    K.exp_ok = semaphore("exp_ok")
    K.rden_ok = semaphore("rden_ok")
    K.probs_ok = semaphore("probs_ok")
    K.trans_full = semaphore("trans_full")
    K.pt_hi = semaphore("pt_hi")
    K.pt_lo = semaphore("pt_lo")
    K.pv_done = semaphore("pv_done")
    K.qk_hi = semaphore("qk_hi")
    K.sig_ok = semaphore("sig_ok")
    K.mix_ok = semaphore("mix_ok")
    K.up_sq = semaphore("up_sq")
    K.lp_ok = semaphore("lp_ok")
    K.lat_sq = semaphore("lat_sq")
    K.lat_sqrt = semaphore("lat_sqrt")
    K.lat_rec = semaphore("lat_rec")
    K.q_out = semaphore("q_out")
    K.k_out = semaphore("k_out")
    K.kpe_ok = semaphore("kpe_ok")
    K.head_sq = semaphore("head_sq")
    K.head_red = semaphore("head_red")
    K.head_v = semaphore("head_v")
    K.head_sqrt = semaphore("head_sqrt")
    K.head_rec = semaphore("head_rec")
    K.head_scaled = semaphore("head_scaled")
    K.rope_ok = semaphore("rope_ok")
    K.qk_ready = semaphore("qk_ready")
    K.pool_ok = semaphore("pool_ok")
    K.out_done = semaphore("out_done")
    K.y_hi = semaphore("y_hi")
    K.ab_hi = semaphore("ab_hi")
    K.w_in_sem = [semaphore(f"slab_in{i}") for i in range(2)]
    K.biasa_in = [semaphore(f"biasa_in{i}") for i in range(2)]
    K.biasb_in = [semaphore(f"biasb_in{i}") for i in range(2)]


def in_tiles():
    tiles = [(t // 2, t % 2, "q", ("qa", t)) for t in range(HALF)]
    tiles += [(2, 0, "k", ("ka", 0)), (2, 1, "tm", ("va", 0))]
    tiles += [(3 + t // 2, t % 2, "q", ("qb", t)) for t in range(HALF)]
    tiles += [(5 + t // 2, t % 2, "k", ("kb", t)) for t in range(HALF)]
    tiles += [(7 + t // 2, t % 2, "tm", ("vb", t)) for t in range(HALF)]
    return tiles


IN_TILES = in_tiles()
IN_ENDS = [F_IN + 1 + max(i for i, t in enumerate(IN_TILES) if t[0] == j) for j in range(9)]


def in_dest(K, to, part):
    name, t = to
    if name == "qa":
        return K.qa[:, part, t, :]
    if name == "qb":
        return K.qb[:, part, t, :].rearrange("p (i c) -> p i c", c=P)[:, :, ::-1]
    if name == "kb":
        return K.kb[:, part, t, :]
    if name == "ka":
        return K.ka[:, part, :]
    if name == "va":
        return K.va[:, part, :, :]
    return K.vb[:, part, 2 * (t % 2):2 * (t % 2) + 2, (t // 2) * SCOL:(t // 2 + 1) * SCOL]


def in_shape(to, ap):
    if to[0] in ("va", "qb"):
        return ap.rearrange("p (t c) -> p t c", t=TT)
    if to[0] == "vb":
        return ap.rearrange("p (t c) -> p t c", t=2)
    return ap


class Heads:

    def __init__(self, K, kind, layer=0):
        self.kind = kind
        self.u0 = {"A": Num(U_A), "B": Num(U_B), "L": Num(U_L, (layer, UL))}[kind]
        self.s0 = {"A": Num(S_A), "B": Num(S_B), "L": Num(S_L + 4, (layer, SL))}[kind]
        self.g0 = {"A": Num(G_A), "B": Num(G_B), "L": Num(G_L + 40, (layer, GL))}[kind]
        self.f0 = Num(F_L + 40, (layer, FL)) if kind == "L" else None
        self.K = K

    def where(self, n):
        h, i = divmod(n, TT)
        lo, hi = (max(0, i - 1), min(TT, i + 2)) if self.kind == "A" else (0, TT)
        return h // 2, h % 2, i, lo, hi

    def g_out(self, h):
        return self.g0 + (h if self.kind != "L" else (6 + 3 * h if h < HEADS - 2 else 2 * HEADS + h))

    def g_qk(self, h):
        return self.g0 + (2 * h if h < 2 else 4 + 3 * (h - 2))

    def pairs(self, m):
        return self.u0 // 2 + m + 1

    def last_of(self, n):
        return (n - 6) // TT if n >= 6 and n % TT == 2 else None

    def turned(self, n):
        h = n // TT + 1
        return h if self.kind == "L" and n % TT == 0 and 2 <= h < HEADS else None

    def rows(self, ap):
        return ap.rearrange("p (i c) -> p i c", c=P)

    def in_order(self, ap):
        return self.rows(ap)[:, :, ::-1] if self.kind == "B" else self.rows(ap)

    def first(self):
        return 1 if self.kind == "A" else 0


def program_sync(nc, sp, K):
    a = K.a

    def slab(j, pieces, pairs=None):
        if (j - 1).due():
            sp.wait_ge(K.w_lo, (j - 1).value())
        if pairs is not None:
            sp.wait_ge(K.pv_done, pairs.value())
        sp.wait_ge(K.x_in, 16 * TT)
        inc = 64 // len(pieces(K.raw[:, j % 2, :]))
        for dst, src, *n in pieces(K.raw[:, j % 2, :]):
            sp.dma_start(dst, src).then_inc(K.w_in_sem[j % 2], n[0] if n else inc)

    def columns(w, c0, rows=None):
        src = w.rearrange("(k p) n -> p k n", p=P)[:, :, c0] if not isinstance(c0, int) else \
            w.rearrange("(k p) n -> p k n", p=P)[:, :, c0:c0 + SCOL]

        def pieces(raw):
            dst = raw.rearrange("p (k n) -> p k n", k=KT)
            return [(dst[:, 0:4, :], src[:, 0:4, :]), (dst[:, 4:8, :], src[:, 4:8, :])]
        return pieces

    def qa_columns(s):
        src = a["w_in"][0].rearrange("(k p) n -> p k n", p=P)

        def pieces(raw):
            dst = raw.rearrange("p (k n) -> p k n", k=KT)
            out = []
            for m in range(2):
                for e in range(2):
                    c = QA0 + e * HALF * HD + (2 * s + m) * HD
                    out.append((dst[:, :, m * P + e * HD:m * P + (e + 1) * HD], src[:, :, c:c + HD]))
            return out
        return pieces

    def pair(wa, wb, c0, permuted):
        def cols(w):
            return w[:, c0] if not isinstance(c0, int) else w[:, c0:c0 + SCOL]

        def pieces(raw):
            dst = raw.rearrange("p (k n) -> p k n", k=KT)
            second = (dst[:, HALF:KT, :], cols(wb).rearrange("(k p) n -> p k n", p=P), 32)
            if not permuted:
                return [(dst[:, 0:HALF, :], cols(wa).rearrange("(k p) n -> p k n", p=P), 32), second]
            rows = cols(wa).rearrange("(e k p) n -> e p k n", e=2, p=HD)
            return [(dst[e * HD:(e + 1) * HD, 0:HALF, :], rows[e], 16) for e in range(2)] + [second]
        return pieces

    xs = a["x"][0].rearrange("(t p) d -> p t d", p=P)
    for t in range(TT):
        sp.dma_start(K.xin[:, t, :], xs[:, t, :]).then_inc(K.x_in, 16)

    def in_slab(j):
        if j < 2:
            slab(Num(j), qa_columns(j))
        else:
            c0 = [KVA0, QB0, QB0 + SCOL, KB0, KB0 + SCOL, VB0, VB0 + SCOL][j - 2]
            slab(Num(j), columns(a["w_in"][0], c0))

    for j in range(3):
        in_slab(j)
    sp.wait_ge(K.zero_ok, 1)
    sp.dma_start(K.tab.rearrange("(p n) -> p n", p=P), K.zero[:, :]).then_inc(K.tab_zeroed, 16)
    sp.wait_ge(K.tab_zeroed, 16)
    rows = K.tab[TAB_PAD:TAB_PAD + HEADS * TAB_H].rearrange("(r c) -> r c", c=GRID_W)
    sp.dma_start(rows[:, 0:2 * KW - 1], a["rpb"][0].rearrange("h r c -> (h r) c")).then_inc(K.tab_in, 16)
    for j in range(3, 9):
        in_slab(j)
    slab(Num(J_MERGE), columns(a["w_in"][0], GA0))
    slab(Num(J_MERGE + 1), columns(a["w_in"][0], GB0))

    for h in range(HEADS):
        if h >= 2:
            sp.wait_ge(K.s_taken, S_A + TT * (h - 1))
        head = (h % 2) * HALF + h // 2
        sp.dma_start(K.biasa[:, h % 2, :], a["alibi"][head]).then_inc(K.biasa_in[h % 2], 16)
    sp.wait_ge(K.tab_in, 16)
    for h in range(HEADS):
        if h >= 2:
            sp.wait_ge(K.s_taken, S_B + TT * (h - 1))
        start = TAB_PAD + h * TAB_H + GRID_W + KW - 1 - (P - 1)
        src = bass.AP(K.tab.tensor, start, [[1, P], [1, BIAS_ROWS * GRID_W]])
        sp.dma_start(K.biasb[:, h % 2, :], src).then_inc(K.biasb_in[h % 2], 16)
    sp.wait_ge(K.pv_done, HEADS * TT)
    for i in range(4):
        if i:
            slab(Num(J_MERGE + 3 * i), columns(a["w_in"][0], GA0 + i * SCOL))
            slab(Num(J_MERGE + 3 * i + 1), columns(a["w_in"][0], GB0 + i * SCOL))
        slab(Num(J_MERGE + 3 * i + 2), pair(a["w_proj_a"][0], a["w_proj_b"][0], i * SCOL, True))
    for i in range(4):
        slab(Num(J_OUT + i), columns(a["w_out"][0], i * SCOL))
    with sp.Fori(0, CHUNKS) as c:
        for i in range(4):
            slab(Num(J_MLP + i, (c, 8)), columns(a["w_up"][0], bass.ds(c * D + i * SCOL, SCOL)))
        for i in range(4):
            down = a["w_down"][0][bass.ds(c * D, D), :]
            slab(Num(J_MLP + 4 + i, (c, 8)), columns(down, i * SCOL))

    with sp.Fori(0, LAYERS) as l:
        def of(w):
            return w[bass.ds(l, 1)].rearrange("o r c -> (o r) c")

        j0 = Num(J_L, (l, JL))
        w_in = of(a["w_in_2"])
        for k, c0 in enumerate((CQ0, CKV0)):
            slab(j0 + k, columns(w_in, c0))
        small(sp, K, l, w_in)
        slab(j0 + 2, lambda raw: [(raw[:, 0:2 * HEADS * QK].rearrange("p (k n) -> p k n", k=2),
                                   of(a["w_uq_2"]).rearrange("(k p) n -> p k n", p=P))])
        slab(j0 + 3, lambda raw: [(raw.rearrange("p (k n) -> p k n", k=2),
                                   of(a["w_ukv_2"]).rearrange("(k p) n -> p k n", p=P))])
        for k, c0 in enumerate((UF0, UF0 + SCOL, ZF0, ZF0 + SCOL)):
            slab(j0 + 4 + k, columns(w_in, c0))
        for k in range(2):
            slab(j0 + 8 + k, lambda raw: [(raw.rearrange("p (k n) -> p k n", k=TT),
                                           a["dft_seq"][k].rearrange("(k p) n -> p k n", p=P))])
        slab(j0 + 10, columns(w_in, ZA0))
        slab(j0 + 11, columns(w_in, ZA0 + SCOL), Num(U_L // 2 + UL // 2, (l, UL // 2)))
        for i in range(4):
            slab(j0 + 12 + 3 * i, columns(w_in, MA0 + i * SCOL))
            slab(j0 + 13 + 3 * i, columns(w_in, MF0 + i * SCOL))
            slab(j0 + 14 + 3 * i, pair(of(a["w_attn_proj_2"]), of(a["w_fourier_proj_2"]), i * SCOL, False))
        for i in range(4):
            slab(j0 + 24 + i, columns(of(a["w_out_2"]), i * SCOL))
    slab(Num(J_END), lambda raw: [(raw[:, 0:TAB // P], a["dft_seq"][0][0:P, 0:TAB // P])])

    os_ = K.out[0].rearrange("(t p) d -> p t d", p=P)
    g_end = G_L + LAYERS * GL
    for t in range(TT):
        sp.wait_ge(K.tile_out, g_end + 2 * t + 2)
        sp.dma_start(os_[:, t, :], K.xout[:, t, :]).then_inc(K.out_done, 16)
    sp.wait_ge(K.out_done, 16 * TT)


def small(sp, K, l, w_in):
    sp.wait_ge(K.split_lo, Num(H_L, (l, HL)).value())
    sp.wait_ge(K.x_in, 16 * TT)
    sp.dma_start(K.sraw[:, 0:SCOL], K.a["dft_dim"]).then_inc(K.small_in, 16)
    sp.dma_start(K.sraw[:, SCOL:2 * SCOL].rearrange("p (k n) -> p k n", k=KT),
                 w_in[:, KPE0:KPE0 + ROPE].rearrange("(k p) n -> p k n", p=P)).then_inc(K.small_in, 16)


def program_pool(nc, pool, K):
    nc.gpsimd.memset(K.zero[:, :], 0.0).then_inc(K.zero_ok, 1)
    nc.gpsimd.memset(K.ones[:, :], 1.0).then_inc(K.ones_ok, 1)

    def sums(norm):
        for k in range(1, KT):
            pool.wait_ge(K.sq_ok, (norm * KT + k + 1).value())
            if (norm * (KT - 1) + k - 1).due():
                pool.wait_ge(K.sum_ok, (norm * (KT - 1) + k - 1).value())
            nc.gpsimd.tensor_tensor(K.sumsq[:, :], K.sumsq[:, :], K.sq[:, k % 2, :], ALU.add).then_inc(K.sum_ok, 1)

    def probabilities(A):
        for n in range(HEADS * TT):
            _, _, _, lo, hi = A.where(n)
            if A.kind == "B" and n % TT == 0 and n // TT + 1 < HEADS:
                masked(n // TT + 1)
            c = slice(A.first(), A.first() + (hi - lo) * P)
            pool.wait_ge(K.rden_ok, (A.u0 + n + 1).value())
            p = K.t[:, n % 3, c]
            nc.gpsimd.tensor_tensor(p, p, K.rden[:, n % 4:n % 4 + 1].broadcast_to([P, (hi - lo) * P]),
                                    ALU.mult).then_inc(K.probs_ok, 1)

    def masked(h):
        pool.wait_ge(K.biasb_in[h % 2], 16 * (h // 2 + 1))
        b = K.biasb[:, h % 2, :].rearrange("p (r c) -> p r c", c=GRID_W)
        nc.gpsimd.tensor_tensor(b, b, K.mask[:, :].unsqueeze(1).broadcast_to([P, BIAS_ROWS, GRID_W]),
                                ALU.add).then_inc(K.biasb_ok, 1)

    def mixed(sig, h0, g0):
        for m in range(2):
            pool.wait_ge(K.tile_out, (g0 + 4 + 2 * m + 2).value())
            pool.wait_ge(K.split_lo, (h0 + m - 1).value())
            nc.gpsimd.tensor_tensor(K.t[:, m, :], sig[:, m, :], sig[:, 2 + m, :], ALU.add).then_inc(K.mix_ok, 1)

    def gain(l, q):
        pool.wait_ge(K.head_scaled, Num(q + 1, (l, 2)).value())
        v = K.qk[:, q, :, :].rearrange("p t (h c) -> p (t h) c", h=HEADS)
        g = K.lp[:, LP_HEAD + q * QK:LP_HEAD + (q + 1) * QK]
        nc.gpsimd.tensor_tensor(v, v, g.unsqueeze(1).broadcast_to([P, TT * HEADS, QK]),
                                ALU.mult).then_inc(K.qk_ready, 1)

    def rotate(l, q, i):
        half = ROPE // 2
        ts = slice(2 * i, 2 * i + 2)
        x = K.qk[:, q, ts, :].rearrange("p t (h c) -> p t h c", h=HEADS)
        x1, x2 = x[:, :, :, NOPE:NOPE + half], x[:, :, :, NOPE + half:QK]
        cos = K.rope[:, ts, 0:half].unsqueeze(2).broadcast_to([P, 2, HEADS, half])
        sin = K.rope[:, ts, half:ROPE].unsqueeze(2).broadcast_to([P, 2, HEADS, half])
        ra, rb, rc = [b.rearrange("p (t h c) -> p t h c", t=2, h=HEADS)
                      for b in (K.rt[:, 0, :], K.rt[:, 1, :], K.sumsq[:, 0:2 * P])]
        r = Num(12 * q + 6 * i, (l, 24))
        pool.wait_ge(K.qk_ready, Num(q + 1, (l, 2)).value())
        if r.due():
            pool.wait_ge(K.rope_ok, r.value())
        nc.gpsimd.tensor_tensor(ra, x1, cos, ALU.mult).then_inc(K.rope_ok, 1)
        nc.gpsimd.tensor_tensor(rb, x2, sin, ALU.mult).then_inc(K.rope_ok, 1)
        nc.gpsimd.tensor_tensor(rc, x1, sin, ALU.mult).then_inc(K.rope_ok, 1)
        nc.gpsimd.tensor_tensor(x2, x2, cos, ALU.mult).then_inc(K.rope_ok, 1)
        pool.wait_ge(K.rope_ok, (r + 4).value())
        nc.gpsimd.tensor_tensor(x1, ra, rb, ALU.subtract).then_inc(K.rope_ok, 1)
        nc.gpsimd.tensor_tensor(x2, x2, rc, ALU.add).then_inc(K.rope_ok, 1)

    def silu_f(l, t):
        pool.wait_ge(K.sig_ok, (sig_num(l, t) + 1).value())
        nc.gpsimd.tensor_tensor(K.z[:, t, :], K.t[:, t % 3, :], K.sq[:, t % 2, :], ALU.mult).then_inc(K.pool_ok, 1)

    sums(Num(0))
    probabilities(Heads(K, "A"))
    pool.wait_ge(K.par_in, 16 * PAR_DMAS)
    masked(0)
    probabilities(Heads(K, "B"))
    for i in range(4):
        mixed(K.sig1, Num(H_MERGE + 2 * i), Num(G_MERGE + 8 * i))
    sums(Num(1))
    for k in range(1, KT):
        for i, (total, square) in enumerate(((K.sumsq_f, K.sq_f), (K.sumsq, K.sq))):
            n = 2 * (KT - 1) + 2 * (k - 1) + i
            pool.wait_ge(K.sq_ok, 2 * KT + 2 * k + i + 1)
            if n >= 2:
                pool.wait_ge(K.sum_ok, n - 1)
            nc.gpsimd.tensor_tensor(total[:, :], total[:, :], square[:, k % 2, :], ALU.add).then_inc(K.sum_ok, 1)
    with pool.Fori(0, LAYERS) as l:
        gain(l, 0)
        rotate(l, 0, 0)
        silu_f(l, 0)
        silu_f(l, 1)
        rotate(l, 0, 1)
        silu_f(l, 2)
        silu_f(l, 3)
        gain(l, 1)
        rotate(l, 1, 0)
        rotate(l, 1, 1)
        probabilities(Heads(K, "L", l))
        for t in range(HALF):
            pool.wait_ge(K.sig_ok, (sig_num(l, 4 + t) + 1).value())
            nc.gpsimd.tensor_tensor(K.sq[:, t % 2, :], K.sq[:, t % 2, :], K.t[:, t % 3, :],
                                    ALU.mult).then_inc(K.pool_ok, 1)
            pool.wait_ge(K.pool_ok, Num(4 + 2 * t + 1, (l, 12)).value())
            nc.gpsimd.tensor_tensor(K.t[:, t % 3, :], K.sq[:, t % 2, :], K.z[:, t, :],
                                    ALU.mult).then_inc(K.pool_ok, 1)
        for i in range(4):
            mixed(K.sig2, Num(H_L + 24 + 2 * i, (l, HL)), Num(G_L + 68 + 8 * i, (l, GL)))
        sums(Num(4, (l, 1)))


def sig_num(l, k):
    return Num(16 + k, (l, 24))


def program_act(nc, act, K):
    a = K.a
    def by_feature(v):
        return v.rearrange("(k p) -> p k", p=P)

    act.dma_start(K.ident[:, :], a["ident"]).then_inc(K.gain_in, 16)
    for i, g in enumerate((a["norm_mix"][0], a["norm_mlp"][0], a["norm_final"])):
        act.dma_start(K.gains[:, i, :], by_feature(g), allow_slow_non_contiguous=True).then_inc(K.gain_in, 16)
    act.dma_start(K.mask[:, :], a["mask"]).then_inc(K.par_in, 16)
    act.dma_start(K.bg[:, :], by_feature(a["b_gate"][0]), allow_slow_non_contiguous=True).then_inc(K.par_in, 16)
    act.dma_start(K.sink[:, :], a["sink"][0].partition_broadcast(P)).then_inc(K.par_in, 16)
    act.dma_start(K.rope[:, :, :], a["rope"].rearrange("(t p) c -> p t c", p=P)).then_inc(K.par_in, 16)
    for l in range(LAYERS + 1):
        act.dma_start(K.norm_all[:, l, :], by_feature(a["norm_g_2"][min(l, LAYERS - 1)]),
                      allow_slow_non_contiguous=True).then_inc(K.par_in, 16)
    for l in range(LAYERS):
        for c, n, src in ((LP_MERGE, KT, by_feature(a["b_merge_2"][l, 0])),
                          (LP_MERGE + KT, KT, by_feature(a["b_merge_2"][l, 1])),
                          (LP_LAT, 2, by_feature(a["q_latent_g_2"][l])),
                          (LP_LAT + 2, 2, by_feature(a["kv_latent_g_2"][l]))):
            act.dma_start(K.lp_all[:, l, c:c + n], src, allow_slow_non_contiguous=True).then_inc(K.par_in, 16)
        for c, g in ((LP_HEAD, a["q_head_g_2"]), (LP_HEAD + QK, a["k_head_g_2"])):
            act.dma_start(K.lp_all[:, l, c:c + QK], g[l].partition_broadcast(P)).then_inc(K.par_in, 16)

    def split(j, used):
        act.wait_ge(K.w_in_sem[j % 2], ((j // 2 + 1) * 64).value())
        if used.due():
            act.wait_ge(K.tile_full, used.value())
        nc.scalar.activation(K.w[:, j % 2, 0, :], K.raw[:, j % 2, :], ACT.Copy).then_inc(K.w_hi, 1)

    def norm_tile(norm, k, gains, ready):
        act.wait_ge(K.tile_out, ready.value())
        if k > 2:
            act.wait_ge(K.sum_ok, (norm * (KT - 1) + k - 2).value())
        nc.scalar.activation(K.sq[:, k % 2, :] if k else K.sumsq[:, :], K.x[:, k, :],
                             ACT.Square).then_inc(K.sq_ok, 1)
        nc.scalar.activation(K.gx[:, 0, k, :], K.x[:, k, :], ACT.Copy,
                             scale=gains[:, k:k + 1]).then_inc(K.gx_hi, 1)

    def final_tile(k, ready):
        act.wait_ge(K.tile_out, ready.value())
        if k > 2:
            act.wait_ge(K.sum_ok, 2 * (KT - 1) + 2 * (k - 2))
        gain = K.gains[:, 2, k:k + 1]
        nc.scalar.activation(K.sq_f[:, k % 2, :] if k else K.sumsq_f[:, :], K.x[:, k, :],
                             ACT.Square).then_inc(K.sq_ok, 1)
        nc.scalar.activation(K.sq[:, k % 2, :] if k else K.sumsq[:, :], K.x[:, k, :], ACT.Square,
                             scale=gain).then_inc(K.sq_ok, 1)
        nc.scalar.activation(K.gx[:, 0, k, :], K.x[:, k, :], ACT.Copy,
                             scale=K.gains[:, 3, k:k + 1]).then_inc(K.gx_hi, 1)

    def stat(norm, s):
        act.wait_ge(K.s_taken, (s + 1).value())
        nc.scalar.activation(K.d4[:, :], K.v4[:, :], ACT.Sqrt).then_inc(K.stat_sqrt, 1)

    def hi(dst, src):
        nc.scalar.activation(dst, src, ACT.Copy).then_inc(K.split_hi, 1)

    def attention(A, midway=None):
        U, S = A.u0, A.s0

        def exps(n):
            _, _, _, lo, hi_ = A.where(n)
            width = A.first() + (hi_ - lo) * P
            act.wait_ge(K.max_ok, (U + n + 1).value())
            if (U + n - 2).due():
                act.wait_ge(K.trans_full, (U + n - 2).value())
            src = K.S[(S + n) % 2][:, :] if A.kind == "L" else K.sq[:, n % 2, 0:width]
            scale = float(QK) ** -0.5 if A.kind == "L" else 1.0
            e = nc.scalar.activation(K.t[:, n % 3, 0:width], src, ACT.Exp, bias=K.nm[:, n % 4:n % 4 + 1],
                                     scale=scale, accum_out=K.den[:, n % 4:n % 4 + 1])
            e.then_inc(K.exp_ok, 1)

        def qk_hi(h):
            for q in range(2):
                act.wait_ge(K.tile_full, (A.f0 + 2 * h + q + 1).value())
                nc.scalar.activation(K.qkh[0:QK, h % 2, q, 0, :], K.G[(A.g_qk(h) + q) % GB][0:QK, :],
                                     ACT.Copy).then_inc(K.qk_hi, 1)

        def out_hi(h):
            act.wait_ge(K.pv_done, A.pairs(2 * h + 1).value())
            t, e = h // 2, h % 2
            r = slice(e * HD, (e + 1) * HD)
            q = K.qa if A.kind == "A" else K.qb
            nc.scalar.activation(A.rows(q[r, 0, t, :]), A.in_order(K.G[A.g_out(h) % GB][r, :]), ACT.Copy).then_inc(K.y_hi, 1)

        if A.kind == "L":
            qk_hi(0)
        exps(0)
        if A.kind == "L":
            qk_hi(1)
        exps(1)
        for n in range(HEADS * TT):
            if n == MIDWAY and midway is not None:
                midway()
            if A.turned(n) is not None:
                qk_hi(A.turned(n))
            if A.last_of(n) is not None and A.kind != "L":
                out_hi(A.last_of(n))
            if n + 2 < HEADS * TT:
                exps(n + 2)
            m, e = n // 2, n % 2
            _, _, _, lo, hi_ = A.where(n)
            act.wait_ge(K.trans_full, (U + n + 1).value())
            if A.pairs(m - 2).due():
                act.wait_ge(K.pv_done, A.pairs(m - 2).value())
            nc.scalar.activation(K.pt[A.kind][m % 2][:, 0, lo:hi_, e, :],
                                 K.T[(U + n) % 2][:, 0:(hi_ - lo) * P].rearrange("p (k c) -> p k c", c=P),
                                 ACT.Copy).then_inc(K.pt_hi, 1)
        if A.kind != "L":
            out_hi(HEADS - 1)

    def sigmoid(dst, src, bias=0.0):
        nc.scalar.activation(dst, src, ACT.Sigmoid, bias=bias).then_inc(K.sig_ok, 1)

    def merge(sig, dst, bias, j, g, f, mix, pair_):
        for b in range(2):
            split(j + b + 1, f + 2 * b)
            for k in range(2):
                col = b * KT + 2 * pair_ + k
                act.wait_ge(K.tile_out, (g + 2 * b + k + 1).value())
                sigmoid(sig[:, 2 * b + k, :], sig[:, 2 * b + k, :], bias=bias[:, col:col + 1])
        split(j + 3, f + 4)
        for k in range(2):
            act.wait_ge(K.mix_ok, (mix + k + 1).value())
            hi(dst[:, 0, 2 * pair_ + k, :], K.t[:, k, :])

    split(Num(0), Num(0))
    act.wait_ge(K.gain_in, 16 * GAIN_DMAS)
    for k in range(KT):
        norm_tile(Num(0), k, K.gains[:, 0, :], Num(G_X + k + 1))
    act.wait_ge(K.par_in, 16 * PAR_DMAS)
    last = -1
    for k, (j, _, form, to) in enumerate(IN_TILES):
        if j != last:
            split(Num(j + 1), Num(IN_ENDS[j - 1] if j else 0))
            last = j
        if k == 0:
            stat(Num(0), Num(0))
        act.wait_ge(K.tile_out, Num(G_IN + k + 1).value())
        hi(in_dest(K, to, 0), in_shape(to, K.t[:, k % 3, :]))
    attention(Heads(K, "A"))
    attention(Heads(K, "B"))
    for i in range(4):
        merge(K.sig1, K.big, K.bg, Num(J_MERGE + 3 * i), Num(G_MERGE + 8 * i), Num(F_MERGE + 8 * i), Num(2 * i), i)
    for i in range(4):
        split(Num(J_OUT + i + 1), Num(F_OUT + 2 * i))
        for k in range(2 * i, 2 * i + 2):
            norm_tile(Num(1), k, K.gains[:, 1, :], Num(G_OUT + k + 1))
    stat(Num(1), Num(S_N2))

    def chunk(c, last=False):
        for i in range(8):
            split(Num(J_MLP + i + 1, (c, 8)), Num(F_MLP + 2 * i, (c, 16)))
            for k in range(2 * i, 2 * i + 2):
                if i < 4:
                    h = Num(H_MLP + k, (c, 8))
                    act.wait_ge(K.tile_out, Num(G_MLP + k + 1, (c, 16)).value())
                    act.wait_ge(K.split_lo, (h - 1).value())
                    nc.scalar.activation(K.sq[:, k % 2, :], K.t[:, k % 3, :], ACT.Square).then_inc(K.up_sq, 1)
                    nc.scalar.activation(K.big[:, 0, k, :], K.t[:, k % 3, :], ACT.Square).then_inc(K.split_hi, 1)
                elif last:
                    final_tile(k - KT, Num(G_MLP + k + 1, (c, 16)))

    with act.Fori(0, CHUNKS - 1) as c:
        chunk(c)
    act.wait_ge(K.gain_ok, 1)
    chunk(CHUNKS - 1, True)
    stat(Num(2), Num(S_NF))
    with act.Fori(0, LAYERS) as l:
        j, g, f, h, s = (Num(n, (l, per)) for n, per in ((J_L, JL), (G_L, GL), (F_L, FL), (H_L, HL), (S_L, SL)))
        act.wait_ge(K.lp_ok, Num(1, (l, 1)).value())
        act.wait_ge(K.small_in, Num(32, (l, 32)).value())
        nc.scalar.activation(K.sw[:, 0, :], K.sraw[:, :], ACT.Copy).then_inc(K.small_hi, 1)
        act.wait_ge(K.prior_ok, Num(3, (l, 4)).value())
        nc.scalar.activation(K.d4[:, :], K.v4[:, :], ACT.Sqrt).then_inc(K.stat_sqrt, 1)
        squares = [K.sq[:, 0, :], K.sq[:, 1, :], K.hsq[:, 0, 0:SEQ], K.hsq[:, 1, 0:SEQ]]
        for k in range(4):
            if k % 2 == 0:
                split(j + k // 2 + 1, f + 2 * (k // 2 + 1) - 2)
            act.wait_ge(K.tile_out, (g + k + 1).value())
            nc.scalar.activation(squares[k], K.t[:, k % 3, :], ACT.Square).then_inc(K.lat_sq, 1)
            nc.scalar.activation(K.u[:, 0, k, :], K.t[:, k % 3, :], ACT.Copy,
                                 scale=K.lp[:, LP_LAT + k:LP_LAT + k + 1]).then_inc(K.split_hi, 1)
        split(j + 3, f + 4)
        act.wait_ge(K.s_taken, (s + 4).value())
        nc.scalar.activation(K.lat_d[:, :], K.lat_v[:, :], ACT.Sqrt).then_inc(K.lat_sqrt, 1)
        split(j + 4, f + 12)
        for t in range(TT):
            for half in range(2):
                k = 2 * t + half
                act.wait_ge(K.tile_out, (g + 12 + k + 1).value())
                hi(K.v[:, 0, t, half * SCOL:(half + 1) * SCOL], K.t[:, k % 3, 0:SCOL])
        for i in range(4):
            split(j + 5 + i, f + 20 + 2 * i)
            for k in range(2 * i, 2 * i + 2):
                for n in HEAD_SQUARES[k]:
                    q, t = divmod(n, TT)
                    act.wait_ge(K.tile_out, (g + (4, 12)[q] + 2 * t + 2).value())
                    if Num(n - 1, (l, 2 * TT)).due():
                        act.wait_ge(K.head_red, Num(n - 1, (l, 2 * TT)).value())
                    nc.scalar.activation(K.hsq[:, n % 2, :], K.qk[:, q, t, :], ACT.Square).then_inc(K.head_sq, 1)
                if i < 2:
                    act.wait_ge(K.tile_out, (g + 20 + k + 1).value())
                    hi(K.u[:, 0, k, :], K.t[:, k % 3, :])
                else:
                    if Num(k - 4 - 1, (l, 12)).due():
                        act.wait_ge(K.pool_ok, Num(k - 4 - 1, (l, 12)).value())
                    act.wait_ge(K.tile_out, (g + 20 + k + 1).value())
                    sigmoid(K.sq[:, k % 2, :], K.t[:, (k - 4) % 3, :])
                if k in HEAD_ROOT:
                    q = HEAD_ROOT[k]
                    act.wait_ge(K.head_v, Num(q + 1, (l, 2)).value())
                    nc.scalar.activation(K.hd_[:, q, :], K.hs[:, q, :], ACT.Sqrt).then_inc(K.head_sqrt, 1)
        gi = 28
        for stage, grp in FOURIER:
            if (stage, grp) == ("seq", 0):
                split(j + 9, f + 28)
            if stage == "dim":
                for half in range(2):
                    act.wait_ge(K.tile_full, (f + gi + 1).value())
                    nc.scalar.activation(K.ab[:, grp % 2, 0, 2 * half:2 * half + 2, :],
                                         K.G[(g + gi) % GB][:, :].rearrange("p (t c) -> p t c", t=2),
                                         ACT.Copy).then_inc(K.ab_hi, 1)
                    gi += 1
            else:
                act.wait_ge(K.tile_out, (g + gi + 1).value())
                hi(K.u[:, 0, grp, :], K.t[:, grp % 3, :])
                gi += 1
        attention(Heads(K, "L", l), lambda: split(j + 10, f + 40))
        for i in range(2):
            split(j + 11 + i, f + 56 + 2 * i)
            for t in range(2 * i, 2 * i + 2):
                act.wait_ge(K.pool_ok, Num(4 + 2 * t - 2, (l, 12)).value())
                act.wait_ge(K.tile_out, (g + 64 + t + 1).value())
                sigmoid(K.sq[:, t % 2, :], K.t[:, t % 3, :])
                act.wait_ge(K.pool_ok, Num(4 + 2 * t + 2, (l, 12)).value())
                hi(K.v[:, 0, t, :], K.t[:, t % 3, :])
        for i in range(4):
            merge(K.sig2, K.m2, K.lp[:, LP_MERGE:LP_MERGE + 2 * KT], j + 12 + 3 * i, g + 68 + 8 * i,
                  f + 60 + 8 * i, Num(KT + 2 * i, (l, KT)), i)
        for i in range(4):
            split(j + 24 + i + 1, f + 92 + 2 * i)
            if i == 0:
                act.wait_ge(K.next_ok, Num(1, (l, 1)).value())
            for k in range(2 * i, 2 * i + 2):
                norm_tile(Num(4, (l, 1)), k, K.norm_next, g + 100 + k + 1)


def program_vector(nc, dve, K):
    def split(j):
        dve.wait_ge(K.w_hi, (j + 1).value())
        s = j % 2
        nc.vector.tensor_tensor(K.w[:, s, 1, :], K.raw[:, s, :], K.w[:, s, 0, :].bitcast(F32),
                                ALU.subtract).then_inc(K.w_lo, 1)

    def lo(dst, src, hi, h):
        dve.wait_ge(K.split_hi, (h + 1).value())
        nc.vector.tensor_tensor(dst, src, hi.bitcast(F32), ALU.subtract).then_inc(K.split_lo, 1)

    def lo_gain(dst, src, gain, hi, done):
        nc.vector.scalar_tensor_tensor(out=dst, in0=src, scalar=gain, in1=hi.bitcast(F32), op0=ALU.mult,
                                       op1=ALU.subtract).then_inc(done, 1)

    def gx_lo(k, gains, gx):
        dve.wait_ge(K.gx_hi, (gx + k + 1).value())
        lo_gain(K.gx[:, 1, k, :], K.x[:, k, :], gains[:, k:k + 1], K.gx[:, 0, k, :], K.gx_lo)

    def full(f):
        dve.wait_ge(K.tile_full, (f + 1).value())

    def psum(g):
        return K.G[g % GB]

    def normed(dst, g, f, scale=1.0):
        full(f)
        nc.vector.scalar_tensor_tensor(out=dst, in0=psum(g)[:, :], scalar=scale, in1=K.rstd[:, :], op0=ALU.mult,
                                       op1=ALU.mult).then_inc(K.tile_out, 1)

    def rsqrt(y, root, v, sem, n):
        nc.vector.reciprocal(y, root).then_inc(sem, 1)
        dve.wait_ge(sem, (n + 1).value())
        nc.vector.tensor_tensor(root, y, y, ALU.mult).then_inc(sem, 1)
        dve.wait_ge(sem, (n + 2).value())
        nc.vector.scalar_tensor_tensor(out=root, in0=root, scalar=-0.5, in1=v, op0=ALU.mult, op1=ALU.mult).then_inc(sem, 1)
        dve.wait_ge(sem, (n + 3).value())
        nc.vector.scalar_tensor_tensor(out=y, in0=root, scalar=1.5, in1=y, op0=ALU.add, op1=ALU.mult).then_inc(sem, 1)
        dve.wait_ge(sem, (n + 4).value())

    def stat(norm, s):
        dve.wait_ge(K.s_full, (s + 1).value())
        nc.vector.tensor_scalar(K.v4[:, :], K.S[s % 2][:, 0:TT], 1.0 / D, EPS, ALU.mult, ALU.add).then_inc(K.s_taken, 1)
        dve.wait_ge(K.stat_sqrt, (norm + 1).value())
        rsqrt(K.r4[:, :], K.d4[:, :], K.v4[:, :], K.stat_rec, norm * 4)
        spread(norm, s)

    def spread(norm, s):
        diag = K.sq[:, 0, :].rearrange("p (t c) -> p t c", t=TT)
        nc.vector.tensor_tensor(diag, K.ident[:, :].unsqueeze(1).broadcast_to([P, TT, P]),
                                K.r4[:, :].unsqueeze(2).broadcast_to([P, TT, P]), ALU.mult).then_inc(K.stat_diag, 1)
        dve.wait_ge(K.s_full, (s + 2).value())
        nc.vector.tensor_copy(K.rstd[:, :], K.S[(s + 1) % 2][:, :]).then_inc(K.s_taken, 1)
        dve.wait_ge(K.s_taken, (s + 2).value())

    def layer_stat(l, s):
        norm = Num(3, (l, 1))
        dve.wait_ge(K.prior_ok, Num(1, (l, 4)).value())
        nc.vector.tensor_tensor(K.prior2[:, :], K.prior[:, :], K.prior[:, :], ALU.mult).then_inc(K.prior_ok, 1)
        dve.wait_ge(K.s_full, (s + 1).value())
        dve.wait_ge(K.prior_ok, Num(2, (l, 4)).value())
        nc.vector.scalar_tensor_tensor(out=K.v4[:, :], in0=K.S[s % 2][:, 0:TT], scalar=1.0 / D, in1=K.prior2[:, :],
                                       op0=ALU.mult, op1=ALU.mult).then_inc(K.s_taken, 1)
        dve.wait_ge(K.s_taken, (s + 1).value())
        nc.vector.tensor_scalar(K.v4[:, :], K.v4[:, :], EPS, None, ALU.add).then_inc(K.prior_ok, 1)
        dve.wait_ge(K.stat_sqrt, (norm + 1).value())
        rsqrt(K.r4[:, :], K.d4[:, :], K.v4[:, :], K.stat_rec, norm * 4)
        nc.vector.tensor_tensor(K.r4[:, :], K.r4[:, :], K.prior[:, :], ALU.mult).then_inc(K.prior_ok, 1)
        dve.wait_ge(K.prior_ok, Num(4, (l, 4)).value())
        spread(norm, s)
        nc.vector.memset(K.prior[:, :], 1.0).then_inc(K.prior_ok, 1)

    def attention(A, midway=None):
        U, S = A.u0, A.s0
        total = HEADS * TT

        def scores(n):
            h = n // TT
            t, e, i, b0, b1 = A.where(n)
            bank = K.S[(S + n) % 2]
            c = slice(A.first(), A.first() + (b1 - b0) * P)
            m = K.mx[:, n % 4:n % 4 + 1]
            if A.kind == "L":
                dve.wait_ge(K.s_full, (S + n + 1).value())
                nc.vector.tensor_reduce(m, bank[:, :], AX_X, ALU.max).then_inc(K.s_taken, 1)
                return
            if (U + n - 1).due():
                dve.wait_ge(K.exp_ok, (U + n - 1).value())
            first = -3.0e38
            if A.kind == "A":
                head = e * HALF + t
                dve.wait_ge(K.biasa_in[h % 2], 16 * (h // 2 + 1))
                off = (b0 - i + 1) * P
                bias = K.biasa[:, h % 2, off:off + (b1 - b0) * P]
                first = K.sink[:, head:head + 1]
                nc.vector.tensor_copy(K.sq[:, n % 2, 0:1], first)
            else:
                dve.wait_ge(K.biasb_ok, h + 1)
                off = (KH - 2 - 2 * i) * GRID_W
                bias = K.biasb[:, h % 2, off:off + SEQ]
            dve.wait_ge(K.s_full, (S + n + 1).value())
            nc.vector.tensor_tensor_reduce(K.sq[:, n % 2, c], bank[:, 0:(b1 - b0) * P], bias, 1.0, first,
                                           ALU.add, ALU.max, m).then_inc(K.s_taken, 1)

        def negate(n):
            c = slice(n % 4, n % 4 + 1)
            dve.wait_ge(K.s_taken, (S + n + 1).value())
            scale = -float(QK) ** -0.5 if A.kind == "L" else -1.0
            nc.vector.tensor_scalar(K.nm[:, c], K.mx[:, c], scale, None, ALU.mult).then_inc(K.max_ok, 1)

        def rden(n):
            c = slice(n % 4, n % 4 + 1)
            dve.wait_ge(K.exp_ok, (U + n + 1).value())
            nc.vector.reciprocal(K.rden[:, c], K.den[:, c]).then_inc(K.rden_ok, 1)

        def out(h):
            g = A.g_out(h)
            t, e = h // 2, h % 2
            r = slice(e * HD, (e + 1) * HD)
            if A.kind == "L":
                dve.wait_ge(K.pv_done, A.pairs(2 * h + 1).value())
                nc.vector.tensor_copy(K.z[r, t, :], psum(g)[r, :]).then_inc(K.tile_out, 1)
                return
            q = K.qa if A.kind == "A" else K.qb
            dve.wait_ge(K.y_hi, (0 if A.kind == "A" else HEADS) + h + 1)
            nc.vector.tensor_tensor(A.rows(q[r, 1, t, :]), A.in_order(psum(g)[r, :]), A.rows(q[r, 0, t, :]).bitcast(F32),
                                    ALU.subtract).then_inc(K.tile_out, 1)

        def qk_lo(h):
            for q in range(2):
                dve.wait_ge(K.qk_hi, Num(2 * h + q + 1, *[(r, 2 * HEADS) for r, _ in U.terms]).value())
                nc.vector.tensor_tensor(K.qkh[0:QK, h % 2, q, 1, :], psum(A.g_qk(h) + q)[0:QK, :],
                                        K.qkh[0:QK, h % 2, q, 0, :].bitcast(F32), ALU.subtract).then_inc(K.tile_out, 1)

        def low(n):
            m, e = n // 2, n % 2
            _, _, _, b0, b1 = A.where(n)
            dve.wait_ge(K.pt_hi, (U + n + 1).value())
            nc.vector.tensor_tensor(K.pt[A.kind][m % 2][:, 1, b0:b1, e, :],
                                    K.T[(U + n) % 2][:, 0:(b1 - b0) * P].rearrange("p (k c) -> p k c", c=P),
                                    K.pt[A.kind][m % 2][:, 0, b0:b1, e, :].bitcast(F32), ALU.subtract).then_inc(K.pt_lo, 1)

        if A.kind == "L":
            qk_lo(0)
        for n in range(AHEAD):
            if n == 2 and A.kind == "L":
                qk_lo(1)
            scores(n)
            negate(n)
        rden(0)
        rden(1)
        for n in range(total):
            if n == MIDWAY and midway is not None:
                midway()
            if A.turned(n) is not None:
                qk_lo(A.turned(n))
            if n + AHEAD < total:
                scores(n + AHEAD)
            if A.last_of(n) is not None:
                out(A.last_of(n))
            if n + AHEAD < total:
                negate(n + AHEAD)
            if n + 2 < total:
                rden(n + 2)
            low(n)
        out(HEADS - 1)

    def merge(sig, dst, j, g, f, h, mix, sig0, pair_):
        for b in range(2):
            split(j + b + 1)
            for k in range(2):
                if b == 0:
                    if (mix + k - 1).due():
                        dve.wait_ge(K.mix_ok, (mix + k - 1).value())
                normed(sig[:, 2 * b + k, :], g + 2 * b + k, f + 2 * b + k)
        split(j + 3)
        for k in range(2):
            for b in range(2):
                n = 4 + 2 * k + b
                full(f + n)
                dve.wait_ge(K.sig_ok, (sig0 + 2 * b + k + 1).value())
                s = sig[:, 2 * b + k, :]
                nc.vector.tensor_tensor(s, psum(g + n)[:, :], s, ALU.mult).then_inc(K.tile_out, 1)
        for k in range(2):
            c = 2 * pair_ + k
            lo(dst[:, 1, c, :], K.t[:, k, :], dst[:, 0, c, :], h + k)

    split(Num(0))
    for k in range(KT + 1):
        if k < KT:
            full(Num(F_X + k))
            nc.vector.tensor_copy(K.x[:, k, :], psum(Num(G_X + k))[:, :]).then_inc(K.tile_out, 1)
        if k:
            if k == 1:
                dve.wait_ge(K.gain_in, 16 * GAIN_DMAS)
            gx_lo(k - 1, K.gains[:, 0, :], Num(0))
    def in_lo(k):
        to = IN_TILES[k][3]
        lo(in_dest(K, to, 1), in_shape(to, K.t[:, k % 3, :]), in_dest(K, to, 0), Num(H_IN + k))

    last = -1
    for k, (j, _, form, to) in enumerate(IN_TILES):
        if j != last:
            split(Num(j + 1))
            last = j
        if k == 0:
            stat(Num(0), Num(0))
        t = K.t[:, k % 3, :]
        g, f = Num(G_IN + k), Num(F_IN + k)
        if H_IN + k - 2 > 0:
            dve.wait_ge(K.split_lo, H_IN + k - 2)
        if form == "tm":
            tts = slice(0, TT) if to[0] == "va" else slice(2 * (to[1] % 2), 2 * (to[1] % 2) + 2)
            n = tts.stop - tts.start
            full(f)
            nc.vector.tensor_tensor(in_shape(to, t), in_shape(to, psum(g)[:, :]),
                                    K.r4[:, tts].unsqueeze(2).broadcast_to([P, n, SEQ // n]),
                                    ALU.mult).then_inc(K.tile_out, 1)
        else:
            normed(t, g, f, float(HD) ** -0.5 if form == "q" else 1.0)
        if k:
            in_lo(k - 1)
    in_lo(len(IN_TILES) - 1)
    dve.wait_ge(K.par_in, 16 * PAR_DMAS)
    attention(Heads(K, "A"))
    attention(Heads(K, "B"))
    for i in range(4):
        merge(K.sig1, K.big, Num(J_MERGE + 3 * i), Num(G_MERGE + 8 * i), Num(F_MERGE + 8 * i),
              Num(H_MERGE + 2 * i), Num(2 * i), Num(4 * i), i)

    def residual(k, g, f):
        full(f)
        nc.vector.tensor_tensor(K.x[:, k, :], psum(g)[:, :], K.x[:, k, :], ALU.add).then_inc(K.tile_out, 1)

    for i in range(4):
        split(Num(J_OUT + i + 1))
        for k in range(2 * i, 2 * i + 2):
            residual(k, Num(G_OUT + k), Num(F_OUT + k))
            if k:
                gx_lo(k - 1, K.gains[:, 1, :], Num(KT))
    gx_lo(KT - 1, K.gains[:, 1, :], Num(KT))
    stat(Num(1), Num(S_N2))
    nc.vector.tensor_tensor(K.gains[:, 3, :], K.gains[:, 2, :], K.norm_all[:, 0, :], ALU.mult).then_inc(K.gain_ok, 1)

    def chunk(c, last=False):
        def up_lo(k):
            lo(K.big[:, 1, k, :], K.sq[:, k % 2, :], K.big[:, 0, k, :], Num(H_MLP + k, (c, 8)))

        for i in range(8):
            split(Num(J_MLP + i + 1, (c, 8)))
            for k in range(2 * i, 2 * i + 2):
                g, f = Num(G_MLP + k, (c, 16)), Num(F_MLP + k, (c, 16))
                if i < 4:
                    full(f)
                    nc.vector.scalar_tensor_tensor(out=K.t[:, k % 3, :], in0=psum(g)[:, :], scalar=0.0, in1=K.rstd[:, :],
                                                   op0=ALU.max, op1=ALU.mult).then_inc(K.tile_out, 1)
                else:
                    residual(k - KT, g, f)
                    if last and k > KT:
                        gx_lo(k - KT - 1, K.gains[:, 3, :], Num(2 * KT))
                if 0 < k < KT:
                    up_lo(k - 1)
                if k == KT - 1:
                    up_lo(k)

    with dve.Fori(0, CHUNKS - 1) as c:
        chunk(c)
    dve.wait_ge(K.gain_ok, 1)
    chunk(CHUNKS - 1, True)
    gx_lo(KT - 1, K.gains[:, 3, :], Num(2 * KT))
    stat(Num(2), Num(S_NF))
    nc.vector.tensor_copy(K.prior[:, :], K.r4[:, :]).then_inc(K.prior_ok, 1)
    for k in range(KT):
        nc.vector.scalar_tensor_tensor(out=K.x[:, k, :], in0=K.x[:, k, :], scalar=K.gains[:, 2, k:k + 1],
                                       in1=K.rstd[:, :], op0=ALU.mult, op1=ALU.mult).then_inc(K.x_fin, 1)
    with dve.Fori(0, LAYERS) as l:
        j, g, f, h, s = (Num(n, (l, per)) for n, per in ((J_L, JL), (G_L, GL), (F_L, FL), (H_L, HL), (S_L, SL)))
        nc.vector.tensor_copy(K.lp[:, :], K.lp_all[:, bass.ds(l, 1), :].rearrange("p o c -> p (o c)")).then_inc(K.lp_ok, 1)
        dve.wait_ge(K.gx_lo, Num(3 * KT, (l, KT)).value())
        nc.vector.tensor_copy(K.norm_next[:, :], K.norm_all[:, bass.ds(l + 1, 1), :].rearrange("p o c -> p (o c)")).then_inc(K.next_ok, 1)
        dve.wait_ge(K.lp_ok, Num(1, (l, 1)).value())
        dve.wait_ge(K.x_fin, KT)
        dve.wait_ge(K.small_hi, Num(1, (l, 1)).value())
        nc.vector.tensor_tensor(K.sw[:, 1, :], K.sraw[:, :], K.sw[:, 0, :].bitcast(F32), ALU.subtract).then_inc(K.small_lo, 1)
        layer_stat(l, s)

        def lat_lo(k):
            dve.wait_ge(K.split_hi, (h + k + 1).value())
            lo_gain(K.u[:, 1, k, :], K.t[:, k % 3, :], K.lp[:, LP_LAT + k:LP_LAT + k + 1], K.u[:, 0, k, :], K.split_lo)

        for k in range(4):
            if k % 2 == 0:
                split(j + k // 2 + 1)
            if k == 3:
                dve.wait_ge(K.split_lo, (h + 1).value())
            normed(K.t[:, k % 3, :], g + k, f + k)
            if k:
                lat_lo(k - 1)
        lat_lo(3)
        dve.wait_ge(K.s_full, (s + 3).value())
        nc.vector.tensor_tensor(K.kpe[:, :, :], K.S[(s + 2) % 2][:, 0:TT * ROPE].rearrange("p (t c) -> p t c", t=TT),
                                K.r4[:, :].unsqueeze(2).broadcast_to([P, TT, ROPE]), ALU.mult).then_inc(K.s_taken, 1)
        dve.wait_ge(K.s_taken, (s + 3).value())
        nc.vector.tensor_copy(
            K.qk[:, 1, :, :].rearrange("p t (h c) -> p t h c", h=HEADS)[:, :, :, NOPE:QK],
            K.kpe[:, :, :].unsqueeze(2).broadcast_to([P, TT, HEADS, ROPE])).then_inc(K.kpe_ok, 1)
        dve.wait_ge(K.s_full, (s + 4).value())
        nc.vector.tensor_scalar(K.lat_v[:, :], K.S[(s + 3) % 2][:, 0:2 * TT], 1.0 / LAT, EPS, ALU.mult,
                                ALU.add).then_inc(K.s_taken, 1)
        split(j + 3)
        dve.wait_ge(K.lat_sqrt, Num(1, (l, 1)).value())
        rsqrt(K.lat_r[:, :], K.lat_d[:, :], K.lat_v[:, :], K.lat_rec, Num(0, (l, 4)))
        for t in range(TT):
            for half in range(2):
                k = 4 + 2 * t + half
                w = HEADS * QK // 2
                full(f + k)
                nc.vector.tensor_scalar(K.qk[:, 0, t, half * w:(half + 1) * w], psum(g + k)[:, 0:w],
                                        K.lat_r[:, t:t + 1], None, ALU.mult).then_inc(K.tile_out, 1)
        split(j + 4)
        def v_lo(i):
            t, c = i // 2, slice(i % 2 * SCOL, (i % 2 + 1) * SCOL)
            lo(K.v[:, 1, t, c], K.t[:, i % 3, 0:SCOL], K.v[:, 0, t, c], h + 4 + i)

        for t in range(TT):
            for half in range(2):
                i = 2 * t + half
                k = 12 + i
                n = HEADS // 2
                src = psum(g + k)[:, :].rearrange("p (h c) -> p h c", h=n)
                dst = K.qk[:, 1, t, :].rearrange("p (h c) -> p h c", h=HEADS)[:, half * n:(half + 1) * n, 0:NOPE]
                full(f + k)
                nc.vector.tensor_scalar(dst, src[:, :, 0:NOPE], K.lat_r[:, TT + t:TT + t + 1], None,
                                        ALU.mult).then_inc(K.k_out, 1)
                dve.wait_ge(K.split_lo, (h + 4 + i - 2).value())
                v = K.t[:, i % 3, 0:SCOL]
                nc.vector.tensor_scalar(v.rearrange("p (h c) -> p h c", h=n), src[:, :, NOPE:P],
                                        K.lat_r[:, TT + t:TT + t + 1], None, ALU.mult).then_inc(K.tile_out, 1)
                if i:
                    v_lo(i - 1)
        v_lo(2 * TT - 1)

        def u_lo(k):
            lo(K.u[:, 1, k, :], K.t[:, k % 3, :], K.u[:, 0, k, :], h + 12 + k)

        def head_scale(q):
            dve.wait_ge(K.head_sqrt, Num(q + 1, (l, 2)).value())
            rsqrt(K.hr[:, q, :], K.hd_[:, q, :], K.hs[:, q, :], K.head_rec, Num(4 * q, (l, 8)))
            v = K.qk[:, q, :, :].rearrange("p t (h c) -> p (t h) c", h=HEADS)
            nc.vector.tensor_tensor(v, v, K.hr[:, q, :].unsqueeze(2).broadcast_to([P, TT * HEADS, QK]),
                                    ALU.mult).then_inc(K.head_scaled, 1)

        for i in range(4):
            split(j + 5 + i)
            for k in range(2 * i, 2 * i + 2):
                for n in HEAD_SQUARES[k]:
                    dve.wait_ge(K.head_sq, Num(n + 1, (l, 2 * TT)).value())
                    nc.vector.tensor_reduce(K.hs[:, n // TT, (n % TT) * HEADS:(n % TT + 1) * HEADS],
                                            K.hsq[:, n % 2, :].rearrange("p (h c) -> p h c", h=HEADS), AX_X,
                                            ALU.add).then_inc(K.head_red, 1)
                if i < 2:
                    dve.wait_ge(K.split_lo, (h + 10 + k + (k < 2)).value())
                    normed(K.t[:, k % 3, :], g + 20 + k, f + 20 + k)
                    if k:
                        u_lo(k - 1)
                    if k == TT - 1:
                        u_lo(k)
                else:
                    t = k - 4
                    dve.wait_ge(K.split_lo, (h + 16).value())
                    if Num(t - 2, (l, 12)).due():
                        dve.wait_ge(K.pool_ok, Num(t - 2, (l, 12)).value())
                    normed(K.t[:, t % 3, :], g + 20 + k, f + 20 + k)
                if k in HEAD_ROOT:
                    q = HEAD_ROOT[k]
                    dve.wait_ge(K.head_red, Num(TT * (q + 1), (l, 2 * TT)).value())
                    nc.vector.tensor_scalar(K.hs[:, q, :], K.hs[:, q, :], 1.0 / QK, EPS, ALU.mult, ALU.add).then_inc(K.head_v, 1)
                if k in HEAD_SCALE:
                    head_scale(HEAD_SCALE[k])
        gi, n, ab = 28, 16, 0
        for stage, grp in FOURIER:
            if (stage, grp) == ("seq", 0):
                split(j + 9)
            if stage == "dim":
                for half in range(2):
                    ab += 1
                    part = K.ab[:, grp % 2, :, 2 * half:2 * half + 2, :]
                    dve.wait_ge(K.ab_hi, Num(ab, (l, 8)).value())
                    nc.vector.tensor_tensor(part[:, 1], psum(g + gi)[:, :].rearrange("p (t c) -> p t c", t=2),
                                            part[:, 0].bitcast(F32), ALU.subtract).then_inc(K.tile_out, 1)
                    gi += 1
            else:
                dve.wait_ge(K.pool_ok, Num(4, (l, 12)).value())
                if grp == 3:
                    dve.wait_ge(K.split_lo, (h + 17).value())
                full(f + gi)
                nc.vector.tensor_tensor(K.t[:, grp % 3, :], psum(g + gi)[:, :], K.z[:, grp, :],
                                        ALU.mult).then_inc(K.tile_out, 1)
                lo(K.u[:, 1, grp, :], K.t[:, grp % 3, :], K.u[:, 0, grp, :], h + n)
                gi, n = gi + 1, n + 1
        attention(Heads(K, "L", l), lambda: split(j + 10))

        def za_lo(t):
            lo(K.v[:, 1, t, :], K.t[:, t % 3, :], K.v[:, 0, t, :], h + 20 + t)

        for i in range(2):
            split(j + 11 + i)
            for t in range(2 * i, 2 * i + 2):
                if t == 3:
                    za_lo(0)
                    dve.wait_ge(K.split_lo, (h + 21).value())
                normed(K.t[:, t % 3, :], g + 64 + t, f + 56 + t)
        for t in range(1, 4):
            za_lo(t)
        for i in range(4):
            merge(K.sig2, K.m2, j + 12 + 3 * i, g + 68 + 8 * i, f + 60 + 8 * i, h + 24 + 2 * i,
                  Num(KT + 2 * i, (l, KT)), sig_num(l, 8 + 4 * i), i)
        for i in range(4):
            split(j + 24 + i + 1)
            if i == 0:
                dve.wait_ge(K.next_ok, Num(1, (l, 1)).value())
            for k in range(2 * i, 2 * i + 2):
                residual(k, g + 100 + k, f + 92 + k)
                if k:
                    gx_lo(k - 1, K.norm_next, Num(3 * KT, (l, KT)))
        gx_lo(KT - 1, K.norm_next, Num(3 * KT, (l, KT)))
    g, f = Num(G_L + LAYERS * GL), Num(F_L + LAYERS * FL)
    for k in range(2 * TT):
        full(f + k)
        nc.vector.tensor_copy(K.xout[:, k // 2, (k % 2) * SEQ:(k % 2 + 1) * SEQ], psum(g + k)[:, :]).then_inc(K.tile_out, 1)


def program_pe(nc, pe, K):
    def product(bank, pairs, stop_sem):
        for i, (lhs, rhs) in enumerate(pairs):
            mm = nc.tensor.matmul(bank, lhs, rhs, start=(i == 0), stop=(i == len(pairs) - 1))
        if stop_sem is not None:
            mm.then_inc(stop_sem, 1)

    def bank(g):
        if (g - GB + 1).due():
            pe.wait_ge(K.tile_out, (g - GB + 1).value())
        return K.G[g % GB]

    def fm(g, w, x, kts=KT, ready=None):
        b = bank(g)
        for k in range(kts):
            if ready is not None:
                ready(k)
            for i, (p, q) in enumerate(PASSES):
                mm = nc.tensor.matmul(b[:, :], w(p, k), x(q, k), start=(k == i == 0),
                                      stop=(k == kts - 1 and i == len(PASSES) - 1))
        mm.then_inc(K.tile_full, 1)

    def slab_ready(j):
        pe.wait_ge(K.w_lo, (j + 1).value())

    def wcol(j, m, kt0=0):
        v = K.w[:, j % 2, :, :].rearrange("p h (k c) -> p h k c", k=KT)
        return lambda part, k: v[:, part, kt0 + k, m * P:(m + 1) * P]

    def gx(part, k):
        return K.gx[:, part, k, :]

    def norm_ready(gx0):
        def ready(k):
            pe.wait_ge(K.gx_lo, (gx0 + k + 1).value())
        return ready

    def split_ready(h):
        def ready(k):
            pe.wait_ge(K.split_lo, (h + k + 1).value())
        return ready

    def stat_sum(norm, s, sums=K.sumsq):
        pe.wait_ge(K.sum_ok, (norm * (KT - 1) + KT - 1).value())
        if (s - 1).due():
            pe.wait_ge(K.s_taken, (s - 1).value())
        for t in range(TT):
            mm = nc.tensor.matmul(K.S[s % 2][:, t:t + 1], sums[:, t * P:(t + 1) * P], K.ones[:, 0:1],
                                  start=True, stop=True)
        mm.then_inc(K.s_full, 1)

    def stat_spread(norm, s):
        pe.wait_ge(K.stat_diag, (norm + 1).value())
        if s.due():
            pe.wait_ge(K.s_taken, s.value())
        nc.tensor.matmul(K.S[(s + 1) % 2][:, :], K.ones[:, :], K.sq[:, 0, :], start=True, stop=True).then_inc(K.s_full, 1)

    def attention(A):
        U, S = A.u0, A.s0
        total = HEADS * TT

        def scores(n):
            t, e, i, b0, b1 = A.where(n)
            h = n // TT
            r = slice(e * HD, (e + 1) * HD)
            w = (b1 - b0) * P
            qs = slice(i * P, (i + 1) * P)
            if A.kind == "L" and n >= 2:
                pe.wait_ge(K.exp_ok, (U + n - 1).value())
            else:
                pe.wait_ge(K.s_taken, (S + n - 1).value())
            if A.kind == "A":
                pairs = [(K.qa[r, p, t, qs], K.ka[r, q, b0 * P:b1 * P]) for p, q in PASSES]
            elif A.kind == "B":
                pairs = [(K.qb[r, p, t, qs], K.kb[r, q, t, :]) for p, q in PASSES]
            else:
                if i == 0:
                    pe.wait_ge(K.tile_out, (A.g_qk(h) + 2).value())
                pairs = [(K.qkh[0:QK, h % 2, 0, p, qs], K.qkh[0:QK, h % 2, 1, q, :]) for p, q in PASSES]
            product(K.S[(S + n) % 2][:, 0:w], pairs, K.s_full)

        def transposes(n):
            _, _, _, b0, b1 = A.where(n)
            pe.wait_ge(K.probs_ok, (U + n + 1).value())
            if (U + n - 1).due():
                pe.wait_ge(K.pt_lo, (U + n - 1).value())
            for k in range(b1 - b0):
                c = A.first() + k * P
                mm = nc.tensor.transpose(K.T[(U + n) % 2][:, k * P:(k + 1) * P], K.t[:, n % 3, c:c + P], K.ident[:, :])
            mm.then_inc(K.trans_full, 1)

        def values(m):
            h = m // 2
            t, _, _, a0, a1 = A.where(2 * m)
            _, _, _, b0, b1 = A.where(2 * m + 1)
            b = bank(A.g_out(h)) if m % 2 == 0 else K.G[A.g_out(h) % GB]
            out = b[:, m % 2 * 2 * P:(m % 2 + 1) * 2 * P].rearrange("p (e c) -> p e c", e=2)
            pe.wait_ge(K.pt_lo, (U + 2 * m + 2).value())
            blocks = [(k, slice(0, 2)) for k in range(max(a0, b0), min(a1, b1))]
            blocks += [(k, slice(0, 1)) for k in range(a0, b0)] + [(k, slice(1, 2)) for k in range(a1, b1)]
            for i, (k, e) in enumerate(blocks):
                for p, q in PASSES:
                    v = {"A": lambda: K.va[:, p, k, :], "B": lambda: K.vb[:, p, k, t * P:(t + 1) * P],
                         "L": lambda: K.v[:, p, k, t * P:(t + 1) * P]}[A.kind]()
                    mm = nc.tensor.matmul(out[:, e, :], v, K.pt[A.kind][m % 2][:, q, k, e, :], start=(i == p == q == 0),
                                          stop=(i == len(blocks) - 1 and (p, q) == PASSES[-1]))
            mm.then_inc(K.pv_done, 1)

        def turn(h):
            for q in range(2):
                b = bank(A.g_qk(h) + q)
                for t in range(TT):
                    mm = nc.tensor.transpose(b[0:QK, t * P:(t + 1) * P], K.qk[:, q, t, h * QK:(h + 1) * QK], K.ident[:, :])
                mm.then_inc(K.tile_full, 1)

        if A.kind == "L":
            turn(0)
        scores(0)
        scores(1)
        if A.kind == "L":
            turn(1)
        scores(2)
        for n in range(total):
            if n + AHEAD < total:
                scores(n + AHEAD)
            transposes(n)
            if n >= 3 and n % 2 == 1:
                values(n // 2 - 1)
            if A.turned(n + 1) is not None:
                turn(A.turned(n + 1))
        values(total // 2 - 1)

    def merge(j, g, ya, yb, y_ready):
        for b in range(2):
            slab_ready(j + b)
            for m in range(2):
                fm(g + 2 * b + m, wcol(j + b, m), gx)
        slab_ready(j + 2)
        y_ready()
        for m in range(2):
            fm(g + 4 + 2 * m, wcol(j + 2, m), ya, HALF)
            fm(g + 5 + 2 * m, wcol(j + 2, m, HALF), yb, HALF)

    def eight(j, g, x, ready=None, norm=None):
        for i in range(4):
            slab_ready(j + i)
            for m in range(2):
                fm(g + 2 * i + m, wcol(j + i, m), x, ready=ready if i == m == 0 else None)
                if norm is not None and i == 0:
                    (stat_spread if m else stat_sum)(*norm)

    pe.wait_ge(K.gain_in, 16 * GAIN_DMAS)
    pe.wait_ge(K.ones_ok, 1)
    pe.wait_ge(K.x_in, 16 * TT)
    for k in range(KT):
        b = bank(Num(G_X + k))
        for t in range(TT):
            mm = nc.tensor.transpose(b[:, t * P:(t + 1) * P], K.xin[:, t, k * P:(k + 1) * P], K.ident[:, :])
        mm.then_inc(K.tile_full, 1)
    for k, (j, m, form, to) in enumerate(IN_TILES):
        g = Num(G_IN + k)
        slab_ready(Num(j))
        if form != "tm":
            fm(g, wcol(Num(j), m), gx, ready=norm_ready(Num(0)) if k == 0 else None)
        else:
            b = bank(g)
            w = K.w[:, j % 2, :, :].rearrange("p h (k c) -> p h k c", k=KT)
            whole = to[0] == "va"
            cols, n = (slice(P, 2 * P), P) if whole else (slice(0, SCOL), SCOL)
            tts = range(TT) if whole else range(2 * (to[1] % 2), 2 * (to[1] % 2) + 2)
            for i, t in enumerate(tts):
                pairs = [(K.gx[:, p, kt, t * P:(t + 1) * P], w[:, q, kt, cols]) for kt in range(KT) for p, q in PASSES]
                product(b[:, i * n:(i + 1) * n], pairs, K.tile_full if i == len(tts) - 1 else None)
        if k == 0:
            stat_sum(Num(0), Num(0))
        if k == 1:
            stat_spread(Num(0), Num(0))
    pe.wait_ge(K.split_lo, Num(H_MERGE).value())
    attention(Heads(K, "A"))
    attention(Heads(K, "B"))

    def heads_ready():
        pe.wait_ge(K.tile_out, G_B + HEADS)

    for i in range(4):
        merge(Num(J_MERGE + 3 * i), Num(G_MERGE + 8 * i), lambda p, k: K.qa[:, p, k, :], lambda p, k: K.qb[:, p, k, :],
              heads_ready)

    def big(part, k):
        return K.big[:, part, k, :]

    eight(Num(J_OUT), Num(G_OUT), big, split_ready(Num(H_MERGE)))

    def chunk(c, **first):
        eight(Num(J_MLP, (c, 8)), Num(G_MLP, (c, 16)), gx, **first)
        eight(Num(J_MLP + 4, (c, 8)), Num(G_MLP + 8, (c, 16)), big, split_ready(Num(H_MLP, (c, 8))))

    chunk(0, ready=norm_ready(Num(KT)), norm=(Num(1), Num(S_N2)))
    with pe.Fori(1, CHUNKS) as c:
        chunk(c)
    stat_sum(Num(3), Num(S_NF), K.sumsq_f)
    stat_spread(Num(2), Num(S_NF))
    with pe.Fori(0, LAYERS) as l:
        j, g, f, h, s = (Num(n, (l, per)) for n, per in ((J_L, JL), (G_L, GL), (F_L, FL), (H_L, HL), (S_L, SL)))
        norm = Num(3, (l, 1))
        for k in range(4):
            slab_ready(j + k // 2)
            fm(g + k, wcol(j + k // 2, k % 2), gx,
               ready=norm_ready(Num(2 * KT, (l, KT))) if k == 0 else None)
            if k == 0:
                stat_sum(norm, s)
            if k == 1:
                stat_spread(norm, s)
        pe.wait_ge(K.small_lo, Num(1, (l, 1)).value())
        pe.wait_ge(K.s_taken, (s + 1).value())
        wk = K.sw[:, :, SCOL:2 * SCOL].rearrange("p h (k c) -> p h k c", k=KT)
        for t in range(TT):
            pairs = [(K.gx[:, p, kt, t * P:(t + 1) * P], wk[:, q, kt, :]) for kt in range(KT) for p, q in PASSES]
            product(K.S[(s + 2) % 2][:, t * ROPE:(t + 1) * ROPE], pairs, K.s_full if t == TT - 1 else None)
        squares = [K.sq[:, 0, :], K.sq[:, 1, :], K.hsq[:, 0, 0:SEQ], K.hsq[:, 1, 0:SEQ]]
        pe.wait_ge(K.lat_sq, Num(4, (l, 4)).value())
        pe.wait_ge(K.s_taken, (s + 2).value())
        for i in range(2):
            for t in range(TT):
                for m in range(2):
                    mm = nc.tensor.matmul(K.S[(s + 3) % 2][:, i * TT + t:i * TT + t + 1],
                                          squares[2 * i + m][:, t * P:(t + 1) * P], K.ones[:, 0:1],
                                          start=(m == 0), stop=(m == 1))
        mm.then_inc(K.s_full, 1)
        pe.wait_ge(K.split_lo, (h + 4).value())
        for i, n in enumerate((HEADS * QK // 2, SEQ)):
            slab_ready(j + 2 + i)
            w = K.w[:, (j + 2 + i) % 2, :, 0:4 * n].rearrange("p h (k c) -> p h k c", k=2)
            for t in range(TT):
                for half in range(2):
                    b = bank(g + 4 + 8 * i + 2 * t + half)
                    pairs = [(K.u[:, p, 2 * i + k, t * P:(t + 1) * P], w[:, q, k, half * n:(half + 1) * n])
                             for k in range(2) for p, q in PASSES]
                    product(b[:, 0:n], pairs, K.tile_full)
        for k in range(8):
            slab_ready(j + 4 + k // 2)
            fm(g + 20 + k, wcol(j + 4 + k // 2, k % 2), gx)
        gi = 28
        for stage, grp in FOURIER:
            if stage == "dim":
                pe.wait_ge(K.split_lo, (h + 12 + grp + 1).value())
                for half in range(2):
                    b = bank(g + gi)
                    for i, t in enumerate((2 * half, 2 * half + 1)):
                        pairs = [(K.u[:, p, grp, t * P:(t + 1) * P], K.sw[:, q, 0:SCOL]) for p, q in PASSES]
                        product(b[:, i * SCOL:(i + 1) * SCOL], pairs, K.tile_full if i else None)
                    gi += 1
            else:
                b = bank(g + gi)
                pe.wait_ge(K.tile_out, (g + fourier_tile(grp)).value())
                slab_ready(j + 9)
                pairs = []
                for part in range(2):
                    w = K.w[:, (j + 8 + part) % 2, :, :].rearrange("p h (k c) -> p h k c", k=TT)
                    pairs += [(K.ab[:, grp % 2, p, t, part * P:(part + 1) * P], w[:, q, t, :])
                              for t in range(TT) for p, q in PASSES]
                product(b[:, :], pairs, K.tile_full)
                gi += 1
        pe.wait_ge(K.rope_ok, Num(24, (l, 24)).value())
        attention(Heads(K, "L", l))
        for k in range(4):
            slab_ready(j + 10 + k // 2)
            fm(g + 64 + k, wcol(j + 10 + k // 2, k % 2), gx)

        def branches_ready():
            pe.wait_ge(K.split_lo, (h + 24).value())

        for i in range(4):
            merge(j + 12 + 3 * i, g + 68 + 8 * i, lambda p, k: K.v[:, p, k, :], lambda p, k: K.u[:, p, k, :],
                  branches_ready)
        eight(j + 24, g + 100, lambda p, k: K.m2[:, p, k, :], split_ready(h + 24))
    g = Num(G_L + LAYERS * GL)
    for k in range(2 * TT):
        b = bank(g + k)
        pe.wait_ge(K.tile_out, (g if k % 2 else g - KT // 2).value())
        for i in range(KT // 2):
            kt = (k % 2) * (KT // 2) + i
            mm = nc.tensor.transpose(b[:, i * P:(i + 1) * P], K.x[:, kt, (k // 2) * P:(k // 2 + 1) * P], K.ident[:, :])
        mm.then_inc(K.tile_full, 1)


def fourier_tile(grp):
    n = 28
    for stage, of in FOURIER:
        n += 2 if stage == "dim" else 1
        if (stage, of) == ("dim", grp):
            return n


_INS = ["x", "norm_mix", "w_in", "b_gate", "sink", "rpb", "w_proj_a", "w_proj_b", "w_out", "norm_mlp", "w_up", "w_down",
        "norm_final", "norm_g_2", "w_in_2", "q_latent_g_2", "kv_latent_g_2", "w_uq_2", "w_ukv_2", "q_head_g_2",
        "k_head_g_2", "w_attn_proj_2", "w_fourier_proj_2", "b_merge_2", "w_out_2"]


def constants():
    f = np.float32
    c = {"ident": np.eye(P, dtype=f)}
    dist = np.abs(np.arange(P)[:, None] - (np.arange(3 * P) - P)[None, :])
    slopes = np.exp2(-8.0 * np.arange(1, HEADS + 1, dtype=f) / HEADS).astype(f)
    c["alibi"] = np.where(dist <= P, -slopes[:, None, None] * dist.astype(f), f(MASKED)).astype(f)
    col = np.arange(GRID_W)
    start = np.clip(col - KW // 2, 0, GRID_W - KW)
    near = ((col[None, :] >= start[:, None]) & (col[None, :] < start[:, None] + KW))[::-1]
    c["mask"] = np.tile(np.where(near, f(0), f(MASKED)), (2, 1)).astype(f)
    s = np.outer(np.arange(SEQ), np.arange(SEQ)) % SEQ * (2 * np.pi / SEQ)
    c["dft_seq"] = np.stack([np.cos(s), -np.sin(s)]).astype(f)
    d = np.outer(np.arange(P), np.arange(P)) % P * (2 * np.pi / P)
    c["dft_dim"] = (np.concatenate([np.cos(d), np.sin(d)], 1) / np.sqrt(SEQ * P)).astype(f)
    half = ROPE // 2
    inv = (f(10000.0) ** (-np.arange(half, dtype=f) / f(half))).astype(f)
    ang = np.arange(SEQ, dtype=f)[:, None] * inv[None, :]
    c["rope"] = np.concatenate([np.cos(ang), np.sin(ang)], 1).astype(f)
    return c


def kernel(**inputs):
    import concourse.bacc as _bacc
    from concourse.bass_utils import run_bass_kernel_spmd as _run

    nc = _bacc.Bacc("TRN2", target_bir_lowering=False, num_devices=1)
    arrays, a = {}, {}
    given = {n: np.ascontiguousarray(inputs[n]) for n in _INS}
    for name, v in {**given, **constants()}.items():
        arrays[f"in_{name}"] = v
        a[name] = nc.dram_tensor(f"in_{name}", v.shape, mybir.dt.from_np(v.dtype), kind="ExternalInput").ap()
    out = nc.dram_tensor("out", (1, SEQ, D), F32, kind="ExternalOutput").ap()
    build(nc, a, out)
    r = _run(nc, [arrays], core_ids=[0])
    return r.results[0]["out"]
```

```python
from contextlib import ExitStack

import numpy as np
import concourse.bass as bass
from concourse import mybir

F32 = mybir.dt.float32
F32R = mybir.dt.float32r
ALU = mybir.AluOpType
ACT = mybir.ActivationFunctionType
AX_X = mybir.AxisListType.X

P = 128
SEQ = 512
D = 1024
KT = D // P
TT = SEQ // P
HEADS = 8
HD = 64
HALF = HEADS // 2
D_FF = 4 * D
CHUNKS = D_FF // D
LAYERS = 2
QK = 96
NOPE = 64
ROPE = 32
LAT = 256
GRID_W = 64
KH, KW = 8, 16
EPS = 1e-6
MASKED = -1e30

SLAB = 2048
SCOL = 256
GB = 4
QA0, KVA0, QB0, KB0, VB0, GA0, GB0 = 0, 512, 768, 1280, 1792, 2304, 3328
CQ0, CKV0, KPE0, ZA0, UF0, ZF0, MA0, MF0 = 0, 256, 512, 544, 1056, 1568, 2080, 3104
W2 = 4128

TAB_PAD = 64
TAB_H = (2 * KH - 1) * GRID_W
TAB = 8192
BIAS_ROWS = 2 * KH - 2

J_IN, J_MERGE, J_OUT, J_MLP = 0, 9, 21, 25
J_L, JL = 57, 28
J_END = J_L + LAYERS * JL
G_X, G_IN, G_A, G_B, G_MERGE, G_OUT, G_MLP = 0, 8, 26, 34, 42, 74, 82
G_L, GL = 146, 108
F_X, F_IN, F_MERGE, F_OUT, F_MLP = 0, 8, 26, 58, 66
F_L, FL = 130, 100
H_IN, H_MERGE, H_MLP, H_L, HL = 0, 18, 26, 58, 32
S_A, S_B, S_N2, S_NF, S_L, SL = 2, 34, 66, 68, 69, 36
U_A, U_B, U_L, UL = 0, 32, 64, 32
AHEAD = 3
LP_MERGE, LP_LAT, LP_HEAD = 0, 2 * KT, 2 * KT + 4
LP_N = LP_HEAD + 2 * QK
PASSES = ((0, 0), (0, 1), (1, 0))
FOURIER = (("dim", 0), ("dim", 1), ("seq", 0), ("dim", 2), ("seq", 1), ("dim", 3), ("seq", 2), ("turn", 0), ("seq", 3))
HEAD_SQUARES = ((0, 1), (2, 3), (4, 5), (6, 7), (), (), (), ())
HEAD_ROOT = 4
KEY_SCALE = {5: 0, 6: 1}
PAR_DMAS = 7 + LAYERS * 7


class Num:

    def __init__(self, k, *terms):
        self.k, self.terms = k, tuple(t for t in terms if not isinstance(t[0], int))
        self.k += sum(t[0] * t[1] for t in terms if isinstance(t[0], int))

    def __add__(self, n):
        return Num(self.k + n, *self.terms)

    def __sub__(self, n):
        return self + (-n)

    def __mod__(self, m):
        assert all(per % m == 0 for _, per in self.terms)
        return self.k % m

    def __floordiv__(self, m):
        assert all(per % m == 0 for _, per in self.terms)
        return Num(self.k // m, *((r, per // m) for r, per in self.terms))

    def __mul__(self, m):
        return Num(self.k * m, *((r, per * m) for r, per in self.terms))

    def due(self):
        return self.k > 0

    def value(self):
        v = self.k
        for r, per in self.terms:
            v = r * per + v
        return v


class Core:
    pass


def build(nc, a, out):
    with ExitStack() as ctx:
        K = Core()
        K.a, K.out = a, out
        allocate(nc, ctx, K)
        block = ctx.enter_context(nc.Block())

        @block.sync
        def _(sp):
            program_sync(nc, sp, K)

        @block.gpsimd
        def _(pool):
            program_pool(nc, pool, K)

        @block.scalar
        def _(act):
            program_act(nc, act, K)

        @block.vector
        def _(dve):
            program_vector(nc, dve, K)

        @block.tensor
        def _(pe):
            program_pe(nc, pe, K)


def allocate(nc, ctx, K):
    def sb(name, shape, dt):
        return ctx.enter_context(nc.sbuf_tensor(name, shape, dt))

    def semaphore(name):
        return ctx.enter_context(nc.semaphore(name))

    raw0 = (nc.sbuf_base + 31) // 32 * 32
    K.raw = sb("raw", [P, 2, SLAB], F32)
    K.w = sb("w", [P, 2, 2, SLAB], F32R)
    K.x = sb("x", [P, KT, SEQ], F32)
    K.gx = sb("gx", [P, 2, KT, SEQ], F32R)
    K.rstd = sb("rstd", [P, SEQ], F32)
    K.sumsq = sb("sumsq", [P, SEQ], F32)
    K.sq = sb("sq", [P, 2, SEQ], F32)
    K.t = sb("t", [P, 3, SEQ], F32)
    K.ident = sb("ident", [P, P], F32)
    K.ones = sb("ones", [P, P], F32)
    K.r4 = sb("r4", [P, TT], F32)
    K.v4 = sb("v4", [P, TT], F32)
    K.d4 = sb("d4", [P, TT], F32)
    K.lat_v = sb("lat_v", [P, 2 * TT], F32)
    K.lat_d = sb("lat_d", [P, 2 * TT], F32)
    K.lat_r = sb("lat_r", [P, 2 * TT], F32)
    K.hs = sb("hs", [P, 2, TT * HEADS], F32)
    K.hd_ = sb("hd_", [P, 2, TT * HEADS], F32)
    K.hr = sb("hr", [P, 2, TT * HEADS], F32)
    K.nm = sb("nm", [P, 4], F32)
    K.den = sb("den", [P, 4], F32)
    K.rden = sb("rden", [P, 4], F32)
    K.zeros = sb("zeros", [P, 1], F32)
    K.spare = sb("spare", [P, 1], F32)
    K.unused = sb("unused", [P, 1], F32)
    K.gains = sb("gains", [P, 4, KT], F32)
    K.norm_all = sb("norm_all", [P, LAYERS + 1, KT], F32)
    K.norm_next = sb("norm_next", [P, KT], F32)
    K.prior = sb("prior", [P, TT], F32)
    K.prior2 = sb("prior2", [P, TT], F32)
    K.bg = sb("bg", [P, 2 * KT], F32)
    K.sink = sb("sink", [P, HEADS], F32)
    K.lp_all = sb("lp_all", [P, LAYERS, LP_N], F32)
    K.lp = sb("lp", [P, LP_N], F32)
    K.rope = sb("rope", [P, TT, ROPE], F32)
    p0 = nc.sbuf_base
    sb("pt_area", [P, 8 * 256], F32)
    a0 = nc.sbuf_base
    sb("arena", [P, 84 * 256], F32)

    def at(name, kb, shape, dt, start=None):
        off = (a0 if start is None else start) + kb * 1024
        return nc.alloc_sbuf_tensor_at(name, shape, dt, offset=off)

    pt0 = at("pt0", 0, [P, 2, TT, 2, P], F32R, p0)
    K.pt = {"L": [pt0, at("pt1_l", 0, [P, 2, TT, 2, P], F32R, raw0)]}
    K.pt["A"] = K.pt["B"] = [pt0, at("pt1", 0, [P, 2, TT, 2, P], F32R, raw0 + SLAB * 4)]
    K.hsq = at("hsq", 0, [P, 2, HEADS * QK], F32, p0)
    K.sraw = at("sraw", 0, [P, SCOL + SEQ], F32, p0)
    K.zero = at("zero", 6, [P, TAB // P], F32, p0)
    K.rt = at("rt", 6, [P, 2, 2 * P], F32, p0)
    K.qa = at("qa", 0, [P, 2, HALF, SEQ], F32R)
    K.ka = at("ka", 16, [P, 2, SEQ], F32R)
    K.va = at("va", 20, [P, 2, TT, P], F32R)
    K.qb = at("qb", 24, [P, 2, HALF, SEQ], F32R)
    K.kvb = at("kvb", 40, [P, 2 * 2 * HALF * SEQ], F32R)
    n = 2 * HALF * SEQ
    K.kb = K.kvb[:, 0:n].rearrange("p (h t s) -> p h t s", h=2, t=HALF)
    K.vb = K.kvb[:, n:2 * n].rearrange("p (h t s) -> p h t s", h=2, t=TT)
    K.big = K.kvb[:, :].rearrange("p (h t s) -> p h t s", h=2, t=KT)
    K.mask = at("mask", 72, [P, GRID_W], F32)
    K.biasa = at("biasa", 74, [P, 2, 3 * P], F32)
    K.biasb = at("biasb", 77, [P, 2, BIAS_ROWS * GRID_W], F32)
    K.sig1 = at("sig1", 74, [P, 4, SEQ], F32)
    K.sumsq_f = at("sumsq_f", 0, [P, SEQ], F32)
    K.sq_f = at("sq_f", 2, [P, 2, SEQ], F32)
    K.xin = at("xin", 24, [P, TT, D], F32)
    K.xout = at("xout", 0, [P, TT, D], F32)
    K.v = at("v", 0, [P, 2, TT, SEQ], F32R)
    K.qk = at("qk", 16, [P, 2, TT, HEADS * QK], F32)
    K.ab = at("ab", 40, [P, 2, 2, TT, SCOL], F32R)
    K.rstd_f = at("rstd_f", 40, [P, SEQ], F32)
    K.qkh = K.ab[:, :, :, :, :].rearrange("p r h t s -> p (r h t s)").rearrange(
        "p (r q h s) -> p r q h s", r=2, q=2, h=2)
    K.u = at("u", 56, [P, 2, 4, SEQ], F32R)
    K.kpe = at("kpe", 78, [P, SEQ], F32)
    K.z = at("z", 72, [P, 4, SEQ], F32)
    K.sw = at("sw", 80, [P, 2, SCOL], F32R)
    K.alt = at("alt", 82, [P, SEQ], F32R)
    K.sig2 = at("sig2", 16, [P, 4, SEQ], F32)
    K.m2 = at("m2", 24, [P, 2, KT, SEQ], F32R)

    K.G = [ctx.enter_context(nc.psum_tensor(f"G{i}", [P, 512], F32)) for i in range(GB)]
    K.S = [ctx.enter_context(nc.psum_tensor(f"S{i}", [P, 512], F32)) for i in range(2)]
    K.T = [ctx.enter_context(nc.psum_tensor(f"T{i}", [P, 512], F32)) for i in range(2)]
    K.tab = nc.dram_tensor("bias_table", (TAB,), F32).ap()

    K.x_in = [semaphore(f"x_in{i}") for i in range(2)]
    K.ident_in = semaphore("ident_in")
    K.gain_in = semaphore("gain_in")
    K.par_in = semaphore("par_in")
    K.ones_ok = semaphore("ones_ok")
    K.zero_ok = semaphore("zero_ok")
    K.tab_zeroed = semaphore("tab_zeroed")
    K.tab_in = semaphore("tab_in")
    K.biasb_ok = semaphore("biasb_ok")
    K.w_hi = semaphore("w_hi")
    K.w_lo = semaphore("w_lo")
    K.group_in = semaphore("group_in")
    K.group_hi = semaphore("group_hi")
    K.group_lo = semaphore("group_lo")
    K.fold_ok = semaphore("fold_ok")
    K.va_full = semaphore("va_full")
    K.pt_zero = semaphore("pt_zero")
    K.tile_full = semaphore("tile_full")
    K.tile_out = semaphore("tile_out")
    K.split_hi = semaphore("split_hi")
    K.split_lo = semaphore("split_lo")
    K.s_full = semaphore("s_full")
    K.s_taken = semaphore("s_taken")
    K.sq_ok = semaphore("sq_ok")
    K.sum_ok = semaphore("sum_ok")
    K.gx_hi = semaphore("gx_hi")
    K.gx_lo = semaphore("gx_lo")
    K.stat_sqrt = semaphore("stat_sqrt")
    K.prior_ok = semaphore("prior_ok")
    K.prior_diag = semaphore("prior_diag")
    K.prior_full = semaphore("prior_full")
    K.prior_taken = semaphore("prior_taken")
    K.gain_ok = semaphore("gain_ok")
    K.next_ok = semaphore("next_ok")
    K.stat_rec = semaphore("stat_rec")
    K.stat_diag = semaphore("stat_diag")
    K.x_fin = semaphore("x_fin")
    K.exp_ok = semaphore("exp_ok")
    K.rden_ok = semaphore("rden_ok")
    K.sink_ok = semaphore("sink_ok")
    K.probs_ok = semaphore("probs_ok")
    K.trans_full = semaphore("trans_full")
    K.pt_hi = semaphore("pt_hi")
    K.pt_lo = semaphore("pt_lo")
    K.pv_done = semaphore("pv_done")
    K.qk_hi = semaphore("qk_hi")
    K.sig_ok = semaphore("sig_ok")
    K.mix_ok = semaphore("mix_ok")
    K.up_sq = semaphore("up_sq")
    K.lp_ok = semaphore("lp_ok")
    K.lat_sq = semaphore("lat_sq")
    K.lat_sum = semaphore("lat_sum")
    K.lat_sqrt = semaphore("lat_sqrt")
    K.lat_rec = semaphore("lat_rec")
    K.k_out = semaphore("k_out")
    K.kpe_ok = semaphore("kpe_ok")
    K.kpe_full = semaphore("kpe_full")
    K.head_sq = semaphore("head_sq")
    K.head_red = semaphore("head_red")
    K.head_v = semaphore("head_v")
    K.head_sqrt = semaphore("head_sqrt")
    K.head_rec = semaphore("head_rec")
    K.head_scaled = semaphore("head_scaled")
    K.rope_ok = semaphore("rope_ok")
    K.qk_ready = semaphore("qk_ready")
    K.pool_ok = semaphore("pool_ok")
    K.out_done = semaphore("out_done")
    K.y_hi = semaphore("y_hi")
    K.ab_hi = semaphore("ab_hi")
    K.w_in_sem = [semaphore(f"slab_in{i}") for i in range(2)]
    K.biasa_in = [semaphore(f"biasa_in{i}") for i in range(2)]
    K.biasb_in = [semaphore(f"biasb_in{i}") for i in range(2)]


def in_tiles():
    tiles = [(1, t, "q", ("qa", t)) for t in range(HALF)]
    tiles += [(2, 1, "turn", ("va", 0)), (2, 0, "k", ("ka", 0))]
    tiles += [(3 + t // 2, t % 2, "q", ("qb", t)) for t in range(HALF)]
    tiles += [(5 + t // 2, t % 2, "k", ("kb", t)) for t in range(HALF)]
    tiles += [(7 + t // 2, t % 2, "tm", ("vb", t)) for t in range(HALF)]
    return tiles


IN_TILES = in_tiles()
IN_ENDS = [F_IN + 1] + [F_IN + 1 + max(i for i, t in enumerate(IN_TILES) if t[0] == j) for j in range(1, 9)]


def in_dest(K, to, part):
    name, t = to
    if name == "qa":
        return K.qa[:, part, t, :]
    if name == "qb":
        return K.qb[:, part, t, :].rearrange("p (i c) -> p i c", c=P)[:, :, ::-1]
    if name == "kb":
        return K.kb[:, part, t, :]
    if name == "ka":
        return K.ka[:, part, :]
    if name == "va":
        return K.va[:, part, :, :]
    return K.vb[:, part, 2 * (t % 2):2 * (t % 2) + 2, (t // 2) * SCOL:(t // 2 + 1) * SCOL]


def in_shape(to, ap):
    if to[0] in ("va", "qb"):
        return ap.rearrange("p (t c) -> p t c", t=TT)
    if to[0] == "vb":
        return ap.rearrange("p (t c) -> p t c", t=2)
    return ap


class Heads:

    def __init__(self, K, kind, layer=0):
        self.kind = kind
        self.u0 = {"A": Num(U_A), "B": Num(U_B), "L": Num(U_L, (layer, UL))}[kind]
        self.s0 = {"A": Num(S_A), "B": Num(S_B), "L": Num(S_L + 4, (layer, SL))}[kind]
        self.g0 = {"A": Num(G_A), "B": Num(G_B), "L": Num(G_L + 40, (layer, GL))}[kind]
        self.scaled = Num(3, (layer, 3))
        self.qk0 = Num(0, (layer, 2 * HEADS))
        self.f0 = Num(F_L + 40, (layer, FL)) if kind == "L" else None
        self.K = K

    def where(self, n):
        h, i = divmod(n, TT)
        lo, hi = (max(0, i - 1), min(TT, i + 2)) if self.kind == "A" else (0, TT)
        return h // 2, h % 2, i, lo, hi

    def g_out(self, h):
        return self.g0 + (h if self.kind != "L" else (6 + 3 * h if h < HEADS - 2 else 2 * HEADS + h))

    def g_qk(self, h):
        return self.g0 + (3 * h - 1 if h < 2 else 4 + 3 * (h - 2))

    def f_qk(self, h, q):
        return self.f0 + (2 * h if h else -1) + q + 1

    def split(self, h, q):
        return self.qk0 + 2 * h + q + 1

    def pairs(self, m):
        return self.u0 // 2 + m + 1

    def last_of(self, n):
        return (n - 6) // TT if n >= 6 and n % TT == 2 else None

    def turned(self, n):
        h = n // TT + 1
        return h if self.kind == "L" and n % TT == 0 and 2 <= h < HEADS else None

    def rows(self, ap):
        return ap.rearrange("p (i c) -> p i c", c=P)

    def in_order(self, ap):
        return self.rows(ap)[:, :, ::-1] if self.kind == "B" else self.rows(ap)

    def first(self):
        return 1 if self.kind == "A" else 0


def by_feature(v):
    return v.rearrange("(k p) -> p k", p=P)


def qa_raw_order(w, e):
    return w.rearrange("p (k e t c) -> p e k t c", k=HALF, e=2, t=HALF)[:, e]


def qa_order(w, e):
    return w.rearrange("p (k t e c) -> p e k t c", k=HALF, e=2, t=HALF)[:, e]


def program_sync(nc, sp, K):
    a = K.a

    def slab(j, pieces, pairs=None):
        if (j - 1).due():
            sp.wait_ge(K.w_lo, (j - 1).value())
        if pairs is not None:
            sp.wait_ge(K.pv_done, pairs.value())
        sp.wait_ge(K.x_in[0], 16)
        inc = 64 // len(pieces(K.raw[:, j % 2, :]))
        for dst, src, *n in pieces(K.raw[:, j % 2, :]):
            sp.dma_start(dst, src).then_inc(K.w_in_sem[j % 2], n[0] if n else inc)

    def columns(w, c0):
        src = w.rearrange("(k p) n -> p k n", p=P)[:, :, c0] if not isinstance(c0, int) else \
            w.rearrange("(k p) n -> p k n", p=P)[:, :, c0:c0 + SCOL]

        def pieces(raw):
            dst = raw.rearrange("p (k n) -> p k n", k=KT)
            return [(dst[:, 0:4, :], src[:, 0:4, :]), (dst[:, 4:8, :], src[:, 4:8, :])]
        return pieces

    def k_pe(w):
        src = w.rearrange("(k p) n -> p k n", p=P)[:, :, KPE0:KPE0 + P]

        def pieces(raw):
            dst = raw[:, 0:KT * P].rearrange("p (k n) -> p k n", k=KT)
            return [(dst[:, 0:4, :], src[:, 0:4, :]), (dst[:, 4:8, :], src[:, 4:8, :])]
        return pieces

    def qa_rows(i):
        src = a["w_in"][0].rearrange("(k p) n -> p k n", p=P)[:, i * HALF:(i + 1) * HALF, QA0:KVA0]

        def pieces(raw):
            dst = raw.rearrange("p (k n) -> p k n", k=HALF)
            return [(dst[:, 0:2, :], src[:, 0:2, :]), (dst[:, 2:4, :], src[:, 2:4, :])]
        return pieces

    def pair(wa, wb, c0, permuted):
        def cols(w):
            return w[:, c0] if not isinstance(c0, int) else w[:, c0:c0 + SCOL]

        def pieces(raw):
            dst = raw.rearrange("p (k n) -> p k n", k=KT)
            second = (dst[:, HALF:KT, :], cols(wb).rearrange("(k p) n -> p k n", p=P), 32)
            if not permuted:
                return [(dst[:, 0:HALF, :], cols(wa).rearrange("(k p) n -> p k n", p=P), 32), second]
            rows = cols(wa).rearrange("(e k p) n -> e p k n", e=2, p=HD)
            return [(dst[e * HD:(e + 1) * HD, 0:HALF, :], rows[e], 16) for e in range(2)] + [second]
        return pieces

    xs = a["x"][0].rearrange("(t p) d -> p t d", p=P)
    for i in range(2):
        c = slice(i * D // 2, (i + 1) * D // 2)
        sp.dma_start(K.xin[:, :, c], xs[:, :, c]).then_inc(K.x_in[i], 16)

    def in_slab(j):
        if j < 2:
            slab(Num(j), qa_rows(j))
        else:
            c0 = [KVA0, QB0, QB0 + SCOL, KB0, KB0 + SCOL, VB0, VB0 + SCOL][j - 2]
            slab(Num(j), columns(a["w_in"][0], c0))

    for j in range(3):
        in_slab(j)
    for i, gain in ((1, a["norm_mlp"][0]), (2, a["norm_final"])):
        sp.dma_start(K.gains[:, i, :], by_feature(gain), allow_slow_non_contiguous=True).then_inc(K.par_in, 16)
    sp.dma_start(K.mask[:, :], a["mask"]).then_inc(K.par_in, 16)
    sp.dma_start(K.bg[:, :], by_feature(a["b_gate"][0]), allow_slow_non_contiguous=True).then_inc(K.par_in, 16)
    sp.dma_start(K.sink[:, :], a["sink"][0].partition_broadcast(P)).then_inc(K.par_in, 16)
    sp.dma_start(K.rope[:, :, :], a["rope"].rearrange("(t p) c -> p t c", p=P)).then_inc(K.par_in, 16)
    for l in range(LAYERS + 1):
        sp.dma_start(K.norm_all[:, l, :], by_feature(a["norm_g_2"][min(l, LAYERS - 1)]),
                     allow_slow_non_contiguous=True).then_inc(K.par_in, 16)
    for l in range(LAYERS):
        for c, n, src in ((LP_MERGE, KT, by_feature(a["b_merge_2"][l, 0])),
                          (LP_MERGE + KT, KT, by_feature(a["b_merge_2"][l, 1])),
                          (LP_LAT, 2, by_feature(a["q_latent_g_2"][l])),
                          (LP_LAT + 2, 2, by_feature(a["kv_latent_g_2"][l]))):
            sp.dma_start(K.lp_all[:, l, c:c + n], src, allow_slow_non_contiguous=True).then_inc(K.par_in, 16)
        for c, g in ((LP_HEAD, a["q_head_g_2"]), (LP_HEAD + QK, a["k_head_g_2"])):
            sp.dma_start(K.lp_all[:, l, c:c + QK], g[l].partition_broadcast(P)).then_inc(K.par_in, 16)
    sp.wait_ge(K.zero_ok, 1)
    sp.dma_start(K.tab.rearrange("(p n) -> p n", p=P), K.zero[:, :]).then_inc(K.tab_zeroed, 16)
    sp.wait_ge(K.tab_zeroed, 16)
    rows = K.tab[TAB_PAD:TAB_PAD + HEADS * TAB_H].rearrange("(r c) -> r c", c=GRID_W)
    sp.dma_start(rows[:, 0:2 * KW - 1], a["rpb"][0].rearrange("h r c -> (h r) c")).then_inc(K.tab_in, 16)
    for j in range(3, 9):
        in_slab(j)
    slab(Num(J_MERGE), columns(a["w_in"][0], GA0))
    slab(Num(J_MERGE + 1), columns(a["w_in"][0], GB0))

    for h in range(HEADS):
        if h >= 2:
            sp.wait_ge(K.s_taken, S_A + TT * (h - 1))
        head = (h % 2) * HALF + h // 2
        sp.dma_start(K.biasa[:, h % 2, :], a["alibi"][head]).then_inc(K.biasa_in[h % 2], 16)
    sp.wait_ge(K.tab_in, 16)
    for h in range(HEADS):
        if h >= 2:
            sp.wait_ge(K.s_taken, S_B + TT * (h - 1))
        start = TAB_PAD + h * TAB_H + GRID_W + KW - 1 - (P - 1)
        src = bass.AP(K.tab.tensor, start, [[1, P], [1, BIAS_ROWS * GRID_W]])
        sp.dma_start(K.biasb[:, h % 2, :], src).then_inc(K.biasb_in[h % 2], 16)
    sp.wait_ge(K.pv_done, HEADS * TT)
    for i in range(4):
        if i:
            slab(Num(J_MERGE + 3 * i), columns(a["w_in"][0], GA0 + i * SCOL))
            slab(Num(J_MERGE + 3 * i + 1), columns(a["w_in"][0], GB0 + i * SCOL))
        slab(Num(J_MERGE + 3 * i + 2), pair(a["w_proj_a"][0], a["w_proj_b"][0], i * SCOL, True))
    for i in range(4):
        slab(Num(J_OUT + i), columns(a["w_out"][0], i * SCOL))
    sp.wait_ge(K.split_lo, H_MERGE + KT)
    sp.dma_start(K.sraw[:, 0:SCOL], a["dft_dim"]).then_inc(K.group_in, 16)
    sp.dma_start(K.sraw[:, SCOL:SCOL + SEQ], a["dft_alt"]).then_inc(K.group_in, 16)
    with sp.Fori(0, CHUNKS) as c:
        for i in range(4):
            slab(Num(J_MLP + i, (c, 8)), columns(a["w_up"][0], bass.ds(c * D + i * SCOL, SCOL)))
        for i in range(4):
            down = a["w_down"][0][bass.ds(c * D, D), :]
            slab(Num(J_MLP + 4 + i, (c, 8)), columns(down, i * SCOL))

    with sp.Fori(0, LAYERS) as l:
        def of(w):
            return w[bass.ds(l, 1)].rearrange("o r c -> (o r) c")

        j0 = Num(J_L, (l, JL))
        w_in = of(a["w_in_2"])
        slab(j0, columns(w_in, CQ0))
        slab(j0 + 1, columns(w_in, CKV0))
        slab(j0 + 2, k_pe(w_in))
        slab(j0 + 3, lambda raw: [(raw[:, 0:2 * HEADS * QK].rearrange("p (k n) -> p k n", k=2),
                                   of(a["w_uq_2"]).rearrange("(k p) n -> p k n", p=P))])
        slab(j0 + 4, lambda raw: [(raw.rearrange("p (k n) -> p k n", k=2),
                                   of(a["w_ukv_2"]).rearrange("(k p) n -> p k n", p=P))])
        for k, c0 in enumerate((UF0, UF0 + SCOL, ZF0, ZF0 + SCOL)):
            slab(j0 + 5 + k, columns(w_in, c0))
        slab(j0 + 9, lambda raw: [(raw.rearrange("p (k n) -> p k n", k=TT),
                                   a["dft_seq"].rearrange("(k p) n -> p k n", p=P))])
        slab(j0 + 10, columns(w_in, ZA0))
        slab(j0 + 11, columns(w_in, ZA0 + SCOL), Num(U_L // 2 + UL // 2, (l, UL // 2)))
        for i in range(4):
            slab(j0 + 12 + 3 * i, columns(w_in, MA0 + i * SCOL))
            slab(j0 + 13 + 3 * i, columns(w_in, MF0 + i * SCOL))
            slab(j0 + 14 + 3 * i, pair(of(a["w_attn_proj_2"]), of(a["w_fourier_proj_2"]), i * SCOL, False))
        for i in range(4):
            slab(j0 + 24 + i, columns(of(a["w_out_2"]), i * SCOL))
    slab(Num(J_END), lambda raw: [(raw[:, 0:TAB // P], a["dft_seq"][0:P, 0:TAB // P])])

    os_ = K.out[0].rearrange("(t p) d -> p t d", p=P)
    g_end = G_L + LAYERS * GL
    for t in range(TT):
        sp.wait_ge(K.tile_out, g_end + 2 * t + 2)
        sp.dma_start(os_[:, t, :], K.xout[:, t, :]).then_inc(K.out_done, 16)
    sp.wait_ge(K.out_done, 16 * TT)


def program_pool(nc, pool, K):
    nc.gpsimd.memset(K.zero[:, :], 0.0).then_inc(K.zero_ok, 1)
    nc.gpsimd.memset(K.ones[:, :], 1.0).then_inc(K.ones_ok, 1)

    def sums(norm):
        for k in range(1, KT):
            pool.wait_ge(K.sq_ok, (norm * KT + k + 1).value())
            if (norm * (KT - 1) + k - 1).due():
                pool.wait_ge(K.sum_ok, (norm * (KT - 1) + k - 1).value())
            nc.gpsimd.tensor_tensor(K.sumsq[:, :], K.sumsq[:, :], K.sq[:, k % 2, :], ALU.add).then_inc(K.sum_ok, 1)

    def probabilities(A):
        for n in range(HEADS * TT):
            _, _, _, lo, hi = A.where(n)
            if A.kind == "B" and n % TT == 0 and n // TT + 1 < HEADS:
                masked(n // TT + 1)
            c = slice(A.first(), A.first() + (hi - lo) * P)
            pool.wait_ge(K.rden_ok, (A.u0 + n + 1).value())
            p = K.t[:, n % 3, c]
            nc.gpsimd.tensor_tensor(p, p, K.rden[:, n % 4:n % 4 + 1].broadcast_to([P, (hi - lo) * P]),
                                    ALU.mult).then_inc(K.probs_ok, 1)

    def masked(h):
        pool.wait_ge(K.biasb_in[h % 2], 16 * (h // 2 + 1))
        b = K.biasb[:, h % 2, :].rearrange("p (r c) -> p r c", c=GRID_W)
        nc.gpsimd.tensor_tensor(b, b, K.mask[:, :].unsqueeze(1).broadcast_to([P, BIAS_ROWS, GRID_W]),
                                ALU.add).then_inc(K.biasb_ok, 1)

    def mixed(sig, h0, g0):
        for m in range(2):
            pool.wait_ge(K.tile_out, (g0 + 4 + 2 * m + 2).value())
            pool.wait_ge(K.split_lo, (h0 + m - 1).value())
            nc.gpsimd.tensor_tensor(K.t[:, m, :], sig[:, m, :], sig[:, 2 + m, :], ALU.add).then_inc(K.mix_ok, 1)

    def gain(l, q):
        pool.wait_ge(K.head_sq, Num(TT * (q + 1), (l, 2 * TT)).value())
        c0 = q * NOPE
        v = K.qk[:, q, :, :].rearrange("p t (h c) -> p (t h) c", h=HEADS)[:, :, c0:QK]
        g = K.lp[:, LP_HEAD + q * QK + c0:LP_HEAD + (q + 1) * QK]
        nc.gpsimd.tensor_tensor(v, v, g.unsqueeze(1).broadcast_to([P, TT * HEADS, QK - c0]),
                                ALU.mult).then_inc(K.qk_ready, 1)

    def rotate(l, q, i):
        half = ROPE // 2
        ts = slice(2 * i, 2 * i + 2)
        x = K.qk[:, q, ts, :].rearrange("p t (h c) -> p t h c", h=HEADS)
        x1, x2 = x[:, :, :, NOPE:NOPE + half], x[:, :, :, NOPE + half:QK]
        cos = K.rope[:, ts, 0:half].unsqueeze(2).broadcast_to([P, 2, HEADS, half])
        sin = K.rope[:, ts, half:ROPE].unsqueeze(2).broadcast_to([P, 2, HEADS, half])
        ra, rb, rc = [b.rearrange("p (t h c) -> p t h c", t=2, h=HEADS)
                      for b in (K.rt[:, 0, :], K.rt[:, 1, :], K.sumsq[:, 0:2 * P])]
        r = Num(12 * q + 6 * i, (l, 24))
        pool.wait_ge(K.qk_ready, Num(q + 1, (l, 2)).value())
        if r.due():
            pool.wait_ge(K.rope_ok, r.value())
        nc.gpsimd.tensor_tensor(ra, x1, cos, ALU.mult).then_inc(K.rope_ok, 1)
        nc.gpsimd.tensor_tensor(rb, x2, sin, ALU.mult).then_inc(K.rope_ok, 1)
        nc.gpsimd.tensor_tensor(rc, x1, sin, ALU.mult).then_inc(K.rope_ok, 1)
        nc.gpsimd.tensor_tensor(x2, x2, cos, ALU.mult).then_inc(K.rope_ok, 1)
        pool.wait_ge(K.rope_ok, (r + 4).value())
        nc.gpsimd.tensor_tensor(x1, ra, rb, ALU.subtract).then_inc(K.rope_ok, 1)
        nc.gpsimd.tensor_tensor(x2, x2, rc, ALU.add).then_inc(K.rope_ok, 1)

    def silu_f(l, t):
        pool.wait_ge(K.sig_ok, (sig_num(l, t) + 1).value())
        nc.gpsimd.tensor_tensor(K.z[:, t, :], K.z[:, t, :], sig_f(K, t), ALU.mult).then_inc(K.pool_ok, 1)

    sums(Num(0))
    pool.wait_ge(K.tab_zeroed, 16)
    nc.gpsimd.memset(K.pt["A"][0][:, :, 2, 0, :].bitcast(F32), 0.0).then_inc(K.pt_zero, 1)
    pool.wait_ge(K.w_lo, J_MERGE + 1)
    nc.gpsimd.memset(K.pt["A"][1][:, :, 1, 1, :].bitcast(F32), 0.0).then_inc(K.pt_zero, 1)
    probabilities(Heads(K, "A"))
    pool.wait_ge(K.par_in, 16 * PAR_DMAS)
    masked(0)
    probabilities(Heads(K, "B"))
    for i in range(4):
        mixed(K.sig1, Num(H_MERGE + 2 * i), Num(G_MERGE + 8 * i))
    sums(Num(1))
    for k in range(1, KT):
        for i, (total, square) in enumerate(((K.sumsq_f, K.sq_f), (K.sumsq, K.sq))):
            n = 2 * (KT - 1) + 2 * (k - 1) + i
            pool.wait_ge(K.sq_ok, 2 * KT + 2 * k + i + 1)
            if n >= 2:
                pool.wait_ge(K.sum_ok, n - 1)
            nc.gpsimd.tensor_tensor(total[:, :], total[:, :], square[:, k % 2, :], ALU.add).then_inc(K.sum_ok, 1)
    with pool.Fori(0, LAYERS) as l:
        for i, (one, two) in enumerate(((K.sq[:, 0, :], K.sq[:, 1, :]), (K.hsq[:, 0, 0:SEQ], K.hsq[:, 1, 0:SEQ]))):
            pool.wait_ge(K.lat_sq, Num(2 * i + 2, (l, 4)).value())
            nc.gpsimd.tensor_tensor(one, one, two, ALU.add).then_inc(K.lat_sum, 1)
        pool.wait_ge(K.prior_taken, Num(1, (l, 1)).value())
        nc.gpsimd.tensor_tensor(K.x[:, :, :], K.x[:, :, :], K.rstd_f[:, :].unsqueeze(1).broadcast_to([P, KT, SEQ]),
                                ALU.mult).then_inc(K.x_fin, 1)
        pool.wait_ge(K.x_fin, Num(1, (l, 2)).value())
        nc.gpsimd.tensor_tensor(K.x[:, :, :], K.x[:, :, :], K.gains[:, 2, :].unsqueeze(2).broadcast_to([P, KT, SEQ]),
                                ALU.mult).then_inc(K.x_fin, 1)
        for q in range(2):
            gain(l, q)
            rotate(l, q, 0)
            rotate(l, q, 1)
        for t in range(4):
            silu_f(l, t)
        probabilities(Heads(K, "L", l))
        for t in range(HALF):
            pool.wait_ge(K.sig_ok, (sig_num(l, 4 + t) + 1).value())
            nc.gpsimd.tensor_tensor(K.sq[:, t % 2, :], K.sq[:, t % 2, :], K.t[:, t % 3, :],
                                    ALU.mult).then_inc(K.pool_ok, 1)
            pool.wait_ge(K.pool_ok, Num(4 + 2 * t + 1, (l, 12)).value())
            nc.gpsimd.tensor_tensor(K.t[:, t % 3, :], K.sq[:, t % 2, :], K.z[:, t, :],
                                    ALU.mult).then_inc(K.pool_ok, 1)
        for i in range(4):
            mixed(K.sig2, Num(H_L + 24 + 2 * i, (l, HL)), Num(G_L + 68 + 8 * i, (l, GL)))
        sums(Num(4, (l, 1)))


def sig_f(K, t):
    return K.sq[:, t, :] if t < 2 else K.t[:, t - 1, :]


def sig_num(l, k):
    return Num(16 + k, (l, 24))


def program_act(nc, act, K):
    a = K.a
    act.dma_start(K.ident[:, :], a["ident"]).then_inc(K.ident_in, 16)
    act.dma_start(K.gains[:, 0, :], by_feature(a["norm_mix"][0]), allow_slow_non_contiguous=True).then_inc(K.gain_in, 16)

    def split(j, used, n=SLAB):
        act.wait_ge(K.w_in_sem[j % 2], ((j // 2 + 1) * 64).value())
        if used.due():
            act.wait_ge(K.tile_full, used.value())
        nc.scalar.activation(K.w[:, j % 2, 0, 0:n], K.raw[:, j % 2, 0:n], ACT.Copy).then_inc(K.w_hi, 1)

    def load_table(function):
        nc.scalar.activation(K.unused[:, :], K.ident[:, 0:1], function)

    def split_qa(j):
        act.wait_ge(K.w_in_sem[j], 64)
        for e in range(2):
            part = nc.scalar.activation(qa_order(K.w[:, j, 0, :], e), qa_raw_order(K.raw[:, j, :], e), ACT.Copy)
        part.then_inc(K.w_hi, 1)

    def norm_tile(norm, k, gains, ready):
        act.wait_ge(K.tile_out, ready.value())
        if k > 2:
            act.wait_ge(K.sum_ok, (norm * (KT - 1) + k - 2).value())
        nc.scalar.activation(K.sq[:, k % 2, :] if k else K.sumsq[:, :], K.x[:, k, :],
                             ACT.Square).then_inc(K.sq_ok, 1)
        nc.scalar.activation(K.gx[:, 0, k, :], K.x[:, k, :], ACT.Copy,
                             scale=gains[:, k:k + 1]).then_inc(K.gx_hi, 1)

    def final_tile(k, ready):
        act.wait_ge(K.tile_out, ready.value())
        if k > 2:
            act.wait_ge(K.sum_ok, 2 * (KT - 1) + 2 * (k - 2))
        gain = K.gains[:, 2, k:k + 1]
        nc.scalar.activation(K.sq_f[:, k % 2, :] if k else K.sumsq_f[:, :], K.x[:, k, :],
                             ACT.Square).then_inc(K.sq_ok, 1)
        nc.scalar.activation(K.sq[:, k % 2, :] if k else K.sumsq[:, :], K.x[:, k, :], ACT.Square,
                             scale=gain).then_inc(K.sq_ok, 1)
        nc.scalar.activation(K.gx[:, 0, k, :], K.x[:, k, :], ACT.Copy,
                             scale=K.gains[:, 3, k:k + 1]).then_inc(K.gx_hi, 1)

    def stat(norm, s):
        act.wait_ge(K.s_taken, (s + 1).value())
        nc.scalar.activation(K.d4[:, :], K.v4[:, :], ACT.Sqrt).then_inc(K.stat_sqrt, 1)

    def hi(dst, src):
        nc.scalar.activation(dst, src, ACT.Copy).then_inc(K.split_hi, 1)

    def qk_hi(A, h):
        for q in range(2):
            act.wait_ge(K.tile_full, A.f_qk(h, q).value())
            nc.scalar.activation(K.qkh[0:QK, h % 2, q, 0, :], K.G[(A.g_qk(h) + q) % GB][0:QK, :],
                                 ACT.Copy).then_inc(K.qk_hi, 1)

    def attention(A):
        U, S = A.u0, A.s0

        def exps(n):
            _, _, _, lo, hi_ = A.where(n)
            width = A.first() + (hi_ - lo) * P
            act.wait_ge(K.s_taken, (S + n + 1).value())
            if (U + n - 2).due():
                act.wait_ge(K.trans_full, (U + n - 2).value())
            nc.scalar.activation(K.t[:, n % 3, 0:width], K.sq[:, n % 2, 0:width], ACT.Exp, bias=K.nm[:, n % 4:n % 4 + 1],
                                 scale=-1.0, accum_out=K.den[:, n % 4:n % 4 + 1]).then_inc(K.exp_ok, 1)

        def out_hi(h):
            act.wait_ge(K.pv_done, A.pairs(2 * h + 1).value())
            t, e = h // 2, h % 2
            r = slice(e * HD, (e + 1) * HD)
            q = K.qa if A.kind == "A" else K.qb
            nc.scalar.activation(A.rows(q[r, 0, t, :]), A.in_order(K.G[A.g_out(h) % GB][r, :]), ACT.Copy).then_inc(K.y_hi, 1)

        exps(0)
        if A.kind == "L":
            qk_hi(A, 1)
        exps(1)
        for n in range(HEADS * TT):
            if A.turned(n) is not None:
                qk_hi(A, A.turned(n))
            if A.last_of(n) is not None and A.kind != "L":
                out_hi(A.last_of(n))
            if n + 2 < HEADS * TT:
                exps(n + 2)
            m, e = n // 2, n % 2
            _, _, _, lo, hi_ = A.where(n)
            act.wait_ge(K.trans_full, (U + n + 1).value())
            if A.pairs(m - 2).due():
                act.wait_ge(K.pv_done, A.pairs(m - 2).value())
            nc.scalar.activation(K.pt[A.kind][m % 2][:, 0, lo:hi_, e, :],
                                 K.T[(U + n) % 2][:, 0:(hi_ - lo) * P].rearrange("p (k c) -> p k c", c=P),
                                 ACT.Copy).then_inc(K.pt_hi, 1)
        if A.kind != "A":
            load_table(ACT.Sigmoid)
        if A.kind != "L":
            out_hi(HEADS - 1)

    def sigmoid(dst, src, bias=0.0):
        nc.scalar.activation(dst, src, ACT.Sigmoid, bias=bias).then_inc(K.sig_ok, 1)

    def merge(sig, dst, bias, j, g, f, mix, pair_, first=None):
        for b in range(2):
            split(j + b + 1, f + 2 * b)
            if b == 0 and first is not None:
                first()
            for k in range(2):
                col = b * KT + 2 * pair_ + k
                act.wait_ge(K.tile_out, (g + 2 * b + k + 1).value())
                sigmoid(sig[:, 2 * b + k, :], sig[:, 2 * b + k, :], bias=bias[:, col:col + 1])
        split(j + 3, f + 4)
        for k in range(2):
            act.wait_ge(K.mix_ok, (mix + k + 1).value())
            hi(dst[:, 0, 2 * pair_ + k, :], K.t[:, k, :])

    act.wait_ge(K.ident_in, 16)
    load_table(ACT.Sqrt)
    act.wait_ge(K.gain_in, 16)
    for k in range(KT):
        norm_tile(Num(0), k, K.gains[:, 0, :], Num(G_X + k + 1))
        if k == HALF:
            split_qa(0)
    split_qa(1)
    last = -1
    for k, (j, _, form, to) in enumerate(IN_TILES):
        if k == 0:
            stat(Num(0), Num(0))
            load_table(ACT.Exp)
        if j != last:
            split(Num(j + 1), Num(IN_ENDS[j - 1]))
            last = j
        if form == "turn":
            act.wait_ge(K.va_full, 1)
            hi(in_dest(K, to, 0), in_shape(to, K.T[0][:, :]))
            continue
        act.wait_ge(K.tile_out, Num(G_IN + k + 1).value())
        hi(in_dest(K, to, 0), in_shape(to, K.t[:, k % 3, :]))
    attention(Heads(K, "A"))
    attention(Heads(K, "B"))
    act.wait_ge(K.par_in, 16 * PAR_DMAS)
    for i in range(4):
        merge(K.sig1, K.big, K.bg, Num(J_MERGE + 3 * i), Num(G_MERGE + 8 * i), Num(F_MERGE + 8 * i), Num(2 * i), i)
    load_table(ACT.Sqrt)
    for i in range(4):
        split(Num(J_OUT + i + 1), Num(F_OUT + 2 * i))
        for k in range(2 * i, 2 * i + 2):
            norm_tile(Num(1), k, K.gains[:, 1, :], Num(G_OUT + k + 1))
    stat(Num(1), Num(S_N2))

    def chunk(c, last=False):
        for i in range(8):
            split(Num(J_MLP + i + 1, (c, 8)), Num(F_MLP + 2 * i, (c, 16)))
            for k in range(2 * i, 2 * i + 2):
                if i < 4:
                    h = Num(H_MLP + k, (c, 8))
                    act.wait_ge(K.tile_out, Num(G_MLP + k + 1, (c, 16)).value())
                    act.wait_ge(K.split_lo, (h - 1).value())
                    nc.scalar.activation(K.sq[:, k % 2, :], K.t[:, k % 3, :], ACT.Square).then_inc(K.up_sq, 1)
                    nc.scalar.activation(K.big[:, 0, k, :], K.t[:, k % 3, :], ACT.Square).then_inc(K.split_hi, 1)
                elif last:
                    final_tile(k - KT, Num(G_MLP + k + 1, (c, 16)))

    with act.Fori(0, CHUNKS - 1) as c:
        chunk(c)
    act.wait_ge(K.group_in, 32)
    nc.scalar.activation(K.sw[:, 0, :], K.sraw[:, 0:SCOL], ACT.Copy).then_inc(K.group_hi, 1)
    nc.scalar.activation(K.alt[:, :], K.sraw[:, SCOL:SCOL + SEQ], ACT.Copy).then_inc(K.group_hi, 1)
    act.wait_ge(K.gain_ok, 1)
    chunk(CHUNKS - 1, True)
    stat(Num(2), Num(S_NF))
    with act.Fori(0, LAYERS) as l:
        j, g, f, h, s = (Num(n, (l, per)) for n, per in ((J_L, JL), (G_L, GL), (F_L, FL), (H_L, HL), (S_L, SL)))
        act.wait_ge(K.lp_ok, Num(1, (l, 1)).value())
        split(j + 1, f)
        act.wait_ge(K.prior_ok, Num(3, (l, 4)).value())
        nc.scalar.activation(K.d4[:, :], K.v4[:, :], ACT.Sqrt).then_inc(K.stat_sqrt, 1)
        squares = [K.sq[:, 0, :], K.sq[:, 1, :], K.hsq[:, 0, 0:SEQ], K.hsq[:, 1, 0:SEQ]]
        for k in range(4):
            if k == 0:
                split(j + 2, f + 2, KT * P)
            act.wait_ge(K.tile_out, (g + k + 1).value())
            nc.scalar.activation(squares[k], K.t[:, k % 3, :], ACT.Square).then_inc(K.lat_sq, 1)
            nc.scalar.activation(K.u[:, 0, k, :], K.t[:, k % 3, :], ACT.Copy,
                                 scale=K.lp[:, LP_LAT + k:LP_LAT + k + 1]).then_inc(K.split_hi, 1)
        split(j + 3, f + 4)
        act.wait_ge(K.s_taken, (s + 4).value())
        nc.scalar.activation(K.lat_d[:, :], K.lat_v[:, :], ACT.Sqrt).then_inc(K.lat_sqrt, 1)
        split(j + 4, f + 5)
        split(j + 5, f + 12)
        for t in range(TT):
            for half in range(2):
                k = 2 * t + half
                act.wait_ge(K.tile_out, (g + 12 + k + 1).value())
                hi(K.v[:, 0, t, half * SCOL:(half + 1) * SCOL], K.t[:, k % 3, 0:SCOL])
        for i in range(4):
            split(j + 6 + i, f + 20 + 2 * i)
            for k in range(2 * i, 2 * i + 2):
                for n in HEAD_SQUARES[k]:
                    q, t = divmod(n, TT)
                    act.wait_ge(K.tile_out, (g + (4, 12)[q] + 2 * t + 2).value())
                    if Num(n - 1, (l, 2 * TT)).due():
                        act.wait_ge(K.head_red, Num(n - 1, (l, 2 * TT)).value())
                    nc.scalar.activation(K.hsq[:, n % 2, :], K.qk[:, q, t, :], ACT.Square).then_inc(K.head_sq, 1)
                if k == HEAD_ROOT:
                    act.wait_ge(K.head_v, Num(1, (l, 1)).value())
                    nc.scalar.activation(K.hd_[:, :, :], K.hs[:, :, :], ACT.Sqrt).then_inc(K.head_sqrt, 1)
                if i < 2:
                    for m in {0: (), TT - 1: (TT - 2, TT - 1)}.get(k, (k - 1,)):
                        act.wait_ge(K.fold_ok, Num(m + 1, (l, TT)).value())
                        hi(K.u[:, 0, m, :], K.sq[:, m % 2, :])
                else:
                    act.wait_ge(K.tile_out, (g + 20 + k + 1).value())
                    act.wait_ge(K.split_lo, (h + 12 + TT).value())
                    sigmoid(sig_f(K, k - 4), K.z[:, k - 4, :])
        gi, heads = 28, Heads(K, "L", l)
        for stage, grp in FOURIER:
            if (stage, grp) == ("seq", 2):
                load_table(ACT.Exp)
            if (stage, grp) == ("seq", 0):
                split(j + 10, f + 28)
            if stage == "dim":
                for half in range(2):
                    act.wait_ge(K.tile_full, (f + gi + 1).value())
                    c = ab_columns(half)
                    nc.scalar.activation(K.ab[:, grp % 2, 0, 2 * half:2 * half + 2, c],
                                         K.G[(g + gi) % GB][:, :].rearrange("p (t c) -> p t c", t=2)[:, :, c],
                                         ACT.Copy).then_inc(K.ab_hi, 1)
                    gi += 1
            elif stage == "turn":
                qk_hi(heads, grp)
                gi += 2
            else:
                act.wait_ge(K.tile_out, (g + gi + 1).value())
                hi(K.u[:, 0, grp, :], K.t[:, (grp + 2) % 3, :])
                gi += 1
        attention(heads)
        def branch_hi(t):
            act.wait_ge(K.pool_ok, Num(4 + 2 * t + 2, (l, 12)).value())
            hi(K.v[:, 0, t, :], K.t[:, t % 3, :])

        for i in range(2):
            split(j + 11 + i, f + 56 + 2 * i)
            for t in range(2 * i, 2 * i + 2):
                act.wait_ge(K.pool_ok, Num(4 + 2 * t - 2, (l, 12)).value())
                act.wait_ge(K.tile_out, (g + 64 + t + 1).value())
                sigmoid(K.sq[:, t % 2, :], K.t[:, t % 3, :])
                if t:
                    branch_hi(t - 1)
        for i in range(4):
            merge(K.sig2, K.m2, K.lp[:, LP_MERGE:LP_MERGE + 2 * KT], j + 12 + 3 * i, g + 68 + 8 * i,
                  f + 60 + 8 * i, Num(KT + 2 * i, (l, KT)), i, (lambda: branch_hi(HALF - 1)) if i == 0 else None)
        load_table(ACT.Sqrt)
        for i in range(4):
            split(j + 24 + i + 1, f + 92 + 2 * i)
            if i == 0:
                act.wait_ge(K.next_ok, Num(1, (l, 1)).value())
            for k in range(2 * i, 2 * i + 2):
                norm_tile(Num(4, (l, 1)), k, K.norm_next, g + 100 + k + 1)


def program_vector(nc, dve, K):
    def split(j, n=SLAB):
        dve.wait_ge(K.w_hi, (j + 1).value())
        s = j % 2
        nc.vector.tensor_tensor(K.w[:, s, 1, 0:n], K.raw[:, s, 0:n], K.w[:, s, 0, 0:n].bitcast(F32),
                                ALU.subtract).then_inc(K.w_lo, 1)

    def split_qa(j):
        dve.wait_ge(K.w_hi, j + 1)
        for e in range(2):
            part = nc.vector.tensor_tensor(qa_order(K.w[:, j, 1, :], e), qa_raw_order(K.raw[:, j, :], e),
                                           qa_order(K.w[:, j, 0, :], e).bitcast(F32), ALU.subtract)
        part.then_inc(K.w_lo, 1)

    def lo(dst, src, hi, h):
        dve.wait_ge(K.split_hi, (h + 1).value())
        nc.vector.tensor_tensor(dst, src, hi.bitcast(F32), ALU.subtract).then_inc(K.split_lo, 1)

    def lo_gain(dst, src, gain, hi, done):
        nc.vector.scalar_tensor_tensor(out=dst, in0=src, scalar=gain, in1=hi.bitcast(F32), op0=ALU.mult,
                                       op1=ALU.subtract).then_inc(done, 1)

    def gx_lo(k, gains, gx):
        dve.wait_ge(K.gx_hi, (gx + k + 1).value())
        lo_gain(K.gx[:, 1, k, :], K.x[:, k, :], gains[:, k:k + 1], K.gx[:, 0, k, :], K.gx_lo)

    def full(f):
        dve.wait_ge(K.tile_full, (f + 1).value())

    def psum(g):
        return K.G[g % GB]

    def normed(dst, g, f, scale=1.0):
        full(f)
        nc.vector.scalar_tensor_tensor(out=dst, in0=psum(g)[:, :], scalar=scale, in1=K.rstd[:, :], op0=ALU.mult,
                                       op1=ALU.mult).then_inc(K.tile_out, 1)

    def rsqrt(y, root, v, sem, n):
        nc.vector.reciprocal(y, root).then_inc(sem, 1)
        dve.wait_ge(sem, (n + 1).value())
        nc.vector.tensor_tensor(root, y, y, ALU.mult).then_inc(sem, 1)
        dve.wait_ge(sem, (n + 2).value())
        nc.vector.scalar_tensor_tensor(out=root, in0=root, scalar=-0.5, in1=v, op0=ALU.mult, op1=ALU.mult).then_inc(sem, 1)
        dve.wait_ge(sem, (n + 3).value())
        nc.vector.scalar_tensor_tensor(out=y, in0=root, scalar=1.5, in1=y, op0=ALU.add, op1=ALU.mult).then_inc(sem, 1)
        dve.wait_ge(sem, (n + 4).value())

    def stat(norm, s):
        dve.wait_ge(K.s_full, (s + 1).value())
        nc.vector.tensor_scalar(K.v4[:, :], K.S[s % 2][:, 0:TT], 1.0 / D, EPS, ALU.mult, ALU.add).then_inc(K.s_taken, 1)
        dve.wait_ge(K.stat_sqrt, (norm + 1).value())
        rsqrt(K.r4[:, :], K.d4[:, :], K.v4[:, :], K.stat_rec, norm * 4)

    def diagonal(tile, r, done):
        nc.vector.tensor_tensor(tile.rearrange("p (t c) -> p t c", t=TT), K.ident[:, :].unsqueeze(1).broadcast_to([P, TT, P]),
                                r.unsqueeze(2).broadcast_to([P, TT, P]), ALU.mult).then_inc(done, 1)

    def spread(s, meanwhile=None):
        diagonal(K.sq[:, 0, :], K.r4[:, :], K.stat_diag)
        if meanwhile is not None:
            meanwhile()
        dve.wait_ge(K.s_full, (s + 2).value())
        nc.vector.tensor_copy(K.rstd[:, :], K.S[(s + 1) % 2][:, :]).then_inc(K.s_taken, 1)
        dve.wait_ge(K.s_taken, (s + 2).value())

    def layer_stat(l, s, meanwhile):
        norm = Num(3, (l, 1))
        dve.wait_ge(K.prior_ok, Num(1, (l, 4)).value())
        dve.wait_ge(K.sum_ok, (norm * (KT - 1) + KT - 1).value())
        diagonal(K.sq[:, 1, :], K.prior[:, :], K.prior_diag)
        nc.vector.tensor_tensor(K.prior2[:, :], K.prior[:, :], K.prior[:, :], ALU.mult).then_inc(K.prior_ok, 1)
        dve.wait_ge(K.s_full, (s + 1).value())
        dve.wait_ge(K.prior_ok, Num(2, (l, 4)).value())
        nc.vector.scalar_tensor_tensor(out=K.v4[:, :], in0=K.S[s % 2][:, 0:TT], scalar=1.0 / D, in1=K.prior2[:, :],
                                       op0=ALU.mult, op1=ALU.mult).then_inc(K.s_taken, 1)
        dve.wait_ge(K.s_taken, (s + 1).value())
        nc.vector.tensor_scalar(K.v4[:, :], K.v4[:, :], EPS, None, ALU.add).then_inc(K.prior_ok, 1)
        meanwhile()
        dve.wait_ge(K.stat_sqrt, (norm + 1).value())
        rsqrt(K.r4[:, :], K.d4[:, :], K.v4[:, :], K.stat_rec, norm * 4)
        nc.vector.tensor_tensor(K.r4[:, :], K.r4[:, :], K.prior[:, :], ALU.mult).then_inc(K.prior_ok, 1)
        dve.wait_ge(K.prior_ok, Num(4, (l, 4)).value())
        spread(s)
        nc.vector.memset(K.prior[:, :], 1.0).then_inc(K.prior_ok, 1)
        dve.wait_ge(K.prior_full, Num(1, (l, 1)).value())
        nc.vector.tensor_copy(K.rstd_f[:, :], K.T[1][:, :]).then_inc(K.prior_taken, 1)

    def qk_lo(A, h):
        for q in range(2):
            dve.wait_ge(K.qk_hi, A.split(h, q).value())
            nc.vector.tensor_tensor(K.qkh[0:QK, h % 2, q, 1, :], psum(A.g_qk(h) + q)[0:QK, :],
                                    K.qkh[0:QK, h % 2, q, 0, :].bitcast(F32), ALU.subtract).then_inc(K.tile_out, 1)

    def attention(A, first=None):
        U, S = A.u0, A.s0
        total = HEADS * TT

        def scores(n):
            h = n // TT
            t, e, i, b0, b1 = A.where(n)
            c = slice(A.first(), A.first() + (b1 - b0) * P)
            first, scale = 3.0e38, -1.0
            if A.kind == "L":
                dve.wait_ge(K.s_full, (S + n + 1).value())
                if n:
                    rden(n - 1)
                else:
                    nc.vector.memset(K.spare[:, :], 0.0)
            elif (U + n - 1).due():
                dve.wait_ge(K.exp_ok, (U + n - 1).value())
            if A.kind == "A":
                dve.wait_ge(K.biasa_in[h % 2], 16 * (h // 2 + 1))
                off = (b0 - i + 1) * P
                bias = K.biasa[:, h % 2, off:off + (b1 - b0) * P]
                head = e * HALF + t
                first = K.sink[:, head:head + 1]
                if i < 2:
                    nc.vector.tensor_copy(K.sq[:, n % 2, 0:1], first)
            elif A.kind == "B":
                dve.wait_ge(K.biasb_ok, h + 1)
                off = (KH - 2 - 2 * i) * GRID_W
                bias = K.biasb[:, h % 2, off:off + SEQ]
            else:
                bias = K.zeros[:, :].broadcast_to([P, SEQ])
                scale = K.hr[:, 0, i * HEADS + h:i * HEADS + h + 1]
            if A.kind != "L":
                dve.wait_ge(K.s_full, (S + n + 1).value())
            nc.vector.tensor_tensor_reduce(K.sq[:, n % 2, c], K.S[(S + n) % 2][:, 0:(b1 - b0) * P], bias, scale, first,
                                           ALU.add, ALU.min, K.nm[:, n % 4:n % 4 + 1]).then_inc(K.s_taken, 1)

        def rden(n):
            c = slice(n % 4, n % 4 + 1)
            dve.wait_ge(K.exp_ok, (U + n + 1).value())
            nc.vector.reciprocal(K.rden[:, c], K.den[:, c]).then_inc(K.rden_ok, 1)

        def out(h):
            g = A.g_out(h)
            t, e = h // 2, h % 2
            r = slice(e * HD, (e + 1) * HD)
            if A.kind == "L":
                dve.wait_ge(K.pv_done, A.pairs(2 * h + 1).value())
                nc.vector.tensor_copy(K.z[r, t, :], psum(g)[r, :]).then_inc(K.tile_out, 1)
                return
            q = K.qa if A.kind == "A" else K.qb
            dve.wait_ge(K.y_hi, (0 if A.kind == "A" else HEADS) + h + 1)
            nc.vector.tensor_tensor(A.rows(q[r, 1, t, :]), A.in_order(psum(g)[r, :]), A.rows(q[r, 0, t, :]).bitcast(F32),
                                    ALU.subtract).then_inc(K.tile_out, 1)

        def low(n):
            m, e = n // 2, n % 2
            _, _, _, b0, b1 = A.where(n)
            dve.wait_ge(K.pt_hi, (U + n + 1).value())
            nc.vector.tensor_tensor(K.pt[A.kind][m % 2][:, 1, b0:b1, e, :],
                                    K.T[(U + n) % 2][:, 0:(b1 - b0) * P].rearrange("p (k c) -> p k c", c=P),
                                    K.pt[A.kind][m % 2][:, 0, b0:b1, e, :].bitcast(F32), ALU.subtract).then_inc(K.pt_lo, 1)

        if A.kind == "L":
            dve.wait_ge(K.head_scaled, A.scaled.value())
        for n in range(AHEAD):
            if n == 2 and A.kind == "L":
                qk_lo(A, 1)
            scores(n)
            if n == 0 and first is not None:
                first()
        if A.kind != "L":
            rden(0)
            rden(1)
        for n in range(total):
            if A.turned(n) is not None:
                qk_lo(A, A.turned(n))
            if n + AHEAD < total:
                scores(n + AHEAD)
            if A.last_of(n) is not None:
                out(A.last_of(n))
            if n + 2 < total and (A.kind != "L" or n + AHEAD == total):
                rden(n + 2)
            low(n)
        out(HEADS - 1)

    def merge(sig, dst, j, g, f, h, mix, sig0, pair_, first=None):
        for b in range(2):
            split(j + b + 1)
            if b == 0 and first is not None:
                first()
            for k in range(2):
                if b == 0:
                    if (mix + k - 1).due():
                        dve.wait_ge(K.mix_ok, (mix + k - 1).value())
                normed(sig[:, 2 * b + k, :], g + 2 * b + k, f + 2 * b + k)
        split(j + 3)
        for k in range(2):
            for b in range(2):
                n = 4 + 2 * k + b
                full(f + n)
                dve.wait_ge(K.sig_ok, (sig0 + 2 * b + k + 1).value())
                s = sig[:, 2 * b + k, :]
                nc.vector.tensor_tensor(s, psum(g + n)[:, :], s, ALU.mult).then_inc(K.tile_out, 1)
        for k in range(2):
            c = 2 * pair_ + k
            lo(dst[:, 1, c, :], K.t[:, k, :], dst[:, 0, c, :], h + k)

    for k in range(KT + 1):
        if k < KT:
            full(Num(F_X + k))
            nc.vector.tensor_copy(K.x[:, k, :], psum(Num(G_X + k))[:, :]).then_inc(K.tile_out, 1)
        if k:
            if k == 1:
                dve.wait_ge(K.gain_in, 16)
            gx_lo(k - 1, K.gains[:, 0, :], Num(0))
        if k == HALF + 1:
            split_qa(0)
    split_qa(1)

    def in_lo(k):
        _, _, form, to = IN_TILES[k]
        src = K.T[0][:, :] if form == "turn" else K.t[:, k % 3, :]
        lo(in_dest(K, to, 1), in_shape(to, src), in_dest(K, to, 0), Num(H_IN + k))

    last = -1
    for k, (j, _, form, to) in enumerate(IN_TILES):
        if k == 0:
            stat(Num(0), Num(0))
            spread(Num(0))
        if j != last:
            split(Num(j + 1))
            last = j
        t = K.t[:, k % 3, :]
        g, f = Num(G_IN + k), Num(F_IN + k)
        if H_IN + k - 2 > 0:
            dve.wait_ge(K.split_lo, H_IN + k - 2)
        if form == "tm":
            tts = slice(2 * (to[1] % 2), 2 * (to[1] % 2) + 2)
            full(f)
            nc.vector.tensor_tensor(in_shape(to, t), in_shape(to, psum(g)[:, :]),
                                    K.r4[:, tts].unsqueeze(2).broadcast_to([P, 2, SCOL]),
                                    ALU.mult).then_inc(K.tile_out, 1)
        else:
            normed(t, g, f, float(HD) ** -0.5 if form == "q" else 1.0)
        if k:
            in_lo(k - 1)
    in_lo(len(IN_TILES) - 1)
    dve.wait_ge(K.par_in, 16 * PAR_DMAS)
    nc.vector.tensor_scalar(K.sink[:, :], K.sink[:, :], -1.0, None, ALU.mult).then_inc(K.sink_ok, 1)
    nc.vector.memset(K.zeros[:, :], 0.0).then_inc(K.sink_ok, 1)
    both = [K.lp_all[:, :, LP_HEAD + q * QK:LP_HEAD + q * QK + NOPE] for q in range(2)]
    nc.vector.tensor_tensor(both[0], both[0], both[1], ALU.mult).then_inc(K.sink_ok, 1)
    dve.wait_ge(K.sink_ok, 3)
    attention(Heads(K, "A"))
    attention(Heads(K, "B"))
    for i in range(4):
        merge(K.sig1, K.big, Num(J_MERGE + 3 * i), Num(G_MERGE + 8 * i), Num(F_MERGE + 8 * i),
              Num(H_MERGE + 2 * i), Num(2 * i), Num(4 * i), i)

    def residual(k, g, f):
        full(f)
        nc.vector.tensor_tensor(K.x[:, k, :], psum(g)[:, :], K.x[:, k, :], ALU.add).then_inc(K.tile_out, 1)

    for i in range(4):
        split(Num(J_OUT + i + 1))
        for k in range(2 * i, 2 * i + 2):
            residual(k, Num(G_OUT + k), Num(F_OUT + k))
            if k:
                gx_lo(k - 1, K.gains[:, 1, :], Num(KT))
    gx_lo(KT - 1, K.gains[:, 1, :], Num(KT))
    stat(Num(1), Num(S_N2))
    spread(Num(S_N2), lambda: split(Num(J_MLP + 1)))
    nc.vector.tensor_tensor(K.gains[:, 3, :], K.gains[:, 2, :], K.norm_all[:, 0, :], ALU.mult).then_inc(K.gain_ok, 1)

    def chunk(c, last=False):
        def up_lo(k):
            lo(K.big[:, 1, k, :], K.sq[:, k % 2, :], K.big[:, 0, k, :], Num(H_MLP + k, (c, 8)))

        for i in range(8):
            for k in range(2 * i, 2 * i + 2):
                g, f = Num(G_MLP + k, (c, 16)), Num(F_MLP + k, (c, 16))
                if i < 4:
                    full(f)
                    nc.vector.scalar_tensor_tensor(out=K.t[:, k % 3, :], in0=psum(g)[:, :], scalar=0.0, in1=K.rstd[:, :],
                                                   op0=ALU.max, op1=ALU.mult).then_inc(K.tile_out, 1)
                else:
                    residual(k - KT, g, f)
                    if last and k > KT:
                        gx_lo(k - KT - 1, K.gains[:, 3, :], Num(2 * KT))
                if 0 < k < KT:
                    up_lo(k - 1)
                if k == KT - 1:
                    up_lo(k)
            if not last or i < 7:
                split(Num(J_MLP + i + 2, (c, 8)))

    with dve.Fori(0, CHUNKS - 1) as c:
        chunk(c)
    dve.wait_ge(K.group_hi, 2)
    nc.vector.tensor_tensor(K.sw[:, 1, :], K.sraw[:, 0:SCOL], K.sw[:, 0, :].bitcast(F32),
                            ALU.subtract).then_inc(K.group_lo, 1)
    dve.wait_ge(K.gain_ok, 1)
    chunk(CHUNKS - 1, True)
    gx_lo(KT - 1, K.gains[:, 3, :], Num(2 * KT))
    stat(Num(2), Num(S_NF))
    nc.vector.tensor_copy(K.prior[:, :], K.r4[:, :]).then_inc(K.prior_ok, 1)
    with dve.Fori(0, LAYERS) as l:
        j, g, f, h, s = (Num(n, (l, per)) for n, per in ((J_L, JL), (G_L, GL), (F_L, FL), (H_L, HL), (S_L, SL)))
        nc.vector.tensor_copy(K.lp[:, :], K.lp_all[:, bass.ds(l, 1), :].rearrange("p o c -> p (o c)")).then_inc(K.lp_ok, 1)
        dve.wait_ge(K.gx_lo, Num(3 * KT, (l, KT)).value())
        nc.vector.tensor_copy(K.norm_next[:, :], K.norm_all[:, bass.ds(l + 1, 1), :].rearrange("p o c -> p (o c)")).then_inc(K.next_ok, 1)
        dve.wait_ge(K.lp_ok, Num(1, (l, 1)).value())
        layer_stat(l, s, lambda: split(j + 1))

        def lat_lo(k):
            dve.wait_ge(K.split_hi, (h + k + 1).value())
            lo_gain(K.u[:, 1, k, :], K.t[:, k % 3, :], K.lp[:, LP_LAT + k:LP_LAT + k + 1], K.u[:, 0, k, :], K.split_lo)

        for k in range(4):
            if k == 3:
                dve.wait_ge(K.split_lo, (h + 1).value())
            normed(K.t[:, k % 3, :], g + k, f + k)
            if k == 1:
                split(j + 2, KT * P)
            if k:
                lat_lo(k - 1)
        lat_lo(3)
        split(j + 3)
        dve.wait_ge(K.s_full, (s + 3).value())
        nc.vector.tensor_tensor(K.kpe[0:ROPE, :], K.S[(s + 2) % 2][0:ROPE, :], K.rstd[0:ROPE, :],
                                ALU.mult).then_inc(K.s_taken, 1)
        dve.wait_ge(K.s_full, (s + 4).value())
        nc.vector.tensor_scalar(K.lat_v[:, :], K.S[(s + 3) % 2][:, 0:2 * TT], 1.0 / LAT, EPS, ALU.mult,
                                ALU.add).then_inc(K.s_taken, 1)
        dve.wait_ge(K.lat_sqrt, Num(1, (l, 1)).value())
        rsqrt(K.lat_r[:, :], K.lat_d[:, :], K.lat_v[:, :], K.lat_rec, Num(0, (l, 4)))
        for t in range(TT):
            for half in range(2):
                k = 4 + 2 * t + half
                w = HEADS * QK // 2
                full(f + k)
                nc.vector.tensor_scalar(K.qk[:, 0, t, half * w:(half + 1) * w], psum(g + k)[:, 0:w],
                                        K.lat_r[:, t:t + 1], None, ALU.mult).then_inc(K.tile_out, 1)
            if t == 0:
                split(j + 4)
        dve.wait_ge(K.kpe_full, Num(1, (l, 1)).value())
        nc.vector.tensor_copy(
            K.qk[:, 1, :, :].rearrange("p t (h c) -> p t h c", h=HEADS)[:, :, :, NOPE:QK],
            K.T[0][:, 0:TT * ROPE].rearrange("p (t c) -> p t c", t=TT).unsqueeze(2).broadcast_to([P, TT, HEADS, ROPE])
        ).then_inc(K.kpe_ok, 1)
        split(j + 5)

        def v_lo(i):
            t, c = i // 2, slice(i % 2 * SCOL, (i % 2 + 1) * SCOL)
            lo(K.v[:, 1, t, c], K.t[:, i % 3, 0:SCOL], K.v[:, 0, t, c], h + 4 + i)

        for t in range(TT):
            for half in range(2):
                i = 2 * t + half
                k = 12 + i
                n = HEADS // 2
                src = psum(g + k)[:, :].rearrange("p (h c) -> p h c", h=n)
                dst = K.qk[:, 1, t, :].rearrange("p (h c) -> p h c", h=HEADS)[:, half * n:(half + 1) * n, 0:NOPE]
                full(f + k)
                nc.vector.tensor_scalar(dst, src[:, :, 0:NOPE], K.lat_r[:, TT + t:TT + t + 1], None,
                                        ALU.mult).then_inc(K.k_out, 1)
                dve.wait_ge(K.split_lo, (h + 4 + i - 2).value())
                v = K.t[:, i % 3, 0:SCOL]
                nc.vector.tensor_scalar(v.rearrange("p (h c) -> p h c", h=n), src[:, :, NOPE:P],
                                        K.lat_r[:, TT + t:TT + t + 1], None, ALU.mult).then_inc(K.tile_out, 1)
                if i:
                    v_lo(i - 1)
        v_lo(2 * TT - 1)

        def fold(k):
            dve.wait_ge(K.tile_out, (g + 20 + k + 1).value())
            u, half = K.t[:, k % 3, :], SEQ // 2
            folded = K.sq[:, k % 2, :]
            if k >= 2:
                dve.wait_ge(K.split_lo, (h + 12 + k - 1).value())
            nc.vector.tensor_copy(folded[:, 0::half], u[:, 0::half])
            nc.vector.tensor_tensor(folded[:, 1:half], u[:, 1:half], u[:, :half:-1], ALU.add)
            nc.vector.tensor_tensor(folded[:, half + 1:SEQ], u[:, 1:half], u[:, :half:-1],
                                    ALU.subtract).then_inc(K.fold_ok, 1)

        def u_lo(k):
            lo(K.u[:, 1, k, :], K.sq[:, k % 2, :], K.u[:, 0, k, :], h + 12 + k)

        def head_roots():
            dve.wait_ge(K.head_sqrt, Num(1, (l, 1)).value())
            rsqrt(K.hr[:, :, :], K.hd_[:, :, :], K.hs[:, :, :], K.head_rec, Num(0, (l, 4)))
            nc.vector.tensor_scalar(K.hr[:, 0, :], K.hr[:, 0, :], -float(QK) ** -0.5, None, ALU.mult).then_inc(K.head_scaled, 1)

        def key_scale(i):
            dve.wait_ge(K.rope_ok, Num(12 + 6 * (i + 1), (l, 24)).value())
            v = K.qk[:, 1, 2 * i:2 * i + 2, :].rearrange("p t (h c) -> p (t h) c", h=HEADS)
            r = K.hr[:, 1, 2 * i * HEADS:(2 * i + 2) * HEADS]
            nc.vector.tensor_tensor(v, v, r.unsqueeze(2).broadcast_to([P, 2 * HEADS, QK]),
                                    ALU.mult).then_inc(K.head_scaled, 1)

        dve.wait_ge(K.x_fin, Num(2, (l, 2)).value())
        nc.vector.memset(K.gains[:, 2, :], 1.0).then_inc(K.gain_ok, 1)
        for i in range(4):
            split(j + 6 + i)
            for k in range(2 * i, 2 * i + 2):
                for n in HEAD_SQUARES[k]:
                    dve.wait_ge(K.head_sq, Num(n + 1, (l, 2 * TT)).value())
                    nc.vector.tensor_reduce(K.hs[:, n // TT, (n % TT) * HEADS:(n % TT + 1) * HEADS],
                                            K.hsq[:, n % 2, :].rearrange("p (h c) -> p h c", h=HEADS), AX_X,
                                            ALU.add).then_inc(K.head_red, 1)
                if k == HEAD_ROOT - 1:
                    dve.wait_ge(K.head_red, Num(2 * TT, (l, 2 * TT)).value())
                    nc.vector.tensor_scalar(K.hs[:, :, :], K.hs[:, :, :], 1.0 / QK, EPS, ALU.mult, ALU.add).then_inc(K.head_v, 1)
                if i < 2:
                    if k < 3:
                        dve.wait_ge(K.split_lo, (h + 12).value())
                    else:
                        dve.wait_ge(K.fold_ok, Num(k - 2, (l, TT)).value())
                    normed(K.t[:, k % 3, :], g + 20 + k, f + 20 + k)
                    if k:
                        fold(k - 1)
                    if k > 1:
                        u_lo(k - 2)
                    if k == TT - 1:
                        fold(k)
                        u_lo(k - 1)
                        u_lo(k)
                else:
                    normed(K.z[:, k - 4, :], g + 20 + k, f + 20 + k)
                if k == HEAD_ROOT:
                    head_roots()
                if k in KEY_SCALE:
                    key_scale(KEY_SCALE[k])
        def branch_lo(grp):
            lo(K.u[:, 1, grp, :], K.t[:, (grp + 2) % 3, :], K.u[:, 0, grp, :], h + 16 + grp)

        gi, ab, heads = 28, 0, Heads(K, "L", l)
        for stage, grp in FOURIER:
            if (stage, grp) == ("seq", 0):
                split(j + 10)
            if stage == "dim":
                for half in range(2):
                    ab += 1
                    c = ab_columns(half)
                    part = K.ab[:, grp % 2, :, 2 * half:2 * half + 2, c]
                    dve.wait_ge(K.ab_hi, Num(ab, (l, 8)).value())
                    nc.vector.tensor_tensor(part[:, 1], psum(g + gi)[:, :].rearrange("p (t c) -> p t c", t=2)[:, :, c],
                                            part[:, 0].bitcast(F32), ALU.subtract).then_inc(K.tile_out, 1)
                    gi += 1
            elif stage == "turn":
                qk_lo(heads, grp)
                gi += 2
            else:
                dve.wait_ge(K.pool_ok, Num(4, (l, 12)).value())
                if grp == 3:
                    dve.wait_ge(K.split_lo, (h + 17).value())
                full(f + gi)
                nc.vector.tensor_tensor(K.t[:, (grp + 2) % 3, :], psum(g + gi)[:, :], K.z[:, grp, :],
                                        ALU.mult).then_inc(K.tile_out, 1)
                if grp < 3:
                    branch_lo(grp)
                gi += 1
        attention(heads, lambda: branch_lo(3))

        def za_lo(t):
            lo(K.v[:, 1, t, :], K.t[:, t % 3, :], K.v[:, 0, t, :], h + 20 + t)

        for i in range(2):
            split(j + 11 + i)
            for t in range(2 * i, 2 * i + 2):
                if t == 3:
                    za_lo(0)
                    dve.wait_ge(K.split_lo, (h + 21).value())
                normed(K.t[:, t % 3, :], g + 64 + t, f + 56 + t)
        za_lo(1)
        za_lo(2)
        for i in range(4):
            merge(K.sig2, K.m2, j + 12 + 3 * i, g + 68 + 8 * i, f + 60 + 8 * i, h + 24 + 2 * i,
                  Num(KT + 2 * i, (l, KT)), sig_num(l, 8 + 4 * i), i, (lambda: za_lo(HALF - 1)) if i == 0 else None)
        for i in range(4):
            split(j + 24 + i + 1)
            if i == 0:
                dve.wait_ge(K.next_ok, Num(1, (l, 1)).value())
            for k in range(2 * i, 2 * i + 2):
                residual(k, g + 100 + k, f + 92 + k)
                if k:
                    gx_lo(k - 1, K.norm_next, Num(3 * KT, (l, KT)))
        gx_lo(KT - 1, K.norm_next, Num(3 * KT, (l, KT)))
    g, f = Num(G_L + LAYERS * GL), Num(F_L + LAYERS * FL)
    for k in range(2 * TT):
        full(f + k)
        nc.vector.tensor_copy(K.xout[:, k // 2, (k % 2) * SEQ:(k % 2 + 1) * SEQ], psum(g + k)[:, :]).then_inc(K.tile_out, 1)


def program_pe(nc, pe, K):
    def product(bank, pairs, stop_sem):
        for i, (lhs, rhs) in enumerate(pairs):
            mm = nc.tensor.matmul(bank, lhs, rhs, start=(i == 0), stop=(i == len(pairs) - 1))
        if stop_sem is not None:
            mm.then_inc(stop_sem, 1)

    def bank(g):
        if (g - GB + 1).due():
            pe.wait_ge(K.tile_out, (g - GB + 1).value())
        return K.G[g % GB]

    def fm(g, w, x, kts=KT, ready=None):
        b = bank(g)
        for k in range(kts):
            if ready is not None:
                ready(k)
            for i, (p, q) in enumerate(PASSES):
                mm = nc.tensor.matmul(b[:, :], w(p, k), x(q, k), start=(k == i == 0),
                                      stop=(k == kts - 1 and i == len(PASSES) - 1))
        mm.then_inc(K.tile_full, 1)

    def slab_ready(j):
        pe.wait_ge(K.w_lo, (j + 1).value())

    def wcol(j, m, kt0=0):
        v = K.w[:, j % 2, :, :].rearrange("p h (k c) -> p h k c", k=KT)
        return lambda part, k: v[:, part, kt0 + k, m * P:(m + 1) * P]

    def gx(part, k):
        return K.gx[:, part, k, :]

    def norm_ready(gx0):
        def ready(k):
            pe.wait_ge(K.gx_lo, (gx0 + k + 1).value())
        return ready

    def split_ready(h):
        def ready(k):
            pe.wait_ge(K.split_lo, (h + k + 1).value())
        return ready

    def stat_sum(norm, s, sums=K.sumsq):
        pe.wait_ge(K.sum_ok, (norm * (KT - 1) + KT - 1).value())
        if (s - 1).due():
            pe.wait_ge(K.s_taken, (s - 1).value())
        for t in range(TT):
            mm = nc.tensor.matmul(K.S[s % 2][:, t:t + 1], sums[:, t * P:(t + 1) * P], K.ones[:, 0:1],
                                  start=True, stop=True)
        mm.then_inc(K.s_full, 1)

    def stat_spread(norm, s):
        pe.wait_ge(K.stat_diag, (norm + 1).value())
        if s.due():
            pe.wait_ge(K.s_taken, s.value())
        nc.tensor.matmul(K.S[(s + 1) % 2][:, :], K.ones[:, :], K.sq[:, 0, :], start=True, stop=True).then_inc(K.s_full, 1)

    def turn(A, h):
        for q in range(2):
            b = bank(A.g_qk(h) + q)
            for t in range(TT):
                mm = nc.tensor.transpose(b[0:QK, t * P:(t + 1) * P], K.qk[:, q, t, h * QK:(h + 1) * QK], K.ident[:, :])
            mm.then_inc(K.tile_full, 1)

    def attention(A):
        U, S = A.u0, A.s0
        total = HEADS * TT

        def scores(n):
            t, e, i, b0, b1 = A.where(n)
            h = n // TT
            r = slice(e * HD, (e + 1) * HD)
            w = (b1 - b0) * P
            qs = slice(i * P, (i + 1) * P)
            pe.wait_ge(K.s_taken, (S + n - 1).value())
            if A.kind == "A":
                pairs = [(K.qa[r, p, t, qs], K.ka[r, q, b0 * P:b1 * P]) for p, q in PASSES]
            elif A.kind == "B":
                pairs = [(K.qb[r, p, t, qs], K.kb[r, q, t, :]) for p, q in PASSES]
            else:
                if i == 0:
                    pe.wait_ge(K.tile_out, (A.g_qk(h) + 2).value())
                pairs = [(K.qkh[0:QK, h % 2, 0, p, qs], K.qkh[0:QK, h % 2, 1, q, :]) for p, q in PASSES]
            product(K.S[(S + n) % 2][:, 0:w], pairs, K.s_full)

        def transposes(n):
            _, _, _, b0, b1 = A.where(n)
            pe.wait_ge(K.probs_ok, (U + n + 1).value())
            if (U + n - 1).due():
                pe.wait_ge(K.pt_lo, (U + n - 1).value())
            for k in range(b1 - b0):
                c = A.first() + k * P
                mm = nc.tensor.transpose(K.T[(U + n) % 2][:, k * P:(k + 1) * P], K.t[:, n % 3, c:c + P], K.ident[:, :])
            mm.then_inc(K.trans_full, 1)

        def values(m):
            h = m // 2
            t, _, _, a0, a1 = A.where(2 * m)
            _, _, _, b0, b1 = A.where(2 * m + 1)
            b = bank(A.g_out(h)) if m % 2 == 0 else K.G[A.g_out(h) % GB]
            out = b[:, m % 2 * 2 * P:(m % 2 + 1) * 2 * P].rearrange("p (e c) -> p e c", e=2)
            pe.wait_ge(K.pt_lo, (U + 2 * m + 2).value())
            for i, k in enumerate(range(a0, b1)):
                for p, q in PASSES:
                    v = {"A": lambda: K.va[:, p, k, :], "B": lambda: K.vb[:, p, k, t * P:(t + 1) * P],
                         "L": lambda: K.v[:, p, k, t * P:(t + 1) * P]}[A.kind]()
                    mm = nc.tensor.matmul(out[:, :, :], v, K.pt[A.kind][m % 2][:, q, k, :, :], start=(i == p == q == 0),
                                          stop=(k == b1 - 1 and (p, q) == PASSES[-1]))
            mm.then_inc(K.pv_done, 1)

        scores(0)
        scores(1)
        if A.kind == "L":
            turn(A, 1)
        scores(2)
        for n in range(total):
            if n + AHEAD < total:
                scores(n + AHEAD)
            transposes(n)
            if n >= 3 and n % 2 == 1:
                values(n // 2 - 1)
            if A.turned(n + 1) is not None:
                turn(A, A.turned(n + 1))
        values(total // 2 - 1)

    def merge(j, g, ya, yb, y_ready):
        for b in range(2):
            slab_ready(j + b)
            for m in range(2):
                fm(g + 2 * b + m, wcol(j + b, m), gx)
        slab_ready(j + 2)
        y_ready()
        for m in range(2):
            fm(g + 4 + 2 * m, wcol(j + 2, m), ya, HALF)
            fm(g + 5 + 2 * m, wcol(j + 2, m, HALF), yb, HALF)

    def eight(j, g, x, ready=None, norm=None):
        for i in range(4):
            slab_ready(j + i)
            for m in range(2):
                fm(g + 2 * i + m, wcol(j + i, m), x, ready=ready if i == m == 0 else None)
                if norm is not None and i == 0:
                    (stat_spread if m else stat_sum)(*norm)

    pe.wait_ge(K.ident_in, 16)
    pe.wait_ge(K.ones_ok, 1)
    for k in range(KT):
        pe.wait_ge(K.x_in[k // HALF], 16)
        b = bank(Num(G_X + k))
        for t in range(TT):
            mm = nc.tensor.transpose(b[:, t * P:(t + 1) * P], K.xin[:, t, k * P:(k + 1) * P], K.ident[:, :])
        mm.then_inc(K.tile_full, 1)
    for j in range(2):
        slab_ready(Num(j))
        w = K.w[:, j, :, :].rearrange("p h (k t c) -> p h k t c", k=HALF, t=HALF)
        for t in range(HALF):
            b = bank(Num(G_IN + t)) if j == 0 else K.G[(G_IN + t) % GB]
            for k in range(HALF):
                if t == 0:
                    pe.wait_ge(K.gx_lo, j * HALF + k + 1)
                for i, (p, q) in enumerate(PASSES):
                    mm = nc.tensor.matmul(b[:, :], w[:, p, k, t, :], gx(q, j * HALF + k), start=(j == k == i == 0),
                                          stop=(j == 1 and k == HALF - 1 and i == len(PASSES) - 1))
            if j == 1:
                mm.then_inc(K.tile_full, 1)
                if t < 2:
                    (stat_spread if t else stat_sum)(Num(0), Num(0))
    for k, (j, m, form, to) in enumerate(IN_TILES):
        if to[0] == "qa":
            continue
        g = Num(G_IN + k)
        slab_ready(Num(j))
        if form != "tm":
            fm(g, wcol(Num(j), m), gx)
        else:
            b = bank(g)
            w = K.w[:, j % 2, :, :].rearrange("p h (k c) -> p h k c", k=KT)
            for i in range(2):
                t = 2 * (to[1] % 2) + i
                pairs = [(K.gx[:, p, kt, t * P:(t + 1) * P], w[:, q, kt, :]) for kt in range(KT) for p, q in PASSES]
                product(b[:, i * SCOL:(i + 1) * SCOL], pairs, K.tile_full if i else None)
        if k and IN_TILES[k - 1][2] == "turn":
            pe.wait_ge(K.tile_out, g.value())
            for t in range(TT):
                mm = nc.tensor.transpose(K.T[0][:, t * P:(t + 1) * P], K.t[:, (k - 1) % 3, t * P:(t + 1) * P], K.ident[:, :])
            mm.then_inc(K.va_full, 1)
    pe.wait_ge(K.split_lo, Num(H_MERGE).value())
    pe.wait_ge(K.pt_zero, 2)
    attention(Heads(K, "A"))
    attention(Heads(K, "B"))

    def heads_ready():
        pe.wait_ge(K.tile_out, G_B + HEADS)

    for i in range(4):
        merge(Num(J_MERGE + 3 * i), Num(G_MERGE + 8 * i), lambda p, k: K.qa[:, p, k, :], lambda p, k: K.qb[:, p, k, :],
              heads_ready)

    def big(part, k):
        return K.big[:, part, k, :]

    eight(Num(J_OUT), Num(G_OUT), big, split_ready(Num(H_MERGE)))

    def chunk(c, **first):
        eight(Num(J_MLP, (c, 8)), Num(G_MLP, (c, 16)), gx, **first)
        eight(Num(J_MLP + 4, (c, 8)), Num(G_MLP + 8, (c, 16)), big, split_ready(Num(H_MLP, (c, 8))))

    chunk(0, ready=norm_ready(Num(KT)), norm=(Num(1), Num(S_N2)))
    with pe.Fori(1, CHUNKS) as c:
        chunk(c)
    stat_sum(Num(3), Num(S_NF), K.sumsq_f)
    pe.wait_ge(K.group_lo, 1)
    with pe.Fori(0, LAYERS) as l:
        j, g, f, h, s = (Num(n, (l, per)) for n, per in ((J_L, JL), (G_L, GL), (F_L, FL), (H_L, HL), (S_L, SL)))
        norm = Num(3, (l, 1))
        for k in range(4):
            slab_ready(j + k // 2)
            fm(g + k, wcol(j + k // 2, k % 2), gx,
               ready=norm_ready(Num(2 * KT, (l, KT))) if k == 0 else None)
            if k == 0:
                stat_sum(norm, s)
                pe.wait_ge(K.prior_diag, Num(1, (l, 1)).value())
                nc.tensor.matmul(K.T[1][:, :], K.ones[:, :], K.sq[:, 1, :], start=True, stop=True).then_inc(K.prior_full, 1)
            if k == 1:
                stat_spread(norm - 1, s)
        slab_ready(j + 2)
        pe.wait_ge(K.s_taken, (s + 1).value())
        product(K.S[(s + 2) % 2][:, :], [(K.w[:, (j + 2) % 2, p, i * P:(i + 1) * P], gx(q, i))
                                         for i in range(KT) for p, q in PASSES], K.s_full)
        pe.wait_ge(K.lat_sum, Num(2, (l, 2)).value())
        pe.wait_ge(K.s_taken, (s + 2).value())
        for i, sums in enumerate((K.sq[:, 0, :], K.hsq[:, 0, 0:SEQ])):
            for t in range(TT):
                mm = nc.tensor.matmul(K.S[(s + 3) % 2][:, i * TT + t:i * TT + t + 1], sums[:, t * P:(t + 1) * P],
                                      K.ones[:, 0:1], start=True, stop=True)
        mm.then_inc(K.s_full, 1)
        pe.wait_ge(K.split_lo, (h + 4).value())
        for i, n in enumerate((HEADS * QK // 2, SEQ)):
            slab_ready(j + 3 + i)
            w = K.w[:, (j + 3 + i) % 2, :, 0:4 * n].rearrange("p h (k c) -> p h k c", k=2)
            for t in range(TT):
                for half in range(2):
                    b = bank(g + 4 + 8 * i + 2 * t + half)
                    pairs = [(K.u[:, p, 2 * i + k, t * P:(t + 1) * P], w[:, q, k, half * n:(half + 1) * n])
                             for k in range(2) for p, q in PASSES]
                    if i == t == 0 and half == 1:
                        pe.wait_ge(K.s_taken, (s + 3).value())
                    product(b[:, 0:n], pairs, K.tile_full)
            if i == 0:
                for t in range(TT):
                    mm = nc.tensor.transpose(K.T[0][:, t * ROPE:(t + 1) * ROPE], K.kpe[0:ROPE, t * P:(t + 1) * P],
                                             K.ident[0:ROPE, 0:ROPE])
                mm.then_inc(K.kpe_full, 1)
        for k in range(8):
            slab_ready(j + 5 + k // 2)
            fm(g + 20 + k, wcol(j + 5 + k // 2, k % 2), gx)
        gi, heads = 28, Heads(K, "L", l)
        for stage, grp in FOURIER:
            if stage == "dim":
                pe.wait_ge(K.split_lo, (h + 12 + grp + 1).value())
                for half in range(2):
                    b = bank(g + gi)
                    for i, t in enumerate((2 * half, 2 * half + 1)):
                        pairs = [(K.u[:, p, grp, t * P:(t + 1) * P], K.sw[:, q, 0:SCOL]) for p, q in PASSES]
                        product(b[:, i * SCOL:(i + 1) * SCOL], pairs, K.tile_full if i else None)
                    gi += 1
            elif stage == "turn":
                pe.wait_ge(K.head_scaled, Num(3, (l, 3)).value())
                turn(heads, grp)
                gi += 2
            else:
                b = bank(g + gi)
                pe.wait_ge(K.tile_out, (g + fourier_tile(grp)).value())
                slab_ready(j + 9)
                w = K.w[:, (j + 9) % 2, :, :].rearrange("p h (k c) -> p h k c", k=TT)
                pairs = [(K.ab[:, grp % 2, p, t, t // 2 * P:(t // 2 + 1) * P], w[:, q, t, :])
                         for t in range(TT) for p, q in PASSES]
                pairs += [(K.ab[:, grp % 2, p, TT // 2, 0:P], K.alt[:, :]) for p in range(2)]
                product(b[:, :], pairs, K.tile_full)
                gi += 1
        attention(heads)
        for k in range(4):
            slab_ready(j + 10 + k // 2)
            fm(g + 64 + k, wcol(j + 10 + k // 2, k % 2), gx)

        def branches_ready():
            pe.wait_ge(K.split_lo, (h + 24).value())

        for i in range(4):
            merge(j + 12 + 3 * i, g + 68 + 8 * i, lambda p, k: K.v[:, p, k, :], lambda p, k: K.u[:, p, k, :],
                  branches_ready)
        eight(j + 24, g + 100, lambda p, k: K.m2[:, p, k, :], split_ready(h + 24))
    g = Num(G_L + LAYERS * GL)
    for k in range(2 * TT):
        b = bank(g + k)
        pe.wait_ge(K.tile_out, (g if k % 2 else g - KT // 2).value())
        for i in range(KT // 2):
            kt = (k % 2) * (KT // 2) + i
            mm = nc.tensor.transpose(b[:, i * P:(i + 1) * P], K.x[:, kt, (k // 2) * P:(k // 2 + 1) * P], K.ident[:, :])
        mm.then_inc(K.tile_full, 1)


def ab_columns(half):
    return slice(0, SCOL) if half else slice(0, P)


def fourier_tile(grp):
    n = 28
    for stage, of in FOURIER:
        n += 1 if stage == "seq" else 2
        if (stage, of) == ("dim", grp):
            return n


_INS = ["x", "norm_mix", "w_in", "b_gate", "sink", "rpb", "w_proj_a", "w_proj_b", "w_out", "norm_mlp", "w_up", "w_down",
        "norm_final", "norm_g_2", "w_in_2", "q_latent_g_2", "kv_latent_g_2", "w_uq_2", "w_ukv_2", "q_head_g_2",
        "k_head_g_2", "w_attn_proj_2", "w_fourier_proj_2", "b_merge_2", "w_out_2"]


def constants():
    f = np.float32
    c = {"ident": np.eye(P, dtype=f)}
    dist = np.abs(np.arange(P)[:, None] - (np.arange(3 * P) - P)[None, :])
    slopes = np.exp2(-8.0 * np.arange(1, HEADS + 1, dtype=f) / HEADS).astype(f)
    c["alibi"] = np.where(dist <= P, -slopes[:, None, None] * dist.astype(f), f(MASKED)).astype(f)
    col = np.arange(GRID_W)
    start = np.clip(col - KW // 2, 0, GRID_W - KW)
    near = ((col[None, :] >= start[:, None]) & (col[None, :] < start[:, None] + KW))[::-1]
    c["mask"] = np.tile(np.where(near, f(0), f(MASKED)), (2, 1)).astype(f)
    s = np.outer(np.arange(SEQ // 2), np.arange(SEQ)) % SEQ * (2 * np.pi / SEQ)
    c["dft_seq"] = np.concatenate([np.cos(s), -np.sin(s)]).astype(f)
    c["dft_alt"] = np.zeros((P, SEQ), f)
    c["dft_alt"][0] = 1 - 2 * (np.arange(SEQ) % 2)
    d = np.outer(np.arange(P), np.arange(P)) % P * (2 * np.pi / P)
    c["dft_dim"] = (np.concatenate([np.cos(d), np.sin(d)], 1) / np.sqrt(SEQ * P)).astype(f)
    half = ROPE // 2
    inv = (f(10000.0) ** (-np.arange(half, dtype=f) / f(half))).astype(f)
    ang = np.arange(SEQ, dtype=f)[:, None] * inv[None, :]
    c["rope"] = np.concatenate([np.cos(ang), np.sin(ang)], 1).astype(f)
    return c


def kernel(**inputs):
    import concourse.bacc as _bacc
    from concourse.bass_utils import run_bass_kernel_spmd as _run

    nc = _bacc.Bacc("TRN2", target_bir_lowering=False, num_devices=1)
    arrays, a = {}, {}
    given = {n: np.ascontiguousarray(inputs[n]) for n in _INS}
    for name, v in {**given, **constants()}.items():
        arrays[f"in_{name}"] = v
        a[name] = nc.dram_tensor(f"in_{name}", v.shape, mybir.dt.from_np(v.dtype), kind="ExternalInput").ap()
    out = nc.dram_tensor("out", (1, SEQ, D), F32, kind="ExternalOutput").ap()
    build(nc, a, out)
    r = _run(nc, [arrays], core_ids=[0])
    return r.results[0]["out"]
```
